# Optimizing a Trainium2 kernel written in Bass

```python
import math
import jax
import jax.numpy as jnp
from jax import lax
import numpy as np

D_MODEL = 1024
BATCH = 1
SEQ = 512
DEPTH = 2

N_EVEN = (DEPTH + 1) // 2
N_ODD = DEPTH // 2
DEEPNORM_ALPHA = (2.0 * DEPTH) ** 0.25
DEEPNORM_BETA = (8.0 * DEPTH) ** -0.25
LN_EPS = 1e-5
RMS_EPS = 1e-6
NEG_INF = -1e30

GDN_HEADS = 8
GDN_DK = 64
GDN_DV = 64
GDN_CHUNK = 64
CONV_K = 4
GDN_QK_WIDTH = GDN_HEADS * GDN_DK
GDN_V_WIDTH = GDN_HEADS * GDN_DV
CONV_WIDTH = 2 * GDN_QK_WIDTH + GDN_V_WIDTH
FOX_HEADS = 8
FOX_HEAD_DIM = 64
FOX_WIDTH = FOX_HEADS * FOX_HEAD_DIM
Q_BLOCK = 128
HY_IN_WIDTHS = (CONV_WIDTH, GDN_V_WIDTH, GDN_HEADS, GDN_HEADS, FOX_WIDTH, FOX_WIDTH, FOX_WIDTH, FOX_HEADS)
HY_IN_WIDTH = sum(HY_IN_WIDTHS)
HY_OUT_WIDTH = GDN_V_WIDTH + FOX_WIDTH
MLA_HEADS = 16
MLA_Q_LORA = 512
MLA_KV_LORA = 256
MLA_NOPE = 64
MLA_ROPE = 32
MLA_V = 64
ROPE_THETA = 10000.0
MLA_IN_WIDTHS = (MLA_Q_LORA, MLA_KV_LORA, MLA_ROPE)
MLA_IN_WIDTH = sum(MLA_IN_WIDTHS)
MLA_OUT_WIDTH = MLA_HEADS * MLA_V
N_EXPERTS = 64
N_GROUPS = 8
EXPERTS_PER_GROUP = N_EXPERTS // N_GROUPS
TOP_K = 2
D_FF_EXPERT = 256
MOE_BLOCK = 128
DOC_START_PROB = 1.0 / 2048

kernel_name = 'hybrid_deltanet_fox_mla_grouped_moe'

def split_cols(t, widths):
    cuts = [int(c) for c in np.cumsum(widths)[:-1]]
    return jnp.split(t, cuts, axis=-1)

def layer_norm(x, gain, bias):
    xf = x.astype(jnp.float32)
    mu = jnp.mean(xf, axis=-1, keepdims=True)
    var = jnp.mean(jnp.square(xf - mu), axis=-1, keepdims=True)
    y = (xf - mu) * lax.rsqrt(var + LN_EPS) * gain.astype(jnp.float32) + bias.astype(jnp.float32)
    return y.astype(x.dtype)

def rms_norm(x, gain):
    xf = x.astype(jnp.float32)
    y = xf * lax.rsqrt(jnp.mean(jnp.square(xf), axis=-1, keepdims=True) + RMS_EPS) * gain.astype(jnp.float32)
    return y.astype(x.dtype)

def l2_normalize(x):
    xf = x.astype(jnp.float32)
    return xf * lax.rsqrt(jnp.sum(jnp.square(xf), axis=-1, keepdims=True) + RMS_EPS)

def causal_depthwise_conv(u, w):
    return lax.conv_general_dilated(
        u, w[:, None, :].astype(u.dtype), window_strides=(1,), padding=[(CONV_K - 1, 0)],
        dimension_numbers=('NWC', 'WIO', 'NWC'), feature_group_count=u.shape[-1])

def rotary(t, positions):
    inv_freq = ROPE_THETA ** (-jnp.arange(0, MLA_ROPE, 2, dtype=jnp.float32) / MLA_ROPE)
    ang = positions.astype(jnp.float32)[..., None] * inv_freq
    ang = ang.reshape(ang.shape[:2] + (1,) * (t.ndim - 3) + ang.shape[-1:])
    cos, sin = jnp.cos(ang), jnp.sin(ang)
    t1, t2 = jnp.split(t.astype(jnp.float32), 2, axis=-1)
    return jnp.concatenate([t1 * cos - t2 * sin, t1 * sin + t2 * cos], axis=-1).astype(t.dtype)

def block_causal_attention(q, k, v, log_forget_cum=None):
    b, s, h, dqk = q.shape
    nb = s // Q_BLOCK
    scale = dqk ** -0.5
    key_pos = jnp.arange(s)
    q_blocks = jnp.swapaxes(q.reshape(b, nb, Q_BLOCK, h, dqk), 0, 1)
    xs = (jnp.arange(nb), q_blocks)
    if log_forget_cum is not None:
        c_keys = jnp.transpose(log_forget_cum, (0, 2, 1)).astype(jnp.float32)
        c_blocks = jnp.swapaxes(log_forget_cum.reshape(b, nb, Q_BLOCK, h), 0, 1)
        xs = xs + (c_blocks,)

    def one_block(args):
        blk, q_blk = args[0], args[1]
        logits = jnp.einsum('bqhd,bkhd->bhqk', q_blk, k, preferred_element_type=jnp.float32) * scale
        if log_forget_cum is not None:
            c_q = jnp.transpose(args[2], (0, 2, 1)).astype(jnp.float32)
            logits = logits + (c_q[..., :, None] - c_keys[:, :, None, :])
        query_pos = blk * Q_BLOCK + jnp.arange(Q_BLOCK)
        causal = key_pos[None, :] <= query_pos[:, None]
        logits = jnp.where(causal, logits, NEG_INF)
        probs = jax.nn.softmax(logits, axis=-1).astype(v.dtype)
        return jnp.einsum('bhqk,bkhd->bqhd', probs, v)

    out = lax.map(one_block, xs)
    return jnp.swapaxes(out, 0, 1).reshape(b, s, h, v.shape[-1])

def chunked_gated_delta_rule(q, k, v, log_decay, beta):
    b, s, h, dk = q.shape
    dv = v.shape[-1]
    n = s // GDN_CHUNK
    f32 = jnp.float32

    def chunks(t):
        return jnp.transpose(t.astype(f32).reshape(b, n, GDN_CHUNK, h, -1), (0, 3, 1, 2, 4))

    def chunks_scalar(t):
        return jnp.transpose(t.astype(f32).reshape(b, n, GDN_CHUNK, h), (0, 3, 1, 2))

    qc = chunks(q) * dk ** -0.5
    kc = chunks(k)
    vc = chunks(v)
    bc = chunks_scalar(beta)
    g = jnp.cumsum(chunks_scalar(log_decay), axis=-1)
    incl = jnp.tril(jnp.ones((GDN_CHUNK, GDN_CHUNK), dtype=bool))
    strict = jnp.tril(jnp.ones((GDN_CHUNK, GDN_CHUNK), dtype=bool), -1)
    gdiff = g[..., :, None] - g[..., None, :]
    decay = jnp.where(incl, jnp.exp(jnp.where(incl, gdiff, 0.0)), 0.0)
    k_beta = kc * bc[..., None]
    v_beta = vc * bc[..., None]
    lower = jnp.where(strict, jnp.einsum('bhnid,bhnjd->bhnij', k_beta, kc) * decay, 0.0)
    eye = jnp.eye(GDN_CHUNK, dtype=f32)
    t_inv = lax.linalg.triangular_solve(eye + lower, jnp.broadcast_to(eye, lower.shape),
                                        left_side=True, lower=True, unit_diagonal=True)
    u = jnp.einsum('bhnij,bhnjd->bhnid', t_inv, v_beta)
    w = jnp.einsum('bhnij,bhnjd->bhnid', t_inv, k_beta * jnp.exp(g)[..., None])
    attn = jnp.where(incl, jnp.einsum('bhnid,bhnjd->bhnij', qc, kc) * decay, 0.0)
    q_dec = qc * jnp.exp(g)[..., None]
    g_last = g[..., -1]
    k_tail = kc * jnp.exp(g_last[..., None] - g)[..., None]

    def step(state, xs):
        q_i, w_i, u_i, a_i, k_i, gl_i = xs
        v_new = u_i - jnp.einsum('bhck,bhkv->bhcv', w_i, state)
        o_i = jnp.einsum('bhck,bhkv->bhcv', q_i, state) + jnp.einsum('bhcj,bhjv->bhcv', a_i, v_new)
        state = state * jnp.exp(gl_i)[..., None, None] + jnp.einsum('bhck,bhcv->bhkv', k_i, v_new)
        return state, o_i

    xs = tuple(jnp.moveaxis(t, 2, 0) for t in (q_dec, w, u, attn, k_tail, g_last))
    state0 = jnp.zeros((b, h, dk, dv), f32)
    _, out = lax.scan(step, state0, xs)
    return jnp.transpose(out, (1, 0, 3, 2, 4)).reshape(b, s, h, dv).astype(v.dtype)

def delta_fox_mixer(x, w_in, conv_w, a_log, dt_bias, norm_w, f_bias, w_out):
    b, s, _ = x.shape
    f32 = jnp.float32
    qkv_d, z, beta_logit, a_logit, q_f, k_f, v_f, f_logit = split_cols(x @ w_in, HY_IN_WIDTHS)
    qkv_d = jax.nn.silu(causal_depthwise_conv(qkv_d, conv_w))
    q_d, k_d, v_d = split_cols(qkv_d, (GDN_QK_WIDTH, GDN_QK_WIDTH, GDN_V_WIDTH))
    q_d = l2_normalize(q_d.reshape(b, s, GDN_HEADS, GDN_DK))
    k_d = l2_normalize(k_d.reshape(b, s, GDN_HEADS, GDN_DK))
    v_d = v_d.reshape(b, s, GDN_HEADS, GDN_DV)
    beta = jax.nn.sigmoid(beta_logit.astype(f32))
    log_decay = -jnp.exp(a_log.astype(f32)) * jax.nn.softplus(a_logit.astype(f32) + dt_bias.astype(f32))
    o_d = chunked_gated_delta_rule(q_d, k_d, v_d, log_decay, beta)
    o_d = rms_norm(o_d, norm_w) * jax.nn.silu(z.reshape(b, s, GDN_HEADS, GDN_DV))
    log_f = jax.nn.log_sigmoid(f_logit.astype(f32) + f_bias.astype(f32))
    o_f = block_causal_attention(q_f.reshape(b, s, FOX_HEADS, FOX_HEAD_DIM),
                                 k_f.reshape(b, s, FOX_HEADS, FOX_HEAD_DIM),
                                 v_f.reshape(b, s, FOX_HEADS, FOX_HEAD_DIM),
                                 jnp.cumsum(log_f, axis=1))
    mixed = jnp.concatenate([o_d.reshape(b, s, GDN_V_WIDTH), o_f.reshape(b, s, FOX_WIDTH)], axis=-1)
    return mixed @ w_out

def mla_mixer(x, positions, w_in, q_norm_w, kv_norm_w, w_uq, w_ukv, w_out):
    b, s, _ = x.shape
    c_q, c_kv, k_rope = split_cols(x @ w_in, MLA_IN_WIDTHS)
    q = (rms_norm(c_q, q_norm_w) @ w_uq).reshape(b, s, MLA_HEADS, MLA_NOPE + MLA_ROPE)
    kv = (rms_norm(c_kv, kv_norm_w) @ w_ukv).reshape(b, s, MLA_HEADS, MLA_NOPE + MLA_V)
    q = jnp.concatenate([q[..., :MLA_NOPE], rotary(q[..., MLA_NOPE:], positions)], axis=-1)
    k_rope = jnp.broadcast_to(rotary(k_rope, positions)[:, :, None, :], (b, s, MLA_HEADS, MLA_ROPE))
    k = jnp.concatenate([kv[..., :MLA_NOPE], k_rope], axis=-1)
    o = block_causal_attention(q, k, kv[..., MLA_NOPE:])
    return o.reshape(b, s, MLA_OUT_WIDTH) @ w_out

def grouped_moe(x, router_w, router_bias, w_gate, w_up, w_down):
    b, s, d = x.shape
    n_tok = b * s
    n_pairs = n_tok * TOP_K
    n_blocks = n_pairs // MOE_BLOCK + N_EXPERTS
    xt = x.reshape(n_tok, d)
    scores = jax.nn.sigmoid(jnp.einsum('td,de->te', xt, router_w, preferred_element_type=jnp.float32))
    biased = (scores + router_bias.astype(jnp.float32)).reshape(n_tok, N_GROUPS, EXPERTS_PER_GROUP)
    group = jnp.argmax(jnp.sum(lax.top_k(biased, TOP_K)[0], axis=-1), axis=-1)
    in_group = jnp.take_along_axis(biased, group[:, None, None], axis=1)[:, 0]
    local = lax.top_k(in_group, TOP_K)[1]
    expert_idx = group[:, None] * EXPERTS_PER_GROUP + local
    chosen = jnp.take_along_axis(scores, expert_idx, axis=-1)
    gates = chosen / jnp.sum(chosen, axis=-1, keepdims=True)
    pair_expert = expert_idx.reshape(n_pairs)
    order = jnp.argsort(pair_expert)
    e_sorted = pair_expert[order]
    tok_sorted = order // TOP_K
    gate_sorted = gates.reshape(n_pairs)[order]
    counts = jnp.bincount(pair_expert, length=N_EXPERTS)
    padded = (counts + MOE_BLOCK - 1) // MOE_BLOCK * MOE_BLOCK
    padded_end = jnp.cumsum(padded)
    rank = jnp.arange(n_pairs) - (jnp.cumsum(counts) - counts)[e_sorted]
    dest = (padded_end - padded)[e_sorted] + rank
    rows = jnp.zeros((n_blocks * MOE_BLOCK, d), x.dtype).at[dest].set(xt[tok_sorted])
    block_expert = jnp.minimum(
        jnp.searchsorted(padded_end, jnp.arange(n_blocks) * MOE_BLOCK, side='right'), N_EXPERTS - 1)

    def expert_block(args):
        r, e = args
        hidden = jax.nn.silu(r @ w_gate[e]) * (r @ w_up[e])
        return hidden @ w_down[e]

    out_rows = lax.map(expert_block, (rows.reshape(n_blocks, MOE_BLOCK, d), block_expert)).reshape(-1, d)
    y = jnp.zeros((n_tok, d), x.dtype).at[tok_sorted].add(out_rows[dest] * gate_sorted[:, None].astype(x.dtype))
    return y.reshape(b, s, d)

def setup_inputs(seed: int = 0) -> dict:
    key = jax.random.key(seed)
    ks = jax.random.split(key, 24)
    f32 = jnp.float32

    def nrm(k, shape, scale):
        return jax.random.normal(k, shape, f32) * scale

    x = jax.random.normal(ks[0], (BATCH, SEQ, D_MODEL), f32)
    starts = jax.random.bernoulli(ks[1], DOC_START_PROB, (BATCH, SEQ)).at[:, 0].set(True)
    t = jnp.arange(SEQ, dtype=jnp.int32)
    doc_start = lax.cummax(jnp.where(starts, t[None, :], 0), axis=1)
    positions = (t[None, :] - doc_start).astype(jnp.int32)
    ln_gain = 1.0 + nrm(ks[2], (DEPTH, 2, D_MODEL), 0.02)
    ln_bias = nrm(ks[3], (DEPTH, 2, D_MODEL), 0.02)
    router_w = nrm(ks[4], (D_MODEL, N_EXPERTS), D_MODEL ** -0.5)
    router_bias = nrm(ks[5], (N_EXPERTS,), 0.01)
    moe_w_gate = nrm(ks[6], (DEPTH, N_EXPERTS, D_MODEL, D_FF_EXPERT), D_MODEL ** -0.5)
    moe_w_up = nrm(ks[7], (DEPTH, N_EXPERTS, D_MODEL, D_FF_EXPERT), D_MODEL ** -0.5)
    moe_w_down = nrm(ks[8], (DEPTH, N_EXPERTS, D_FF_EXPERT, D_MODEL), D_FF_EXPERT ** -0.5 * DEEPNORM_BETA)
    hy_w_in = nrm(ks[9], (N_EVEN, D_MODEL, HY_IN_WIDTH), D_MODEL ** -0.5)
    hy_conv_w = nrm(ks[10], (N_EVEN, CONV_K, CONV_WIDTH), CONV_K ** -0.5)
    gdn_a_log = jnp.log(jax.random.uniform(ks[11], (N_EVEN, GDN_HEADS), f32, minval=1.0, maxval=16.0))
    dt = jnp.exp(jax.random.uniform(ks[12], (N_EVEN, GDN_HEADS), f32,
                                    minval=math.log(1e-3), maxval=math.log(1e-1)))
    gdn_dt_bias = dt + jnp.log(-jnp.expm1(-dt))
    gdn_norm_w = 1.0 + nrm(ks[13], (N_EVEN, GDN_DV), 0.02)
    fox_f_bias = jnp.linspace(1.0, 6.0, FOX_HEADS, dtype=f32)[None, :] + nrm(ks[14], (N_EVEN, FOX_HEADS), 0.1)
    hy_w_out = nrm(ks[15], (N_EVEN, HY_OUT_WIDTH, D_MODEL), HY_OUT_WIDTH ** -0.5 * DEEPNORM_BETA)
    mla_w_in = nrm(ks[16], (N_ODD, D_MODEL, MLA_IN_WIDTH), D_MODEL ** -0.5)
    mla_q_norm = 1.0 + nrm(ks[17], (N_ODD, MLA_Q_LORA), 0.02)
    mla_kv_norm = 1.0 + nrm(ks[18], (N_ODD, MLA_KV_LORA), 0.02)
    mla_w_uq = nrm(ks[19], (N_ODD, MLA_Q_LORA, MLA_HEADS * (MLA_NOPE + MLA_ROPE)), MLA_Q_LORA ** -0.5)
    mla_w_ukv = nrm(ks[20], (N_ODD, MLA_KV_LORA, MLA_HEADS * (MLA_NOPE + MLA_V)), MLA_KV_LORA ** -0.5)
    mla_w_out = nrm(ks[21], (N_ODD, MLA_OUT_WIDTH, D_MODEL), MLA_OUT_WIDTH ** -0.5 * DEEPNORM_BETA)
    return {'x': x, 'positions': positions, 'ln_gain': ln_gain, 'ln_bias': ln_bias,
            'router_w': router_w, 'router_bias': router_bias,
            'moe_w_gate': moe_w_gate, 'moe_w_up': moe_w_up, 'moe_w_down': moe_w_down,
            'hy_w_in': hy_w_in, 'hy_conv_w': hy_conv_w, 'gdn_a_log': gdn_a_log,
            'gdn_dt_bias': gdn_dt_bias, 'gdn_norm_w': gdn_norm_w, 'fox_f_bias': fox_f_bias,
            'hy_w_out': hy_w_out, 'mla_w_in': mla_w_in, 'mla_q_norm': mla_q_norm,
            'mla_kv_norm': mla_kv_norm, 'mla_w_uq': mla_w_uq, 'mla_w_ukv': mla_w_ukv,
            'mla_w_out': mla_w_out}

def reference(x, positions, ln_gain, ln_bias, router_w, router_bias, moe_w_gate, moe_w_up, moe_w_down,
              hy_w_in, hy_conv_w, gdn_a_log, gdn_dt_bias, gdn_norm_w, fox_f_bias, hy_w_out,
              mla_w_in, mla_q_norm, mla_kv_norm, mla_w_uq, mla_w_ukv, mla_w_out):
    for layer in range(DEPTH):
        j = layer // 2
        if layer % 2 == 0:
            mixed = delta_fox_mixer(x, hy_w_in[j], hy_conv_w[j], gdn_a_log[j], gdn_dt_bias[j],
                                    gdn_norm_w[j], fox_f_bias[j], hy_w_out[j])
        else:
            mixed = mla_mixer(x, positions, mla_w_in[j], mla_q_norm[j], mla_kv_norm[j],
                              mla_w_uq[j], mla_w_ukv[j], mla_w_out[j])
        x = layer_norm(DEEPNORM_ALPHA * x + mixed, ln_gain[layer, 0], ln_bias[layer, 0])
        ffn = grouped_moe(x, router_w, router_bias, moe_w_gate[layer], moe_w_up[layer], moe_w_down[layer])
        x = layer_norm(DEEPNORM_ALPHA * x + ffn, ln_gain[layer, 1], ln_bias[layer, 1])
    return x


_drawn_inputs = setup_inputs


def setup_inputs(seed=0):
    import zlib

    import numpy as np

    out = dict(_drawn_inputs(seed))
    spreads = {}
    factors = {'mla_q_norm': 8.0, 'mla_kv_norm': 5.661}
    for name, (base, spread) in spreads.items():
        noise = np.random.default_rng([zlib.crc32(name.encode()), seed]).standard_normal(out[name].shape)
        drawn = base * np.exp(spread * noise) if base else spread * noise
        out[name] = jnp.asarray(drawn.astype(out[name].dtype))
    for name, factor in factors.items():
        out[name] = (out[name] * factor).astype(out[name].dtype)
    return out
```

```python
from contextlib import ExitStack

import numpy as np

import concourse.bass as bass
from concourse import mybir

F32 = mybir.dt.float32
F32R = mybir.dt.float32r
I32 = mybir.dt.int32
ALU = mybir.AluOpType
ACT = mybir.ActivationFunctionType
AX = mybir.AxisListType.X

P = 128
S = 512
D = 1024
T = S // P
KD = D // P
DEPTH = 2
ALPHA = (2.0 * DEPTH) ** 0.25
LN_EPS = 1e-5
RMS_EPS = 1e-6
NEG = -1e30

H = 8
DH = 64
C = 64
NCH = S // C
CONV_K = 4
NQKV = 3 * H * DH // P

MH = 16
NOPE, ROPE = 64, 32
QK = NOPE + ROPE
QL, KVL = 512, 256
MIN = QL + KVL + ROPE

E = 64
G = 8
FF = 256
CAP = 32
EPG = 4
NGRP = E // EPG
RNDS = S // CAP
UNITS = 6
RW = EPG * D


def const_layout():
    widths = [("ident", P), ("ones", P), ("chunk_ones", P), ("chunk_incl", P), ("tri_incl", P),
              ("tri_strict", P), ("causal", P), ("first_half", P), ("second_half", P),
              ("rope_swap", P), ("ident64", C), ("chunk_neg", C), ("levels", 6 * C),
              ("expert_rev", E), ("group_rev", G), ("slot_iota", CAP), ("round_step", NGRP),
              ("round_edges", RNDS - 1), ("inv_freq", 1)]
    at, n = {}, 0
    for name, w in widths:
        at[name] = (n, n + w)
        n += w
    return at, n


def const_array():
    at, n = const_layout()
    c = np.zeros((P, n), np.float32)
    j, i = np.arange(P)[:, None], np.arange(P)[None, :]

    def put(name, a):
        c[:, at[name][0]:at[name][1]] = a

    put("ident", j == i)
    put("ones", np.ones((P, P)))
    put("chunk_ones", j // C == i // C)
    put("chunk_incl", (j // C == i // C) & (j <= i))
    put("tri_incl", j <= i)
    put("tri_strict", j < i)
    put("causal", np.where(i > j, NEG, 0.0))
    put("first_half", (j < C) * np.ones((1, P)))
    put("second_half", (j >= C) * np.ones((1, P)))
    half = ROPE // 2
    same = j // ROPE == i // ROPE
    put("rope_swap", np.where(same & (i % ROPE < half) & (j == i + half), -1.0,
                              np.where(same & (i % ROPE >= half) & (j == i - half), 1.0, 0.0)))
    jj, ii = np.arange(P)[:, None] % C, np.arange(C)[None, :]
    put("ident64", jj == ii)
    put("chunk_neg", np.where(jj <= ii, 0.0, NEG))
    lv = [(ii // (2 * s) == jj // (2 * s)) & (ii // s % 2 == 1) & (jj // s % 2 == 0)
          for s in (1, 2, 4, 8, 16, 32)]
    put("levels", np.concatenate([x.astype(np.float32) for x in lv], 1))
    put("expert_rev", E - np.arange(E)[None, :] + 0.0 * j)
    put("round_step", np.where(np.arange(NGRP)[None, :] == 0, CAP, 0) + 0.0 * j)
    put("group_rev", G - np.arange(G)[None, :] + 0.0 * j)
    put("slot_iota", np.arange(CAP)[None, :] + 0.0 * j)
    put("round_edges", CAP * np.arange(1, RNDS)[None, :] + 0.0 * j)
    fr = np.float32(10000.0) ** (-np.arange(0, ROPE, 2, dtype=np.float32) / np.float32(ROPE))
    put("inv_freq", np.tile(fr, P // half)[:, None])
    return c


class Named:
    pass


class Chain:

    def __init__(self, eng, sem):
        self.eng, self.sem, self.n = eng, sem, 0

    def link(self, ins):
        self.n += 1
        ins.then_inc(self.sem, 1)
        self.eng.wait_ge(self.sem, self.n)


def build(nc, a, out):
    with ExitStack() as outer:
        names = [0]

        def sem(name):
            names[0] += 1
            return outer.enter_context(nc.semaphore(f"{name}_{names[0]}"))

        def opened(stack):
            def sb(name, shape, dt=F32):
                names[0] += 1
                return stack.enter_context(nc.sbuf_tensor(f"{name}_{names[0]}", shape, dt))

            def ps(name, shape, dt=F32):
                names[0] += 1
                return stack.enter_context(nc.psum_tensor(f"{name}_{names[0]}", shape, dt))
            return sb, ps

        sb, _ = opened(outer)
        at, ncol = const_layout()
        cst = sb("cst", [P, ncol])
        k = Named()
        k.count, k.cleared = 0, []
        k.nc, k.a, k.out, k.opened = nc, a, out, opened
        k.cst, k.c = cst, {n: cst[:, x:y] for n, (x, y) in at.items()}
        k.ring = sb("ring", [P, UNITS * RW])
        k.ring_full = [sem(f"ring_full{u}") for u in range(UNITS)]
        k.x = sb("x", [P, T, D])
        k.rounds = sb("rounds", [P, DEPTH], I32)
        hybrid_mixer(k)
        for layer in range(DEPTH):
            if layer == 1:
                latent_mixer(k)
            moe_layer(k, layer)


def ringview(kn, lo, words, pattern, **kw):
    return kn.ring[:, lo:lo + words].rearrange(pattern, **kw)



def hybrid_mixer(k):
    nc = k.nc
    W2 = KD * 512
    wb = [ringview(k, b * W2, W2, "p (k n) -> p k n", k=KD) for b in range(2)]
    qkvc = ringview(k, 2 * W2, NQKV * S, "p (n s) -> p n s", n=NQKV)
    base = 2 * W2 + NQKV * S
    z = ringview(k, base, T * 512, "p (t n) -> p t n", t=T)
    vf = ringview(k, base + 2048, T * 512, "p (t n) -> p t n", t=T)
    qf = ringview(k, base + 4096, 4 * S, "p (n s) -> p n s", n=4)
    kf = ringview(k, base + 6144, 4 * S, "p (n s) -> p n s", n=4)
    with ExitStack() as st:
        sb, _ = k.opened(st)
        prm = sb("params", [P, k.a["params"].shape[1]])
        gate = sb("gate", [P, T, 24])
        h = Named()
        h.wb, h.qkvc, h.z, h.vf, h.qf, h.kf, h.prm, h.gate = wb, qkvc, z, vf, qf, kf, prm, gate
        hybrid_project(k, h)
        unit_norms(k, h)
        g = Named()
        g.beta, g.g, g.eg, g.etail, g.logf, g.beg, g.cneg, g.cpos = (
            sb(n, [P, T, H]) for n in ("beta", "g", "eg", "etail", "logf", "beg", "cneg", "cpos"))
        g.estate = sb("estate", [P, NCH, 4])
        gate_scalars(k, h, g)
        mix = sb("mix", [P, T, D])
        delta_rule(k, h, g, mix)
        forgetting_attention(k, h, g, mix)
        project_out(k, mix, k.a["hy_w_out"], k.a["x"], 0)


def hybrid_project(k, h):
    nc, c = k.nc, k.c
    with ExitStack() as st:
        sb, ps = k.opened(st)
        xt = sb("xt", [P, KD, S])
        wsm = sb("wsm", [P, KD, 24])
        acc = sb("acc", [P, 2, S])
        pt = ps("pt", [P, 2, 512])
        pg = ps("pg", [P, T, 24])
        pb = ps("pb", [P, 4, 512])
        s = phase_sems(k, (
            "const_in", "x_in", "wsm_in", "w_in0", "w_in1", "xt_psum", "xt_ready", "gate_psum", "proj_psum",
            "conv_done", "silu_done", "copied", "tap_done"))
        w_in = [s["w_in0"], s["w_in1"]]
        starts = [0, 512, 1024, 2064, 2576, 1536, 3088]

        @nc_block(k, s)
        def _(block):
            @block.sync
            def _(sp):
                sp.dma_start(k.cst[:, :], k.a["const"]).then_inc(s["const_in"], 16)
                sp.dma_start(k.x[:, :, :], k.a["x"].rearrange("(t p) d -> p t d", p=P)).then_inc(s["x_in"], 16)
                for n, col in enumerate(starts):
                    if n >= 2:
                        sp.wait_ge(s["proj_psum"], 4 * (n - 1))
                    src = k.a["hy_w_in"][:, col:col + 512].rearrange("(k p) n -> p k n", p=P)
                    sp.dma_start(h.wb[n % 2], src).then_inc(w_in[n % 2], 16)

            @block.tensor
            def _(pe):
                pe.wait_ge(s["const_in"], 16)
                pe.wait_ge(s["x_in"], 16)
                for kt in range(KD):
                    if kt >= 2:
                        pe.wait_ge(s["xt_ready"], kt - 1)
                    for t in range(T):
                        last = nc.tensor.transpose(pt[:, kt % 2, t * P:(t + 1) * P],
                                                   k.x[:, t, kt * P:(kt + 1) * P], c["ident"])
                    last.then_inc(s["xt_psum"], 1)
                pe.wait_ge(s["xt_ready"], KD)
                pe.wait_ge(s["wsm_in"], 32)
                for t in range(T):
                    for kt in range(KD):
                        last = nc.tensor.matmul(pg[:, t, :], xt[:, kt, t * P:(t + 1) * P], wsm[:, kt, :],
                                                start=(kt == 0), stop=(kt == KD - 1))
                last.then_inc(s["gate_psum"], 1)
                for n in range(28):
                    ch, j = n // 4, n % 4
                    if j == 0:
                        pe.wait_ge(w_in[ch % 2], 16 * (ch // 2 + 1))
                    if n >= 4:
                        if n - 4 < NQKV:
                            pe.wait_ge(s["conv_done"], n - 3)
                        else:
                            pe.wait_ge(s["copied"], n - 4 - NQKV + 1 + 1)
                    for kt in range(KD):
                        if ch < 5:
                            l, r = h.wb[ch % 2][:, kt, j * P:(j + 1) * P], xt[:, kt, :]
                        else:
                            l, r = xt[:, kt, j * P:(j + 1) * P], h.wb[ch % 2][:, kt, :]
                        last = nc.tensor.matmul(pb[:, n % 4, :], l, r, start=(kt == 0), stop=(kt == KD - 1))
                    last.then_inc(s["proj_psum"], 1)

            @block.vector
            def _(dve):
                chain = Chain(dve, s["tap_done"])
                dve.wait_ge(s["wsm_in"], 32)
                cw = h.prm[:, 0:CONV_K * NQKV].rearrange("p (k n) -> p k n", k=CONV_K)
                for n in range(NQKV):
                    dve.wait_ge(s["proj_psum"], n + 1)
                    if n >= 2:
                        dve.wait_ge(s["silu_done"], n - 1)
                    u, o = pb[:, n % 4, :], acc[:, n % 2, :]
                    chain.link(nc.vector.tensor_scalar(o, u, cw[:, 3, n:n + 1], None, ALU.mult))
                    for tap in (2, 1, 0):
                        d = CONV_K - 1 - tap
                        ins = nc.vector.scalar_tensor_tensor(o[:, d:], u[:, 0:S - d], cw[:, tap, n:n + 1],
                                                             o[:, d:], ALU.mult, ALU.add)
                        if tap:
                            chain.link(ins)
                    ins.then_inc(s["conv_done"], 1)

            @block.scalar
            def _(act):
                act.dma_start(wsm[:, :, :], k.a["w_gates"].rearrange("p (k n) -> p k n", k=KD)).then_inc(s["wsm_in"], 16)
                act.dma_start(h.prm[:, :], k.a["params"]).then_inc(s["wsm_in"], 16)
                for kt in range(KD):
                    act.wait_ge(s["xt_psum"], kt + 1)
                    nc.scalar.activation(xt[:, kt, :], pt[:, kt % 2, :], ACT.Copy).then_inc(s["xt_ready"], 1)
                act.wait_ge(s["gate_psum"], 1)
                nc.scalar.activation(h.gate[:, :, :], pg[:, :, :], ACT.Copy).then_inc(s["copied"], 1)
                for n in range(NQKV):
                    act.wait_ge(s["conv_done"], n + 1)
                    nc.scalar.activation(h.qkvc[:, n, :], acc[:, n % 2, :], ACT.Silu).then_inc(s["silu_done"], 1)
                for n in range(NQKV, 28):
                    act.wait_ge(s["proj_psum"], n + 1)
                    ch, j = n // 4, n % 4
                    dst = {3: h.qf, 4: h.kf, 5: h.z, 6: h.vf}[ch][:, j, :]
                    nc.scalar.activation(dst, pb[:, n % 4, :], ACT.Copy,
                                         scale=DH ** -0.5 if ch == 3 else 1.0).then_inc(s["copied"], 1)


def phase_sems(k, names):
    k.count += 1
    return {n: k.nc.alloc_semaphore(f"{n}_{k.count}") for n in names}


def clear(k, s):
    with k.nc.Block() as block:
        @block.vector
        def _(dve):
            for x in s.values():
                dve.sem_clear(x)
    for x in s.values():
        k.nc.release_semaphore(x)


def nc_block(k, s, repeated=False):
    def run(f):
        with k.nc.Block() as block:
            f(block)
        if repeated:
            clear(k, s)
        else:
            for x in s.values():
                k.nc.gpsimd.sem_clear(x)
            for x in k.cleared:
                k.nc.release_semaphore(x)
            k.cleared = list(s.values())
    return run


def unit_norms(k, h):
    nc, c = k.nc, k.c
    with ExitStack() as st:
        sb, ps = k.opened(st)
        sq = sb("sq", [P, 2, S])
        rt = sb("rt", [P, 4, S])
        pn = ps("pn", [P, 4, 512])
        s = phase_sems(k, ("squared", "summed", "eps_added", "rooted", "inverse", "normed"))
        N = 8

        @nc_block(k, s)
        def _(block):
            @block.scalar
            def _(act):
                def root(n):
                    act.wait_ge(s["eps_added"], n + 1)
                    nc.scalar.activation(rt[:, n % 4, :], rt[:, n % 4, :], ACT.Sqrt).then_inc(s["rooted"], 1)
                for n in range(N):
                    if n >= 2:
                        act.wait_ge(s["summed"], n - 1)
                    nc.scalar.activation(sq[:, n % 2, :], h.qkvc[:, n, :], ACT.Square).then_inc(s["squared"], 1)
                    if n >= 2:
                        root(n - 2)
                root(N - 2)
                root(N - 1)

            @block.tensor
            def _(pe):
                for n in range(N):
                    pe.wait_ge(s["squared"], n + 1)
                    if n >= 4:
                        pe.wait_ge(s["eps_added"], n - 3)
                    nc.tensor.matmul(pn[:, n % 4, :], c["chunk_ones"], sq[:, n % 2, :],
                                     start=True, stop=True).then_inc(s["summed"], 1)

            @block.vector
            def _(dve):
                def add_eps(n):
                    dve.wait_ge(s["summed"], n + 1)
                    if n >= 4:
                        dve.wait_ge(s["normed"], n - 3)
                    nc.vector.tensor_scalar(rt[:, n % 4, :], pn[:, n % 4, :], RMS_EPS, None,
                                            ALU.add).then_inc(s["eps_added"], 1)

                def divide(n):
                    dve.wait_ge(s["rooted"], n + 1)
                    nc.vector.reciprocal(rt[:, n % 4, :], rt[:, n % 4, :]).then_inc(s["inverse"], 1)
                    dve.wait_ge(s["inverse"], n + 1)
                    nc.vector.scalar_tensor_tensor(h.qkvc[:, n, :], h.qkvc[:, n, :], DH ** -0.5 if n < 4 else 1.0,
                                                   rt[:, n % 4, :], ALU.mult, ALU.mult).then_inc(s["normed"], 1)
                for n in range(N):
                    add_eps(n)
                    if n >= 2:
                        divide(n - 2)
                divide(N - 2)
                divide(N - 1)


def gate_scalars(k, h, g):
    nc, c = k.nc, k.c
    W = T * 24
    with ExitStack() as st:
        sb, ps = k.opened(st)
        y, ny, e, s2, poly, sp = (sb(n, [P, T, 24]) for n in ("y", "ny", "e", "s2", "poly", "sp"))
        ea = sb("ea", [P, H])
        ld = sb("ld", [P, T, H])
        lf = sb("lf", [P, T, H])
        pref = sb("pref", [P, T, H])
        dif = sb("dif", [P, T, H])
        pg = ps("pg", [P, 512])
        s = phase_sems(k, ("dve", "to_act", "acted", "to_pe", "pe_done"))
        np_ = CONV_K * NQKV
        sgn, off, alog = h.prm[:, np_:np_ + 24], h.prm[:, np_ + 24:np_ + 48], h.prm[:, np_ + 48:np_ + 56]

        def wide(x):
            return x.unsqueeze(1).to_broadcast([P, T, x.shape[1]])

        @nc_block(k, s)
        def _(block):
            @block.vector
            def _(dve):
                ch = Chain(dve, s["dve"])
                v = nc.vector
                ch.link(v.tensor_tensor(y[:, :, :], h.gate[:, :, :], wide(off), ALU.add))
                ch.link(v.tensor_tensor(y[:, :, :], y[:, :, :], wide(sgn), ALU.mult))
                ch.link(v.tensor_scalar(ny[:, :, :], y[:, :, :], -1.0, None, ALU.mult))
                v.tensor_tensor(ny[:, :, :], ny[:, :, :], y[:, :, :], ALU.max).then_inc(s["to_act"], 1)
                dve.wait_ge(s["acted"], 1)
                ch.link(v.tensor_scalar(s2[:, :, :], e[:, :, :], 2.0, None, ALU.add))
                ch.link(v.reciprocal(s2[:, :, :], s2[:, :, :]))
                ch.link(v.tensor_tensor(e[:, :, :], e[:, :, :], s2[:, :, :], ALU.mult))
                ch.link(v.tensor_tensor(s2[:, :, :], e[:, :, :], e[:, :, :], ALU.mult))
                ch.link(v.tensor_scalar(poly[:, :, :], s2[:, :, :], 1 / 17, 1 / 15, ALU.mult, ALU.add))
                for d in (13, 11, 9, 7, 5, 3, 1):
                    ch.link(v.tensor_tensor(poly[:, :, :], poly[:, :, :], s2[:, :, :], ALU.mult))
                    ch.link(v.tensor_scalar(poly[:, :, :], poly[:, :, :], 1.0 / d, None, ALU.add))
                ch.link(v.tensor_tensor(poly[:, :, :], poly[:, :, :], e[:, :, :], ALU.mult))
                ch.link(v.tensor_scalar(sp[:, :, :], y[:, :, :], 0.0, None, ALU.max))
                ch.link(v.scalar_tensor_tensor(sp[:, :, :], poly[:, :, :], 2.0, sp[:, :, :], ALU.mult, ALU.add))
                ch.link(v.tensor_scalar(ea[:, :], ea[:, :], -1.0, None, ALU.mult))
                ch.link(v.tensor_tensor(ld[:, :, :], sp[:, :, 8:16], wide(ea[:, :]), ALU.mult))
                ch.link(v.tensor_scalar(lf[:, :, :], sp[:, :, 16:24], -1.0, None, ALU.mult))
                ch.link(v.memset(pref[:, 0, :], 0.0))
                for t in range(1, T):
                    ch.link(v.tensor_tensor(pref[:, t, :], pref[:, t - 1, :], lf[:, t - 1, :], ALU.add))
                v.nop().then_inc(s["to_pe"], 1)
                dve.wait_ge(s["pe_done"], 1)
                w = T * H

                def cols(n):
                    return pg[:, n * w:(n + 1) * w].rearrange("p (t h) -> p t h", t=T)
                ch.link(v.tensor_copy(g.g[:, :, :], cols(0)))
                ch.link(v.tensor_tensor(dif[:, :, :], cols(1), g.g[:, :, :], ALU.subtract))
                ch.link(v.tensor_copy(g.cpos[:, :, :], cols(4)))
                ch.link(v.tensor_scalar(g.cneg[:, :, :], cols(4), -1.0, None, ALU.mult))
                for par in range(2):
                    for cc in range(2):
                        ch.link(v.tensor_copy(g.estate[64 * par:64 * par + 64, cc::2, :],
                                              cols(2 + cc)[64 * par:64 * par + 64, :, 4 * par:4 * par + 4]))
                v.nop().then_inc(s["to_act"], 1)
                dve.wait_ge(s["acted"], 2)
                ch.link(v.tensor_tensor(g.beg[:, :, :], g.beta[:, :, :], g.eg[:, :, :], ALU.mult))

            @block.scalar
            def _(act):
                act.wait_ge(s["to_act"], 1)
                nc.scalar.activation(ea[:, :], alog, ACT.Exp)
                nc.scalar.activation(e[:, :, :], ny[:, :, :], ACT.Exp, scale=-1.0).then_inc(s["acted"], 1)
                act.wait_ge(s["to_act"], 2)
                nc.scalar.activation(g.eg[:, :, :], g.g[:, :, :], ACT.Exp)
                nc.scalar.activation(g.etail[:, :, :], dif[:, :, :], ACT.Exp)
                nc.scalar.activation(g.estate[:, :, :], g.estate[:, :, :], ACT.Exp)
                nc.scalar.activation(g.beta[:, :, :], y[:, :, 0:8], ACT.Sigmoid, scale=-1.0).then_inc(s["acted"], 1)

            @block.tensor
            def _(pe):
                pe.wait_ge(s["to_pe"], 1)
                w = T * H
                for n, m in enumerate(("chunk_incl", "chunk_ones", "first_half", "second_half")):
                    nc.tensor.matmul(pg[:, n * w:(n + 1) * w], c[m], ld[:, :, :], start=True, stop=True)
                nc.tensor.matmul(pg[:, 4 * w:5 * w], c["tri_incl"], lf[:, :, :], start=True, stop=False)
                nc.tensor.matmul(pg[:, 4 * w:5 * w], c["ones"], pref[:, :, :], start=False,
                                 stop=True).then_inc(s["pe_done"], 1)


def delta_rule(k, h, g, mix):
    nc, c = k.nc, k.c
    HC = [P, 2, 4, C]
    with ExitStack() as st:
        sb, ps = k.opened(st)
        dg, db, dt, m, ml, u, ti, y, att, kt_, kb, vb, uu, vn, o1 = (
            sb(n, [P, H, C]) for n in ("diag_g", "diag_b", "decay", "m", "m_level", "u", "t_inv", "y", "attn_t",
                                       "k_tail", "k_beta", "v_beta", "u_rows", "v_new", "o_first"))
        wt = sb("w_t", [P, 2, 4, C])
        state = sb("state", [P, 4, DH])
        bank = ps("bank", [P, 8, 512])
        s = phase_sems(k, (
            "dve", "diags", "rows_psum", "expo", "decay", "gram_psum", "tok_psum", "scaled", "u_ready", "t_psum",
            "t_copied", "m_level", "y_psum", "y_copied", "z_psum", "grown", "wu_psum", "wu_copied", "state_ready",
            "ws_psum", "v_new", "av_psum", "dve_end"))

        def bk(n):
            return bank[:, n, :]

        def heads(n):
            return bk(n).rearrange("p (h i) -> p h i", h=H)

        def par2(n):
            return bank[:, n:n + 2, 0:4 * C].rearrange("p a (b i) -> p a b i", b=4)

        def hv(x):
            return x[:, :, :].rearrange("p (a b) i -> p a b i", a=2)

        def over_heads(x):
            return x.unsqueeze(1).to_broadcast([P, H, C])

        def over_cols(x):
            return x.unsqueeze(2).to_broadcast([P, H, C])

        LV = c["levels"].rearrange("p (l i) -> p l i", l=6)

        @nc_block(k, s)
        def _(block):
            @block.tensor
            def _(pe):
                mm = nc.tensor.matmul
                for t in range(T):
                    tok = slice(t * P, (t + 1) * P)
                    pe.wait_ge(s["diags"], 2 * (t + 1))
                    if t:
                        pe.wait_ge(s["dve_end"], t)
                    mm(bk(0), c["chunk_ones"], dg[:, :, :], start=True, stop=True)
                    mm(bk(1), c["chunk_ones"], db[:, :, :], start=True, stop=True).then_inc(s["rows_psum"], 1)
                    for lo, off in ((2, 0), (4, -4)):
                        for b in range(4):
                            for cc in range(2):
                                for par in range(2):
                                    r, w = slice(64 * par, 64 * par + 64), slice(64 * cc, 64 * cc + 64)
                                    tc = slice(t * P + 64 * cc, t * P + 64 * cc + 64)
                                    last = mm(par2(lo)[w, par, b, :], h.qkvc[r, 4 + b, tc],
                                              h.qkvc[r, 4 + b + off, tc], start=True, stop=True)
                        last.then_inc(s["gram_psum"], 1)
                    for n, first in ((6, 4), (7, 8)):
                        for b in range(4):
                            last = nc.tensor.transpose(bk(n)[:, b * P:(b + 1) * P], h.qkvc[:, first + b, tok],
                                                       c["ident"])
                        last.then_inc(s["tok_psum"], 1)
                    pe.wait_ge(s["u_ready"], t + 1)

                    def blocks(out, lhs, rhs):
                        for hp in range(H):
                            for cc in range(2):
                                w = slice(64 * cc, 64 * cc + 64)
                                i = mm(out[w, hp, :], lhs[w, hp, :], rhs(w, hp), start=True, stop=True)
                        return i
                    blocks(heads(0), u, lambda w, hp: c["ident64"][w, :]).then_inc(s["t_psum"], 1)
                    for lv in range(1, 6):
                        n = 5 * t + lv
                        pe.wait_ge(s["m_level"], n)
                        if lv == 1:
                            pe.wait_ge(s["t_copied"], t + 1)
                        else:
                            pe.wait_ge(s["grown"], 9 * t + 2 * (lv - 1))
                        blocks(heads(0), ml, lambda w, hp: ti[w, hp, :]).then_inc(s["y_psum"], 1)
                        pe.wait_ge(s["y_copied"], n)
                        if lv < 5:
                            blocks(heads(1), u, lambda w, hp: y[w, hp, :]).then_inc(s["z_psum"], 1)
                        blocks(heads(2), y, lambda w, hp: u[w, hp, :]).then_inc(s["z_psum"], 1)
                    pe.wait_ge(s["grown"], 9 * (t + 1))
                    for cc in range(2):
                        w = slice(64 * cc, 64 * cc + 64)
                        for hp in range(H):
                            par, b = hp // 4, hp % 4
                            mm(bank[64 * par:64 * par + 64, 4 + cc, b * C:(b + 1) * C], kb[w, hp, :], u[w, hp, :],
                               start=True, stop=True)
                            last = mm(heads(3)[w, hp, :], u[w, hp, :], vb[w, hp, :], start=True, stop=True)
                    last.then_inc(s["wu_psum"], 1)
                    for cc in range(2):
                        n = 2 * t + cc
                        w = slice(64 * cc, 64 * cc + 64)
                        tc = slice(t * P + 64 * cc, t * P + 64 * cc + 64)
                        pe.wait_ge(s["state_ready"], n + 1)
                        if cc == 0:
                            pe.wait_ge(s["wu_copied"], 2 * (t + 1))
                        for hp in range(H):
                            par, b = hp // 4, hp % 4
                            r = slice(64 * par, 64 * par + 64)
                            last = mm(bank[w, par, b * C:(b + 1) * C], wt[r, cc, b, :], state[r, b, :],
                                      start=True, stop=True)
                        last.then_inc(s["ws_psum"], 1)
                        for hp in range(H):
                            par, b = hp // 4, hp % 4
                            r = slice(64 * par, 64 * par + 64)
                            last = mm(bank[w, (2, 6)[par], b * C:(b + 1) * C], h.qkvc[r, b, tc], state[r, b, :],
                                      start=True, stop=True)
                        last.then_inc(s["ws_psum"], 1)
                        pe.wait_ge(s["v_new"], n + 1)
                        for hp in range(H):
                            par, b = hp // 4, hp % 4
                            last = mm(bank[64 * par:64 * par + 64, 7, b * C:(b + 1) * C], kt_[w, hp, :],
                                      vn[w, hp, :], start=True, stop=True)
                        last.then_inc(s["av_psum"], 1)
                        for hp in range(H):
                            last = mm(heads(3)[w, hp, :], att[w, hp, :], vn[w, hp, :], start=True, stop=True)
                        last.then_inc(s["av_psum"], 1)

            @block.vector
            def _(dve):
                ch = Chain(dve, s["dve"])
                v = nc.vector
                tt = v.tensor_tensor
                ch.link(v.memset(state[:, :, :], 0.0))
                for t in range(T):
                    tt(dg[:, :, :], over_heads(c["ident64"]), over_cols(g.g[:, t, :]), ALU.mult).then_inc(s["diags"], 1)
                    tt(db[:, :, :], over_heads(c["ident64"]), over_cols(g.beta[:, t, :]), ALU.mult).then_inc(s["diags"], 1)
                    ch.link(tt(dt[:, :, :], over_heads(c["chunk_neg"]), over_cols(g.g[:, t, :]), ALU.subtract))
                    dve.wait_ge(s["rows_psum"], t + 1)
                    tt(dt[:, :, :], dt[:, :, :], heads(0), ALU.add).then_inc(s["expo"], 1)
                    dve.wait_ge(s["decay"], t + 1)
                    dve.wait_ge(s["gram_psum"], 2 * (t + 1))
                    ch.link(tt(hv(m), par2(2), hv(dt), ALU.mult))
                    ch.link(tt(m[:, :, :], m[:, :, :], heads(1), ALU.mult))
                    ch.link(tt(u[:, :, :], m[:, :, :], over_heads(LV[:, 0, :]), ALU.mult))
                    tt(u[:, :, :], over_heads(c["ident64"]), u[:, :, :], ALU.subtract).then_inc(s["u_ready"], 1)
                    tt(ml[:, :, :], m[:, :, :], over_heads(LV[:, 1, :]), ALU.mult).then_inc(s["m_level"], 1)
                    tt(hv(att), par2(4), hv(dt), ALU.mult)
                    dve.wait_ge(s["tok_psum"], 2 * (t + 1))
                    ktok = bk(6).rearrange("p (b a d) -> p a b d", b=4, a=2)
                    vtok = bk(7).rearrange("p (b a d) -> p a b d", b=4, a=2)

                    def per_head(x):
                        return x.rearrange("p (a b) -> p a b", a=2).unsqueeze(3).to_broadcast(HC)
                    tt(hv(kt_), ktok, per_head(g.etail[:, t, :]), ALU.mult)
                    tt(hv(kb), ktok, per_head(g.beg[:, t, :]), ALU.mult)
                    ch.link(tt(hv(vb), vtok, per_head(g.beta[:, t, :]), ALU.mult))
                    dve.wait_ge(s["t_copied"], t + 1)
                    for lv in range(1, 6):
                        nz = 9 * t + 2 * (lv - 1)
                        if lv < 5:
                            dve.wait_ge(s["z_psum"], nz + 1)
                            tt(ml[:, :, :], m[:, :, :], over_heads(LV[:, lv + 1, :]), ALU.mult).then_inc(s["m_level"], 1)
                            tt(ti[:, :, :], ti[:, :, :], heads(1), ALU.subtract).then_inc(s["grown"], 1)
                            dve.wait_ge(s["z_psum"], nz + 2)
                        else:
                            dve.wait_ge(s["z_psum"], nz + 1)
                        tt(u[:, :, :], u[:, :, :], heads(2), ALU.subtract).then_inc(s["grown"], 1)
                        dve.wait_ge(s["grown"], nz + (2 if lv < 5 else 1))
                    if t == 0:
                        v.nop().then_inc(s["state_ready"], 1)
                    for cc in range(2):
                        n = 2 * t + cc
                        w = slice(64 * cc, 64 * cc + 64)
                        if cc == 0:
                            dve.wait_ge(s["wu_copied"], 2 * (t + 1))
                        dve.wait_ge(s["ws_psum"], 2 * n + 1)
                        tt(hv(vn)[w], hv(uu)[w], par2(0)[w], ALU.subtract).then_inc(s["v_new"], 1)
                        dve.wait_ge(s["ws_psum"], 2 * n + 2)
                        ch.link(tt(state[:, :, :], state[:, :, :],
                                   g.estate[:, n, :].unsqueeze(2).to_broadcast([P, 4, DH]), ALU.mult))
                        for par, b0 in ((0, 2), (1, 6)):
                            src = bank[w, b0, 0:4 * C].rearrange("p (b d) -> p b d", b=4)
                            e = g.eg[w, t, 4 * par:4 * par + 4].unsqueeze(2).to_broadcast([64, 4, C])
                            ins = tt(o1[w, 4 * par:4 * par + 4, :], src, e, ALU.mult)
                        ch.link(ins)
                        dve.wait_ge(s["av_psum"], 2 * n + 1)
                        tt(state[:, :, :], state[:, :, :], bk(7)[:, 0:4 * DH].rearrange("p (b d) -> p b d", b=4),
                           ALU.add).then_inc(s["state_ready"], 1)
                        dve.wait_ge(s["av_psum"], 2 * n + 2)
                        dst = mix[w, t, 0:H * DH].rearrange("p (b a d) -> p a b d", b=4, a=2)
                        src = heads(3)[w].rearrange("p (a b) d -> p a b d", a=2)
                        ins = tt(dst, hv(o1)[w], src, ALU.add)
                        if cc == 1:
                            ins.then_inc(s["dve_end"], 1)
                        else:
                            ch.link(ins)

            @block.scalar
            def _(act):
                for t in range(T):
                    act.wait_ge(s["expo"], t + 1)
                    nc.scalar.activation(dt[:, :, :], dt[:, :, :], ACT.Exp).then_inc(s["decay"], 1)
                    act.wait_ge(s["t_psum"], t + 1)
                    nc.scalar.activation(ti[:, :, :], heads(0), ACT.Copy).then_inc(s["t_copied"], 1)
                    for lv in range(1, 6):
                        act.wait_ge(s["y_psum"], 5 * t + lv)
                        nc.scalar.activation(y[:, :, :], heads(0), ACT.Copy).then_inc(s["y_copied"], 1)
                    act.wait_ge(s["wu_psum"], t + 1)
                    nc.scalar.activation(wt[:, :, :, :], bank[:, 4:6, 0:4 * C].rearrange("p c (b i) -> p c b i", b=4),
                                         ACT.Copy).then_inc(s["wu_copied"], 1)
                    nc.scalar.activation(uu[:, :, :], heads(3), ACT.Copy).then_inc(s["wu_copied"], 1)

    with ExitStack() as st:
        sb, ps = k.opened(st)
        o = mix[:, :, 0:H * DH]
        sq = sb("sq", [P, T, H * DH])
        ss = sb("ss", [P, T * H])
        s2 = phase_sems(k, ("squared", "mean", "rooted", "silu", "dve"))
        np_ = CONV_K * NQKV + 56
        gain = h.prm[:, np_:np_ + DH]

        @nc_block(k, s2)
        def _(block):
            @block.scalar
            def _(act):
                nc.scalar.activation(sq[:, :, :], o, ACT.Square).then_inc(s2["squared"], 1)
                nc.scalar.activation(h.z[:, :, :], h.z[:, :, :], ACT.Silu).then_inc(s2["silu"], 1)
                act.wait_ge(s2["mean"], 1)
                nc.scalar.activation(ss[:, :], ss[:, :], ACT.Sqrt).then_inc(s2["rooted"], 1)

            @block.vector
            def _(dve):
                ch = Chain(dve, s2["dve"])
                v = nc.vector
                dve.wait_ge(s2["squared"], 1)
                ch.link(v.reduce_sum(ss[:, :], sq[:, :, :].rearrange("p t (h d) -> p (t h) d", h=H), axis=AX))
                v.tensor_scalar(ss[:, :], ss[:, :], 1.0 / DH, RMS_EPS, ALU.mult, ALU.add).then_inc(s2["mean"], 1)
                dve.wait_ge(s2["silu"], 1)
                for t in range(T):
                    zt = h.z[:, t, :].rearrange("p (h d) -> p h d", h=H)
                    i = v.tensor_tensor(zt, zt, gain.unsqueeze(1).to_broadcast([P, H, DH]), ALU.mult)
                ch.link(i)
                for t in range(T):
                    i = v.tensor_tensor(mix[:, t, 0:H * DH], mix[:, t, 0:H * DH], h.z[:, t, :], ALU.mult)
                dve.wait_ge(s2["rooted"], 1)
                ch.link(v.reciprocal(ss[:, :], ss[:, :]))
                for t in range(T):
                    ot = mix[:, t, 0:H * DH].rearrange("p (h d) -> p h d", h=H)
                    i = v.tensor_tensor(ot, ot, ss[:, t * H:(t + 1) * H].unsqueeze(2).to_broadcast([P, H, DH]),
                                        ALU.mult)
                ch.link(i)


def forgetting_attention(k, h, g, mix):
    def q_of(hd, t):
        return h.qf[64 * (hd % 2):64 * (hd % 2) + 64, hd // 2, t * P:(t + 1) * P]

    def k_of(hd, n):
        return h.kf[64 * (hd % 2):64 * (hd % 2) + 64, hd // 2, 0:n]

    def v_of(hd, kb):
        return h.vf[:, kb, hd * DH:(hd + 1) * DH]

    def out_of(hd, t):
        return mix[:, t, H * DH + hd * DH:H * DH + (hd + 1) * DH]
    attention(k, H, q_of, k_of, v_of, out_of, 1.0, g)


def attention(k, nh, q_of, k_of, v_of, out_of, scale, gates=None):
    nc, c = k.nc, k.c
    N = nh * T
    with ExitStack() as st:
        sb, ps = k.opened(st)
        pr = sb("probs", [P, 2, S])
        prt = sb("probs_t", [P, 2, S])
        mx = sb("row_max", [P, 4])
        rs = sb("row_sum", [P, 4])
        ri = sb("row_inv", [P, 4])
        if gates is not None:
            lg = sb("logits", [P, 2, S])
            dg = sb("diag_c", [P, 2, S])
            ck = sb("c_rows", [P, 2, S])
            ckm = sb("c_rows_causal", [P, 2, S])
            pck = ps("pck", [P, 2, 512])
        pl = ps("pl", [P, 2, 512])
        pt = ps("pt", [P, 2, 512])
        po = ps("po", [P, 2, 512])
        s = phase_sems(k, (
            "logit_psum", "masked", "maxed", "probs", "pt_psum", "pt_copied", "o_psum", "o_copied", "dve",
            "diag", "rows_psum", "rows", "rows_causal"))

        def size(n):
            return (n % T + 1) * P

        @nc_block(k, s)
        def _(block):
            @block.tensor
            def _(pe):
                def rows(hd):
                    pe.wait_ge(s["diag"], hd + 1)
                    if hd >= 2:
                        pe.wait_ge(s["rows"], hd - 1)
                    nc.tensor.matmul(pck[:, hd % 2, :], c["ones"], dg[:, hd % 2, :], start=True,
                                     stop=True).then_inc(s["rows_psum"], 1)

                def logits(n):
                    if n >= 2:
                        pe.wait_ge(s["masked"] if gates is not None else s["probs"], n - 1)
                    nc.tensor.matmul(pl[:, n % 2, 0:size(n)], q_of(n // T, n % T), k_of(n // T, size(n)),
                                     start=True, stop=True).then_inc(s["logit_psum"], 1)

                def transposes(n):
                    pe.wait_ge(s["probs"], n + 1)
                    if n >= 2:
                        pe.wait_ge(s["pt_copied"], n - 1)
                    for kb in range(n % T + 1):
                        last = nc.tensor.transpose(pt[:, n % 2, kb * P:(kb + 1) * P],
                                                   pr[:, n % 2, kb * P:(kb + 1) * P], c["ident"])
                    last.then_inc(s["pt_psum"], 1)

                def values(n):
                    pe.wait_ge(s["pt_copied"], n + 1)
                    if n >= 2:
                        pe.wait_ge(s["o_copied"], n - 1)
                    nb = n % T + 1
                    for kb in range(nb):
                        last = nc.tensor.matmul(po[:, n % 2, 0:DH], prt[:, n % 2, kb * P:(kb + 1) * P],
                                                v_of(n // T, kb), start=(kb == 0), stop=(kb == nb - 1))
                    last.then_inc(s["o_psum"], 1)

                for n in range(N + 2):
                    if gates is not None and n == 0:
                        rows(0)
                    if gates is not None and n % T == 1 and n // T + 1 < nh:
                        rows(n // T + 1)
                    if n < N:
                        logits(n)
                    if 1 <= n <= N:
                        transposes(n - 1)
                    if n >= 2:
                        values(n - 2)

            @block.vector
            def _(dve):
                ch = Chain(dve, s["dve"])
                v = nc.vector

                def diag(hd):
                    if hd >= 2:
                        dve.wait_ge(s["rows_psum"], hd - 1)
                    v.tensor_tensor(dg[:, hd % 2, :].rearrange("p (t i) -> p t i", t=T),
                                    c["ident"].unsqueeze(1).to_broadcast([P, T, P]),
                                    gates.cneg[:, :, hd].unsqueeze(2).to_broadcast([P, T, P]),
                                    ALU.mult).then_inc(s["diag"], 1)

                def normalise(n):
                    dve.wait_ge(s["o_psum"], n + 1)
                    ch.link(v.reciprocal(ri[:, n % 4:n % 4 + 1], rs[:, n % 4:n % 4 + 1]))
                    v.tensor_scalar(out_of(n // T, n % T), po[:, n % 2, 0:DH], ri[:, n % 4:n % 4 + 1], None,
                                    ALU.mult).then_inc(s["o_copied"], 1)

                if gates is not None:
                    diag(0)
                for n in range(N):
                    hd, t, w = n // T, n % T, size(n)
                    if gates is not None and t == 0 and hd + 1 < nh:
                        diag(hd + 1)
                    dve.wait_ge(s["logit_psum"], n + 1)
                    if gates is not None:
                        if n >= 2:
                            dve.wait_ge(s["probs"], n - 1)
                        cq = gates.cpos[:, t, hd:hd + 1]
                        if t:
                            dve.wait_ge(s["rows"], hd + 1)
                            v.scalar_tensor_tensor(lg[:, n % 2, 0:t * P], pl[:, n % 2, 0:t * P], cq,
                                                   ck[:, hd % 2, 0:t * P], ALU.add, ALU.add)
                        dve.wait_ge(s["rows_causal"], hd + 1)
                        v.scalar_tensor_tensor(lg[:, n % 2, t * P:w], pl[:, n % 2, t * P:w], cq,
                                               ckm[:, hd % 2, t * P:w], ALU.add, ALU.add).then_inc(s["masked"], 1)
                        src = lg[:, n % 2, 0:w]
                    else:
                        v.tensor_tensor(pl[:, n % 2, t * P:w], pl[:, n % 2, t * P:w], c["causal"],
                                        ALU.add).then_inc(s["masked"], 1)
                        src = pl[:, n % 2, 0:w]
                    dve.wait_ge(s["masked"], n + 1)
                    m = mx[:, n % 4:n % 4 + 1]
                    ch.link(v.reduce_max(m, src, axis=AX))
                    v.tensor_scalar(m, m, -scale, None, ALU.mult).then_inc(s["maxed"], 1)
                    if n >= 2:
                        normalise(n - 2)
                normalise(N - 2)
                normalise(N - 1)

            if gates is not None:
                @block.gpsimd
                def _(pool):
                    for hd in range(nh):
                        pool.wait_ge(s["rows"], hd + 1)
                        if hd >= 2:
                            pool.wait_ge(s["masked"], T * (hd - 1))
                        nc.gpsimd.tensor_tensor(ckm[:, hd % 2, :].rearrange("p (t i) -> p t i", t=T),
                                                ck[:, hd % 2, :].rearrange("p (t i) -> p t i", t=T),
                                                c["causal"].unsqueeze(1).to_broadcast([P, T, P]),
                                                ALU.add).then_inc(s["rows_causal"], 1)

            @block.scalar
            def _(act):
                def copy_rows(hd):
                    act.wait_ge(s["rows_psum"], hd + 1)
                    if hd >= 2:
                        act.wait_ge(s["masked"], T * (hd - 1))
                        act.wait_ge(s["rows_causal"], hd - 1)
                    nc.scalar.activation(ck[:, hd % 2, :], pck[:, hd % 2, :], ACT.Copy).then_inc(s["rows"], 1)

                def copy_pt(n):
                    act.wait_ge(s["pt_psum"], n + 1)
                    if n >= 2:
                        act.wait_ge(s["o_psum"], n - 1)
                    nc.scalar.activation(prt[:, n % 2, 0:size(n)], pt[:, n % 2, 0:size(n)],
                                         ACT.Copy).then_inc(s["pt_copied"], 1)

                for n in range(N):
                    if gates is not None and n == 0:
                        copy_rows(0)
                    if gates is not None and n % T == 2 and n // T + 1 < nh:
                        copy_rows(n // T + 1)
                    act.wait_ge(s["maxed"], n + 1)
                    if n >= 2:
                        act.wait_ge(s["pt_psum"], n - 1)
                    src = (lg if gates is not None else pl)[:, n % 2, 0:size(n)]
                    nc.scalar.activation(pr[:, n % 2, 0:size(n)], src, ACT.Exp, bias=mx[:, n % 4:n % 4 + 1],
                                         scale=scale, accum_out=rs[:, n % 4:n % 4 + 1]).then_inc(s["probs"], 1)
                    if n >= 1:
                        copy_pt(n - 1)
                copy_pt(N - 1)


def project_out(k, mix, w_out, x_src, ln):
    nc, c = k.nc, k.c
    with ExitStack() as st:
        sb, ps = k.opened(st)
        wo = sb("w_out", [P, KD, D])
        mt = sb("mix_t", [P, KD, S])
        pt = ps("pt", [P, 2, 512])
        py = ps("py", [P, 4, 512])
        s = phase_sems(k, (
            "w_in0", "w_in1", "t_psum", "t_ready", "y_psum", "added", "dve"))

        @nc_block(k, s)
        def _(block):
            @block.sync
            def _(sp):
                src = w_out.rearrange("(k p) n -> p k n", p=P)
                sp.dma_start(wo[:, :, 0:512], src[:, :, 0:512]).then_inc(s["w_in0"], 16)
                sp.dma_start(wo[:, :, 512:D], src[:, :, 512:D]).then_inc(s["w_in1"], 16)

            @block.tensor
            def _(pe):
                for kt in range(KD):
                    if kt >= 2:
                        pe.wait_ge(s["t_ready"], kt - 1)
                    for t in range(T):
                        last = nc.tensor.transpose(pt[:, kt % 2, t * P:(t + 1) * P], mix[:, t, kt * P:(kt + 1) * P],
                                                   c["ident"])
                    last.then_inc(s["t_psum"], 1)
                pe.wait_ge(s["t_ready"], KD)
                for n in range(2 * T):
                    nh, t = n // T, n % T
                    if t == 0:
                        pe.wait_ge((s["w_in0"], s["w_in1"])[nh], 16)
                    if n >= 4:
                        pe.wait_ge(s["added"], n - 3)
                    for kt in range(KD):
                        last = nc.tensor.matmul(py[:, n % 4, :], mt[:, kt, t * P:(t + 1) * P],
                                                wo[:, kt, nh * 512:nh * 512 + 512], start=(kt == 0),
                                                stop=(kt == KD - 1))
                    last.then_inc(s["y_psum"], 1)

            @block.scalar
            def _(act):
                for kt in range(KD):
                    act.wait_ge(s["t_psum"], kt + 1)
                    nc.scalar.activation(mt[:, kt, :], pt[:, kt % 2, :], ACT.Copy).then_inc(s["t_ready"], 1)

            @block.vector
            def _(dve):
                for n in range(2 * T):
                    nh, t = n // T, n % T
                    dve.wait_ge(s["y_psum"], n + 1)
                    xs = k.x[:, t, nh * 512:nh * 512 + 512]
                    nc.vector.scalar_tensor_tensor(xs, xs, ALPHA, py[:, n % 4, :], ALU.mult,
                                                   ALU.add).then_inc(s["added"], 1)
    layer_norm(k, ln, None)


def layer_norm(k, ln, rows_out):
    nc = k.nc
    with ExitStack() as st:
        sb, _ = k.opened(st)
        gain, bias = sb("gain", [P, D]), sb("bias", [P, D])
        stats = sb("stats", [P, T, 2, 6])
        mv = sb("mean_var", [P, T, 2])
        rstd = sb("rstd", [P, T])
        s = phase_sems(k, ("gain_in", "var_ready", "rooted", "dve", "normed", "stored",
                                                     "scaled", "shifted"))

        @nc_block(k, s)
        def _(block):
            @block.sync
            def _(sp):
                sp.dma_start(gain[:, :], k.a["ln_gain"][ln:ln + 1, :].to_broadcast([P, D])).then_inc(s["gain_in"], 16)
                sp.dma_start(bias[:, :], k.a["ln_bias"][ln:ln + 1, :].to_broadcast([P, D])).then_inc(s["gain_in"], 16)
                if rows_out is not None:
                    for t in range(T):
                        sp.wait_ge(s["shifted"], t + 1)
                        sp.dma_start(rows_out[t * P:(t + 1) * P, :], k.x[:, t, :]).then_inc(s["stored"], 16)
                    sp.wait_ge(s["stored"], 16 * T)

            @block.vector
            def _(dve):
                ch = Chain(dve, s["dve"])
                v = nc.vector
                for t in range(T):
                    for hf in range(2):
                        i = v.bn_stats(stats[:, t, hf, :], k.x[:, t, hf * 512:hf * 512 + 512])
                    ch.link(i)
                    i = v.bn_aggr(mv[:, t, :], stats[:, t, :, :])
                ch.link(i)
                v.tensor_scalar(rstd[:, :], mv[:, :, 1], LN_EPS, None, ALU.add).then_inc(s["var_ready"], 1)
                dve.wait_ge(s["rooted"], 1)
                ch.link(v.reciprocal(rstd[:, :], rstd[:, :]))
                dve.wait_ge(s["gain_in"], 32)
                for t in range(T):
                    v.tensor_scalar(k.x[:, t, :], k.x[:, t, :], mv[:, t, 0:1], rstd[:, t:t + 1], ALU.subtract,
                                    ALU.mult).then_inc(s["normed"], 1)
                    dve.wait_ge(s["normed"], t + 1)
                    v.tensor_tensor(k.x[:, t, :], k.x[:, t, :], gain[:, :], ALU.mult).then_inc(s["scaled"], 1)
                    dve.wait_ge(s["scaled"], t + 1)
                    v.tensor_tensor(k.x[:, t, :], k.x[:, t, :], bias[:, :], ALU.add).then_inc(s["shifted"], 1)

            @block.scalar
            def _(act):
                act.wait_ge(s["var_ready"], 1)
                nc.scalar.activation(rstd[:, :], rstd[:, :], ACT.Sqrt).then_inc(s["rooted"], 1)



def latent_mixer(k):
    nc = k.nc
    with ExitStack() as st:
        sb, _ = k.opened(st)
        ct = sb("c_t", [P, 6, S])
        wuq = sb("w_uq", [P, QL // P, MH * QK])
        wukv = sb("w_ukv", [P, KVL // P, MH * 2 * NOPE])
        cos, sin = sb("cos", [P, S]), sb("sin", [P, S])
        kr = sb("k_rope", [P, S])
        h = Named()
        h.ct, h.wuq, h.wukv, h.cos, h.sin, h.kr = ct, wuq, wukv, cos, sin, kr
        h.q = ringview(k, 0, MH * S, "p (h s) -> p h s", h=MH)
        h.k = ringview(k, MH * S, MH * S, "p (h s) -> p h s", h=MH)
        h.v = ringview(k, 2 * MH * S, T * MH * NOPE, "p (t n) -> p t n", t=T)
        latent_down(k, h)
        latent_up(k, h)
    with ExitStack() as st:
        sb, _ = k.opened(st)
        mix = sb("mix1", [P, T, D])
        attention(k, MH, lambda hd, t: h.q[0:QK, hd, t * P:(t + 1) * P], lambda hd, n: h.k[0:QK, hd, 0:n],
                  lambda hd, kb: h.v[:, kb, hd * NOPE:(hd + 1) * NOPE],
                  lambda hd, t: mix[:, t, hd * NOPE:(hd + 1) * NOPE], QK ** -0.5)
        project_out(k, mix, k.a["mla_w_out"], None, 2)


def latent_down(k, h):
    nc, c = k.nc, k.c
    xt = ringview(k, 0, KD * S, "p (k s) -> p k s", k=KD)
    wi = ringview(k, 4096, KD * MIN, "p (k n) -> p k n", k=KD)
    lat = ringview(k, 4096 + KD * MIN, T * (QL + KVL), "p (t n) -> p t n", t=T)
    LW = QL + KVL
    with ExitStack() as st:
        sb, ps = k.opened(st)
        prm = sb("params1", [P, k.a["params"].shape[1]])
        posi = sb("pos_int", [P, S], I32)
        ang = sb("angle", [P, S])
        rot = sb("turns", [P, S])
        sq = sb("square", [P, QL])
        ss = sb("sum_sq", [P, 2 * T])
        pt = ps("pt", [P, 2, 512])
        pc = ps("pc", [P, 4, 512])
        pr = ps("prope", [P, 2, 512])
        s = phase_sems(k, (
            "w_in", "prm_in", "wu_in", "t_psum", "t_ready", "rope_psum", "rope_copied", "swap_psum", "lat_psum",
            "lat_copied", "angles", "sines", "dve", "k_roped"))

        @nc_block(k, s)
        def _(block):
            @block.sync
            def _(sp):
                sp.dma_start(wi, k.a["mla_w_in"].rearrange("(k p) n -> p k n", p=P)).then_inc(s["w_in"], 16)
                sp.dma_start(prm[:, :], k.a["params"]).then_inc(s["prm_in"], 16)
                sp.dma_start(posi[:, :], k.a["positions"].to_broadcast([P, S])).then_inc(s["prm_in"], 16)
                sp.dma_start(h.wuq[:, :, :], k.a["mla_w_uq"].rearrange("(k p) n -> p k n", p=P)).then_inc(s["wu_in"], 16)
                sp.dma_start(h.wukv[:, :, :], k.a["mla_w_ukv"].rearrange("(k p) n -> p k n", p=P)).then_inc(s["wu_in"], 16)
                sp.wait_ge(s["wu_in"], 32)

            @block.tensor
            def _(pe):
                for kt in range(KD):
                    if kt >= 2:
                        pe.wait_ge(s["t_ready"], kt - 1)
                    for t in range(T):
                        last = nc.tensor.transpose(pt[:, kt % 2, t * P:(t + 1) * P], k.x[:, t, kt * P:(kt + 1) * P],
                                                   c["ident"])
                    last.then_inc(s["t_psum"], 1)
                pe.wait_ge(s["t_ready"], KD)
                pe.wait_ge(s["w_in"], 16)
                for kt in range(KD):
                    last = nc.tensor.matmul(pr[NOPE:QK, 0, :], wi[:, kt, LW:MIN], xt[:, kt, :],
                                            start=(kt == 0), stop=(kt == KD - 1))
                last.then_inc(s["rope_psum"], 1)
                for t in range(T):
                    if t >= 2:
                        pe.wait_ge(s["lat_copied"], 2 * (t - 1))
                    for kt in range(KD):
                        lhs = xt[:, kt, t * P:(t + 1) * P]
                        nc.tensor.matmul(pc[:, 2 * (t % 2), :], lhs, wi[:, kt, 0:QL], start=(kt == 0),
                                         stop=(kt == KD - 1))
                        last = nc.tensor.matmul(pc[:, 2 * (t % 2) + 1, 0:KVL], lhs, wi[:, kt, QL:LW],
                                                start=(kt == 0), stop=(kt == KD - 1))
                    last.then_inc(s["lat_psum"], 1)
                pe.wait_ge(s["rope_copied"], 1)
                nc.tensor.matmul(pr[NOPE:QK, 1, :], c["rope_swap"][NOPE:QK, NOPE:QK], h.kr[NOPE:QK, :],
                                 start=True, stop=True).then_inc(s["swap_psum"], 1)

            @block.scalar
            def _(act):
                for kt in range(KD):
                    act.wait_ge(s["t_psum"], kt + 1)
                    nc.scalar.activation(xt[:, kt, :], pt[:, kt % 2, :], ACT.Copy).then_inc(s["t_ready"], 1)
                act.wait_ge(s["rope_psum"], 1)
                nc.scalar.activation(h.kr[NOPE:QK, :], pr[NOPE:QK, 0, :], ACT.Copy).then_inc(s["rope_copied"], 1)
                for t in range(T):
                    act.wait_ge(s["lat_psum"], t + 1)
                    nc.scalar.activation(lat[:, t, 0:QL], pc[:, 2 * (t % 2), :], ACT.Copy).then_inc(s["lat_copied"], 1)
                    nc.scalar.activation(lat[:, t, QL:LW], pc[:, 2 * (t % 2) + 1, 0:KVL],
                                         ACT.Copy).then_inc(s["lat_copied"], 1)
                act.wait_ge(s["angles"], 2)
                nc.scalar.activation(h.sin[:, :], ang[:, :], ACT.Sin)
                nc.scalar.activation(h.cos[:, :], rot[:, :], ACT.Sin).then_inc(s["sines"], 1)

            @block.vector
            def _(dve):
                ch = Chain(dve, s["dve"])
                v = nc.vector
                ts, stt = v.tensor_scalar, v.scalar_tensor_tensor
                dve.wait_ge(s["prm_in"], 32)
                ch.link(v.tensor_copy(rot[:, :], posi[:, :]))
                ch.link(ts(ang[:, :], rot[:, :], c["inv_freq"], None, ALU.mult))
                magic = 1.5 * 2.0 ** 23
                p1, p2 = 6.28125, 0.0019340515136718750
                p3 = 2 * np.pi - p1 - p2
                ch.link(ts(rot[:, :], ang[:, :], 1 / (2 * np.pi), magic, ALU.mult, ALU.add))
                ch.link(ts(rot[:, :], rot[:, :], magic, None, ALU.subtract))
                for part in (p1, p2, p3):
                    ch.link(stt(ang[:, :], rot[:, :], -float(part), ang[:, :], ALU.mult, ALU.add))
                ch.link(ts(rot[:, :], ang[:, :], np.pi / 2, -2 * np.pi, ALU.is_gt, ALU.mult))
                ch.link(stt(rot[:, :], ang[:, :], np.pi / 2, rot[:, :], ALU.add, ALU.add))
                lim = 3.1415925
                ts(ang[:, :], ang[:, :], lim, -lim, ALU.min, ALU.max).then_inc(s["angles"], 1)
                ts(rot[:, :], rot[:, :], lim, -lim, ALU.min, ALU.max).then_inc(s["angles"], 1)
                dve.wait_ge(s["sines"], 1)
                dve.wait_ge(s["swap_psum"], 1)
                w = slice(NOPE, QK)
                v.tensor_tensor(h.kr[w, :], h.kr[w, :], h.cos[w, :], ALU.mult)
                ch.link(v.tensor_tensor(ang[w, :], pr[w, 1, :], h.sin[w, :], ALU.mult))
                ch.link(v.tensor_tensor(h.kr[w, :], h.kr[w, :], ang[w, :], ALU.add))

        s = phase_sems(k, ("squared", "mean", "rooted", "dve", "scaled", "t_psum", "t_ready"))
        np_ = CONV_K * NQKV + 56 + DH
        cuts = ((0, QL), (QL, LW))

        @nc_block(k, s)
        def _(block):
            @block.scalar
            def _(act):
                n = 0
                for t in range(T):
                    for i, (lo, hi) in enumerate(cuts):
                        if n:
                            act.wait_ge(s["squared"], n)
                        nc.scalar.activation(sq[:, 0:hi - lo], lat[:, t, lo:hi], ACT.Square,
                                             accum_out=ss[:, i * T + t:i * T + t + 1]).then_inc(s["squared"], 1)
                        n += 1
                act.wait_ge(s["mean"], 2)
                nc.scalar.activation(ss[:, :], ss[:, :], ACT.Sqrt).then_inc(s["rooted"], 1)
                for n in range(6):
                    act.wait_ge(s["t_psum"], n + 1)
                    nc.scalar.activation(h.ct[:, n, :], pt[:, n % 2, :], ACT.Copy,
                                         scale=prm[:, np_ + n:np_ + n + 1]).then_inc(s["t_ready"], 1)

            @block.vector
            def _(dve):
                ch = Chain(dve, s["dve"])
                v = nc.vector
                dve.wait_ge(s["squared"], 2 * T)
                for i, width in enumerate((QL, KVL)):
                    v.tensor_scalar(ss[:, i * T:(i + 1) * T], ss[:, i * T:(i + 1) * T], 1.0 / width, RMS_EPS,
                                    ALU.mult, ALU.add).then_inc(s["mean"], 1)
                dve.wait_ge(s["rooted"], 1)
                ch.link(v.reciprocal(ss[:, :], ss[:, :]))
                for t in range(T):
                    for i, (lo, hi) in enumerate(cuts):
                        v.tensor_scalar(lat[:, t, lo:hi], lat[:, t, lo:hi], ss[:, i * T + t:i * T + t + 1], None,
                                        ALU.mult).then_inc(s["scaled"], 1)

            @block.tensor
            def _(pe):
                pe.wait_ge(s["scaled"], 2 * T)
                for n in range(6):
                    if n >= 2:
                        pe.wait_ge(s["t_ready"], n - 1)
                    for t in range(T):
                        last = nc.tensor.transpose(pt[:, n % 2, t * P:(t + 1) * P], lat[:, t, n * P:(n + 1) * P],
                                                   c["ident"])
                    last.then_inc(s["t_psum"], 1)


def latent_up(k, h):
    nc, c = k.nc, k.c
    with ExitStack() as st:
        sb, ps = k.opened(st)
        raw = sb("rope_raw", [P, 2, S])
        turned = sb("rope_turned", [P, 2, S])
        pb = ps("pb", [P, 4, 512])
        psw = ps("psw", [P, 2, 512])
        s = phase_sems(k, (
            "tile_psum", "plain_copied", "rope_copied", "v_copied", "swap_psum", "sin_part", "cos_part", "roped",
            "q_rope_placed", "k_rope_placed"))
        uq, ukv = h.wuq, h.wukv
        RB = MH * NOPE
        QN, QR, KN, VN = 8, 4, 8, 8
        NT = QN + QR + KN + VN

        def read(eng, n):
            if n < QN:
                eng.wait_ge(s["plain_copied"], 2 * (n + 1))
            elif n < QN + QR:
                eng.wait_ge(s["rope_copied"], n - QN + 1)
            elif n < QN + QR + KN:
                eng.wait_ge(s["plain_copied"], 2 * (n - QR + 1))
            else:
                eng.wait_ge(s["v_copied"], n - QN - QR - KN + 1)

        @nc_block(k, s)
        def _(block):
            @block.tensor
            def _(pe):
                def swap(g):
                    pe.wait_ge(s["rope_copied"], g + 1)
                    if g >= 2:
                        pe.wait_ge(s["sin_part"], g - 1)
                    nc.tensor.matmul(psw[:, g % 2, :], c["rope_swap"], raw[:, g % 2, :], start=True,
                                     stop=True).then_inc(s["swap_psum"], 1)

                for n in range(NT):
                    if n >= 4:
                        read(pe, n - 4)
                    o = pb[:, n % 4, :]
                    nk = QL // P if n < QN + QR else KVL // P
                    for kt in range(nk):
                        if n < QN:
                            l, r = uq[:, kt, n * P:(n + 1) * P], h.ct[:, kt, :]
                        elif n < QN + QR:
                            j = n - QN
                            l, r = uq[:, kt, RB + j * P:RB + (j + 1) * P], h.ct[:, kt, :]
                        elif n < QN + QR + KN:
                            j = n - QN - QR
                            l, r = ukv[:, kt, j * P:(j + 1) * P], h.ct[:, 4 + kt, :]
                        else:
                            t, hf = (n - QN - QR - KN) // 2, (n - QN - QR - KN) % 2
                            l, r = h.ct[:, 4 + kt, t * P:(t + 1) * P], ukv[:, kt, RB + hf * 512:RB + hf * 512 + 512]
                        last = nc.tensor.matmul(o, l, r, start=(kt == 0), stop=(kt == nk - 1))
                    last.then_inc(s["tile_psum"], 1)
                    if QN + 1 <= n <= QN + QR:
                        swap(n - QN - 1)

            @block.scalar
            def _(act):
                for n in list(range(QN)) + list(range(QN + QR, QN + QR + KN)):
                    act.wait_ge(s["tile_psum"], n + 1)
                    dst, j = (h.q, n) if n < QN else (h.k, n - QN - QR)
                    for i in range(2):
                        nc.scalar.activation(dst[0:NOPE, 2 * j + i, :], pb[NOPE * i:NOPE * (i + 1), n % 4, :],
                                             ACT.Copy).then_inc(s["plain_copied"], 1)

            @block.vector
            def _(dve):
                v = nc.vector

                def turn(g):
                    if g >= 2:
                        dve.wait_ge(s["q_rope_placed"], 4 * (g - 1))
                    v.tensor_tensor(turned[:, g % 2, :], raw[:, g % 2, :], h.cos[:, :],
                                    ALU.mult).then_inc(s["cos_part"], 1)
                    dve.wait_ge(s["swap_psum"], g + 1)
                    dve.wait_ge(s["cos_part"], g + 1)
                    v.tensor_tensor(raw[:, g % 2, :], psw[:, g % 2, :], h.sin[:, :], ALU.mult).then_inc(s["sin_part"], 1)
                    dve.wait_ge(s["sin_part"], g + 1)
                    v.tensor_tensor(turned[:, g % 2, :], turned[:, g % 2, :], raw[:, g % 2, :],
                                    ALU.add).then_inc(s["roped"], 1)

                for g in range(QR):
                    n = QN + g
                    dve.wait_ge(s["tile_psum"], n + 1)
                    if g >= 2:
                        dve.wait_ge(s["roped"], g - 1)
                    v.tensor_copy(raw[:, g % 2, :], pb[:, n % 4, :]).then_inc(s["rope_copied"], 1)
                    if g >= 1:
                        turn(g - 1)
                    else:
                        dve.wait_ge(s["rope_copied"], 1)
                dve.wait_ge(s["rope_copied"], QR)
                turn(QR - 1)
                for m in range(VN):
                    n = QN + QR + KN + m
                    dve.wait_ge(s["tile_psum"], n + 1)
                    v.tensor_copy(h.v[:, m // 2, (m % 2) * 512:(m % 2) * 512 + 512],
                                  pb[:, n % 4, :]).then_inc(s["v_copied"], 1)

            @block.gpsimd
            def _(pool):
                for hd in range(MH):
                    nc.gpsimd.tensor_copy(h.k[NOPE:QK, hd, :], h.kr[NOPE:QK, :]).then_inc(s["k_rope_placed"], 1)
                    if hd % 4 == 3:
                        g = hd // 4
                        pool.wait_ge(s["roped"], g + 1)
                        for j in range(4):
                            nc.gpsimd.tensor_copy(h.q[NOPE:QK, 4 * g + j, :],
                                                  turned[32 * j:32 * j + 32, g % 2, :]).then_inc(s["q_rope_placed"], 1)



def moe_layer(k, layer):
    with ExitStack() as st:
        sb, _ = k.opened(st)
        m = Named()
        m.rank, m.share = sb("rank", [P, T, E]), sb("share", [P, T, E])
        m.rounds = k.rounds[:, layer:layer + 1]
        m.iota = sb("iota", [P, CAP])
        m.xhi, m.xlo = sb("x_hi", [P, T, D], F32R), sb("x_lo", [P, T, D], F32R)
        route(k, layer, m)
        w = expert_buffers(k, st)
        experts(k, layer, m, w)
        overflow_rounds(k, layer, m, w)
    layer_norm(k, 2 * layer + 1, k.out if layer == DEPTH - 1 else None)


def expert_buffers(k, stack):
    sb, ps = k.opened(stack)
    w = Named()
    w.oh, w.ohg = sb("onehot", [P, 2, T, P], F32R), sb("onehot_gate", [P, 2, T, P])
    w.oht = sb("onehot_t", [P, 2, T, P], F32R)
    w.xg, w.xt = sb("xg", [P, D]), sb("xg_t", [P, 2, KD, P])
    w.gate, w.hid, w.ht = sb("silu", [P, 2, FF]), sb("hidden", [P, 2, FF]), sb("hidden_t", [P, 2, 2, P])
    w.sg = sb("slot_gate", [P, 2])
    w.ohi, w.olo = sb("out_hi", [P, 2, 512], F32R), sb("out_lo", [P, 2, 512], F32R)
    w.px, w.po, w.py = (ps(n, [P, 2, 512]) for n in ("px", "po", "py"))
    w.pgu, w.pht = ps("pgu", [P, 512]), ps("pht", [P, 512])
    return w


def ring_load(k, sp, layer, grp, u, sem=None):
    sem = k.ring_full[u] if sem is None else sem
    e0 = grp * EPG + layer * E
    if u < 4:
        for i, name in enumerate(("w_gate", "w_up")):
            src = k.a[name].rearrange("e (p t) f -> p e (t f)", p=P)[:, bass.ds(e0, EPG), u * 512:(u + 1) * 512]
            dst = k.ring[:, u * RW + i * RW // 2:u * RW + (i + 1) * RW // 2].rearrange("p (e w) -> p e w", e=EPG)
            sp.dma_start(dst, src).then_inc(sem, 16)
    else:
        src = k.a["w_down"].rearrange("e (p t) n -> p e (t n)", p=P)[:, bass.ds(e0 + 2 * (u - 4), 2), :]
        dst = k.ring[:, u * RW:(u + 1) * RW].rearrange("p (e w) -> p e w", e=2)
        sp.dma_start(dst, src).then_inc(sem, 16)


def fill_count(u):
    return 32 if u < 4 else 16


def route(k, layer, m):
    nc, c = k.nc, k.c
    with ExitStack() as st:
        sb, ps = k.opened(st)
        xt = sb("xt", [P, KD, S])
        rw = sb("router_w", [P, KD, E])
        rb = sb("router_b", [P, E])
        sc, bi, sel, oh0, oh1, val, both, pref = (sb(n, [P, T, E]) for n in (
            "scores", "biased", "selected", "first", "second", "value", "both", "before"))
        top = sb("top", [P, T * G, 8])
        gs, geq = sb("group_score", [P, T, G]), sb("group_eq", [P, T, G])
        r1 = sb("r1", [P, T])
        top2 = sb("top2", [P, T, 8])
        edge = sb("edge", [P, RNDS - 1])
        cm = sb("count_max", [P, 1])
        pt = ps("pt", [P, 2, 512])
        pr = ps("pr", [P, 512])
        prk = ps("prk", [P, 512])
        pcn = ps("pcn", [P, 512])
        s = phase_sems(k, ("w_in", "t_psum", "t_ready", "score_psum", "scored", "dve", "counted", "rank_psum",
                           "x_hi", "x_lo"))

        @nc_block(k, s)
        def _(block):
            @block.sync
            def _(sp):
                sp.dma_start(rw[:, :, :], k.a["router_w"].rearrange("(k p) e -> p k e", p=P)).then_inc(s["w_in"], 16)
                sp.dma_start(rb[:, :], k.a["router_bias"].to_broadcast([P, E])).then_inc(s["w_in"], 16)
                for u in range(UNITS):
                    ring_load(k, sp, layer, 0, u)

            @block.tensor
            def _(pe):
                for kt in range(KD):
                    if kt >= 2:
                        pe.wait_ge(s["t_ready"], kt - 1)
                    for t in range(T):
                        last = nc.tensor.transpose(pt[:, kt % 2, t * P:(t + 1) * P], k.x[:, t, kt * P:(kt + 1) * P],
                                                   c["ident"])
                    last.then_inc(s["t_psum"], 1)
                pe.wait_ge(s["t_ready"], KD)
                pe.wait_ge(s["w_in"], 32)
                for t in range(T):
                    for kt in range(KD):
                        last = nc.tensor.matmul(pr[:, t * E:(t + 1) * E], xt[:, kt, t * P:(t + 1) * P], rw[:, kt, :],
                                                start=(kt == 0), stop=(kt == KD - 1))
                last.then_inc(s["score_psum"], 1)
                pe.wait_ge(s["counted"], 1)
                nc.tensor.matmul(prk[:, 0:T * E], c["tri_strict"], both[:, :, :], start=True, stop=False)
                nc.tensor.matmul(prk[:, 0:T * E], c["ones"], pref[:, :, :], start=False, stop=True)
                nc.tensor.matmul(pcn[:, 0:E], c["ones"], val[:, 0, :], start=True,
                                 stop=True).then_inc(s["rank_psum"], 1)

            @block.scalar
            def _(act):
                for kt in range(KD):
                    act.wait_ge(s["t_psum"], kt + 1)
                    nc.scalar.activation(xt[:, kt, :], pt[:, kt % 2, :], ACT.Copy).then_inc(s["t_ready"], 1)
                for t in range(T):
                    nc.scalar.activation(m.xhi[:, t, :], k.x[:, t, :], ACT.Copy).then_inc(s["x_hi"], 1)
                act.wait_ge(s["score_psum"], 1)
                nc.scalar.activation(sc[:, :, :], pr[:, 0:T * E].rearrange("p (t e) -> p t e", t=T),
                                     ACT.Sigmoid).then_inc(s["scored"], 1)

            @block.gpsimd
            def _(pool):
                for t in range(T):
                    pool.wait_ge(s["x_hi"], t + 1)
                    nc.gpsimd.tensor_tensor(m.xlo[:, t, :], k.x[:, t, :], m.xhi[:, t, :].bitcast(F32),
                                            ALU.subtract).then_inc(s["x_lo"], 1)

            @block.vector
            def _(dve):
                ch = Chain(dve, s["dve"])
                v = nc.vector
                tt, ts = v.tensor_tensor, v.tensor_scalar

                def tiles(x):
                    return x.unsqueeze(1).to_broadcast([P, T, x.shape[1]])

                def cols(x, n):
                    return x.unsqueeze(2).to_broadcast([P, T, n])

                dve.wait_ge(s["w_in"], 32)
                dve.wait_ge(s["scored"], 1)
                ch.link(tt(bi[:, :, :], sc[:, :, :], tiles(rb[:, :]), ALU.add))
                bg = bi[:, :, :].rearrange("p t (g e) -> p (t g) e", g=G)
                for n in range(T * G):
                    i = v.max(top[:, n, :], bg[:, n, :])
                ch.link(i)
                tg = top[:, :, :].rearrange("p (t g) e -> p t g e", t=T)
                ch.link(tt(gs[:, :, :], tg[:, :, :, 0], tg[:, :, :, 1], ALU.add))
                ch.link(v.reduce_max(r1[:, :], gs[:, :, :], axis=AX))
                ch.link(tt(geq[:, :, :], gs[:, :, :], cols(r1[:, :], G), ALU.is_equal))
                ch.link(tt(geq[:, :, :], geq[:, :, :], tiles(c["group_rev"]), ALU.mult))
                ch.link(v.reduce_max(r1[:, :], geq[:, :, :], axis=AX))
                ch.link(tt(geq[:, :, :], geq[:, :, :], cols(r1[:, :], G), ALU.is_equal))
                selg = sel[:, :, :].rearrange("p t (g e) -> p (t g) e", g=G)
                geqb = geq[:, :, :].rearrange("p t g -> p (t g)").unsqueeze(2).to_broadcast([P, T * G, E // G])
                ch.link(v.tensor_copy(selg, geqb))
                ch.link(tt(bi[:, :, :], bi[:, :, :], sel[:, :, :], ALU.mult))
                ch.link(ts(sel[:, :, :], sel[:, :, :], 1.0, -NEG, ALU.subtract, ALU.mult))
                ch.link(tt(bi[:, :, :], bi[:, :, :], sel[:, :, :], ALU.add))
                for t in range(T):
                    i = v.max(top2[:, t, :], bi[:, t, :])
                ch.link(i)
                for oh, n in ((oh0, 0), (oh1, 1)):
                    ch.link(tt(val[:, :, :], bi[:, :, :], cols(top2[:, :, n], E), ALU.is_equal))
                    if n:
                        ch.link(ts(sel[:, :, :], oh0[:, :, :], -1.0, 1.0, ALU.mult, ALU.add))
                        ch.link(tt(val[:, :, :], val[:, :, :], sel[:, :, :], ALU.mult))
                    ch.link(tt(val[:, :, :], val[:, :, :], tiles(c["expert_rev"]), ALU.mult))
                    ch.link(v.reduce_max(r1[:, :], val[:, :, :], axis=AX))
                    ch.link(tt(oh[:, :, :], val[:, :, :], cols(r1[:, :], E), ALU.is_equal))
                ch.link(tt(both[:, :, :], oh0[:, :, :], oh1[:, :, :], ALU.add))
                ch.link(v.memset(pref[:, 0, :], 0.0))
                for t in range(1, T):
                    ch.link(tt(pref[:, t, :], pref[:, t - 1, :], both[:, t - 1, :], ALU.add))
                tt(val[:, 0, :], pref[:, T - 1, :], both[:, T - 1, :], ALU.add).then_inc(s["counted"], 1)
                ch.link(tt(bi[:, :, :], both[:, :, :], sc[:, :, :], ALU.mult))
                ch.link(v.reduce_sum(r1[:, :], bi[:, :, :], axis=AX))
                ch.link(v.reciprocal(r1[:, :], r1[:, :]))
                tt(m.share[:, :, :], bi[:, :, :], cols(r1[:, :], E), ALU.mult)
                dve.wait_ge(s["rank_psum"], 1)
                ch.link(ts(m.rank[:, :, :], prk[:, 0:T * E].rearrange("p (t e) -> p t e", t=T), 1.0, None, ALU.add))
                ch.link(tt(m.rank[:, :, :], m.rank[:, :, :], both[:, :, :], ALU.mult))
                ts(m.rank[:, :, :], m.rank[:, :, :], 1.0, None, ALU.subtract)
                ch.link(v.reduce_max(cm[:, :], pcn[:, 0:E], axis=AX))
                ch.link(ts(edge[:, :], c["round_edges"], cm[:, 0:1], None, ALU.is_lt))
                ch.link(v.reduce_sum(cm[:, :], edge[:, :], axis=AX))
                v.tensor_copy(m.rounds[:, :], cm[:, :])
                v.tensor_copy(m.iota[:, :], c["slot_iota"])
                for t in range(T):
                    dve.wait_ge(s["x_lo"], t + 1)
                    i = ts(k.x[:, t, :], k.x[:, t, :], ALPHA, None, ALU.mult)
                ch.link(i)



def build_onehot(k, m, w, b, grp):
    v = k.nc.vector

    def wide(x):
        return x[:, :, bass.ds(grp * EPG, EPG)].unsqueeze(3).to_broadcast([P, T, EPG, CAP])
    slots = w.oh[:, b, :, :].rearrange("p t (e s) -> p t e s", e=EPG)
    iota = m.iota[:, :].unsqueeze(1).unsqueeze(1).to_broadcast([P, T, EPG, CAP])
    first = v.tensor_tensor(slots, wide(m.rank), iota, ALU.is_equal)

    def with_share():
        return v.tensor_tensor(w.ohg[:, b, :, :].rearrange("p t (e s) -> p t e s", e=EPG),
                               w.oh[:, b, :, :].bitcast(F32).rearrange("p t (e s) -> p t e s", e=EPG),
                               wide(m.share), ALU.mult)
    return first, with_share


def pick_rows(k, m, w, b):
    for half in range(2):
        for t in range(T):
            for n, x in enumerate((m.xhi, m.xlo)):
                i = k.nc.tensor.matmul(w.px[:, half, :], w.oh[:, b, t, :], x[:, t, half * 512:half * 512 + 512],
                                       start=(t == 0 and n == 0), stop=(t == T - 1 and n == 1))
    return i


def turn_rows(k, w):
    for kt in range(KD):
        i = k.nc.tensor.transpose(w.px[:, kt // 4, (kt % 4) * P:(kt % 4 + 1) * P], w.xg[:, kt::KD], k.c["ident"])
    return i


def gate_up(k, w, b, kt):
    u, j = kt // 2, kt % 2
    wv = k.ring[:, u * RW:(u + 1) * RW].rearrange("p (g e t f) -> p e t g f", g=2, e=EPG, t=2)
    for e in range(EPG):
        r = slice(CAP * e, CAP * e + CAP)
        i = k.nc.tensor.matmul(w.pgu[r, :], w.xt[:, b, kt, r], wv[:, e, j, :, :], start=(kt == 0),
                               stop=(kt == KD - 1))
    return i


def turn_hidden(k, w, b):
    for ft in range(2):
        i = k.nc.tensor.transpose(w.pht[:, ft * P:(ft + 1) * P], w.hid[:, b, ft::2], k.c["ident"])
    return i


def down(k, w, b, half):
    for ft in range(2):
        for e in range(EPG):
            r = slice(CAP * e, CAP * e + CAP)
            at = (4 + e // 2) * RW + (e % 2) * RW // 2 + ft * D + half * 512
            i = k.nc.tensor.matmul(w.po[r, half, :], w.ht[:, b, ft, r], k.ring[:, at:at + 512], start=(ft == 0),
                                   stop=(ft == 1))
    return i


def turn_onehot(k, w, b):
    for t in range(T):
        k.nc.tensor.transpose(w.px[:, 0, t * P:(t + 1) * P], w.oh[:, b, t, :].bitcast(F32), k.c["ident"])
    for t in range(T):
        i = k.nc.tensor.matmul(w.pht[:, 2 * P:2 * P + 1], w.ohg[:, b, t, :], k.c["ones"][:, 0:1],
                               start=(t == 0), stop=(t == T - 1))
    return i


def give_back(k, w, b, n):
    t, half = n // 2, n % 2
    for x, o in enumerate((w.ohi, w.olo)):
        i = k.nc.tensor.matmul(w.py[:, n % 2, :], w.oht[:, b, t, :], o[:, half, :], start=(x == 0), stop=(x == 1))
    return i


def take_in(k, w, n):
    xs = k.x[:, n // 2, (n % 2) * 512:(n % 2) * 512 + 512]
    return k.nc.vector.tensor_tensor(xs, xs, w.py[:, n % 2, :], ALU.add)


def experts(k, layer, m, w):
    nc, c = k.nc, k.c
    NB = 2 * T
    s = phase_sems(k, ("oh", "ohg", "picked", "xg_act", "xg_dve", "xt_psum", "xt_act", "xt_dve", "oht_psum", "oht",
                       "sg", "unit_used", "silu", "hidden", "ht_psum", "ht_ready", "o_psum", "o_hi", "o_lo",
                       "y_psum", "y_added"))
    fill0 = layer * NGRP
    last = NGRP // 2 - 1

    def each_group(eng, group):
        with eng.Fori(0, last) as j:
            group(0, j, True)
            group(1, j, True)
        group(0, last, True)
        group(1, last, False)

    @nc_block(k, s)
    def _(block):
        @block.sync
        def _(sp):
            with sp.Fori(0, NGRP - 1) as i:
                for u in range(UNITS):
                    if u < 4:
                        sp.wait_ge(s["unit_used"], i * 4 + (u + 1))
                    elif u == 4:
                        sp.wait_ge(s["o_psum"], i * 2 + 2)
                    ring_load(k, sp, layer, i + 1, u)

        @block.tensor
        def _(pe):
            def turned_onehot(b, n1):
                pe.wait_ge(s["xt_act"], n1)
                pe.wait_ge(s["ohg"], n1)
                pe.wait_ge(s["sg"], n1)
                turn_onehot(k, w, b).then_inc(s["oht_psum"], 1)

            def group(b, j, more):
                n = 2 * j + b
                pe.wait_ge(s["xt_act"], n + 1)
                pe.wait_ge(s["xt_dve"], n + 1)
                pe.wait_ge(s["hidden"], n + 1)
                for kt in range(KD):
                    u = kt // 2
                    if kt % 2 == 0:
                        pe.wait_ge(k.ring_full[u], fill_count(u) * (n + 1 + fill0))
                    i = gate_up(k, w, b, kt)
                    if kt % 2:
                        i.then_inc(s["unit_used"], 1)
                if more:
                    pe.wait_ge(s["oh"], n + 2)
                    pe.wait_ge(s["oht"], n + 1)
                    pick_rows(k, m, w, 1 - b).then_inc(s["picked"], 1)
                pe.wait_ge(s["hidden"], n + 2)
                turn_hidden(k, w, b).then_inc(s["ht_psum"], 1)
                if more:
                    pe.wait_ge(s["xg_act"], n + 2)
                    pe.wait_ge(s["xg_dve"], n + 2)
                    turn_rows(k, w).then_inc(s["xt_psum"], 1)
                for u in (4, 5):
                    pe.wait_ge(k.ring_full[u], fill_count(u) * (n + 1 + fill0))
                pe.wait_ge(s["ht_ready"], n + 1)
                pe.wait_ge(s["o_hi"], 2 * n + 1)
                pe.wait_ge(s["o_lo"], 2 * n + 1)
                down(k, w, b, 0).then_inc(s["o_psum"], 1)
                down(k, w, b, 1).then_inc(s["o_psum"], 1)
                if more:
                    turned_onehot(1 - b, n + 2)
                for i in range(NB):
                    if i < 2:
                        pe.wait_ge(s["o_hi"], 2 * n + 2 + i)
                        pe.wait_ge(s["o_lo"], 2 * n + 2 + i)
                    if i == 0:
                        pe.wait_ge(s["oht"], n + 1)
                    pe.wait_ge(s["y_added"], NB * n + (i + 1))
                    give_back(k, w, b, i).then_inc(s["y_psum"], 1)

            pe.wait_ge(s["oh"], 1)
            pick_rows(k, m, w, 0).then_inc(s["picked"], 1)
            pe.wait_ge(s["xg_act"], 1)
            pe.wait_ge(s["xg_dve"], 1)
            turn_rows(k, w).then_inc(s["xt_psum"], 1)
            turned_onehot(0, 1)
            each_group(pe, group)

        @block.scalar
        def _(act):
            act.sem_inc(s["o_hi"], 1)
            copy = nc.scalar.activation

            def xg(n1):
                act.wait_ge(s["picked"], n1)
                copy(w.xg[:, 0:512], w.px[:, 0, :], ACT.Copy).then_inc(s["xg_act"], 1)

            def xt(b, n1):
                act.wait_ge(s["xt_psum"], n1)
                copy(w.xt[:, b, 0:4, :], w.px[:, 0, :].rearrange("p (k s) -> p k s", k=4),
                     ACT.Copy).then_inc(s["xt_act"], 1)

            def oht(b, n1):
                act.wait_ge(s["oht_psum"], n1)
                copy(w.oht[:, b, :, :], w.px[:, 0, :].rearrange("p (t s) -> p t s", t=T),
                     ACT.Copy).then_inc(s["oht"], 1)

            def group(b, j, more):
                n = 2 * j + b
                act.wait_ge(s["unit_used"], 4 * n + 4)
                copy(w.gate[:, b, :], w.pgu[:, 0:FF], ACT.Silu).then_inc(s["silu"], 1)
                if more:
                    xg(n + 2)
                act.wait_ge(s["ht_psum"], n + 1)
                copy(w.ht[:, b, :, :], w.pht[:, 0:2 * P].rearrange("p (t s) -> p t s", t=2),
                     ACT.Copy).then_inc(s["ht_ready"], 1)
                if more:
                    xt(1 - b, n + 2)
                act.wait_ge(s["y_psum"], NB * n + 1)
                act.wait_ge(s["sg"], n + 2)
                for half in range(2):
                    act.wait_ge(s["o_psum"], 2 * n + half + 1)
                    copy(w.ohi[:, half, :], w.po[:, half, :], ACT.Copy,
                         scale=w.sg[:, b:b + 1]).then_inc(s["o_hi"], 1)
                if more:
                    oht(1 - b, n + 2)

            xg(1)
            xt(0, 1)
            oht(0, 1)
            each_group(act, group)

        @block.vector
        def _(dve):
            v = nc.vector
            for name, credit in (("hidden", 1), ("o_lo", 1), ("sg", 1), ("y_added", 2), ("y_psum", 1)):
                dve.sem_inc(s[name], credit)

            def onehots(b, grp, n1):
                first, with_share = build_onehot(k, m, w, b, grp)
                first.then_inc(s["oh"], 1)
                dve.wait_ge(s["oh"], n1)
                with_share().then_inc(s["ohg"], 1)

            def xg(n1):
                dve.wait_ge(s["picked"], n1)
                v.tensor_copy(w.xg[:, 512:D], w.px[:, 1, :]).then_inc(s["xg_dve"], 1)

            def xt(b, n1):
                dve.wait_ge(s["xt_psum"], n1)
                v.tensor_copy(w.xt[:, b, 4:8, :],
                              w.px[:, 1, :].rearrange("p (k s) -> p k s", k=4)).then_inc(s["xt_dve"], 1)

            def sg(b, n1):
                dve.wait_ge(s["oht_psum"], n1)
                v.tensor_copy(w.sg[:, b:b + 1], w.pht[:, 2 * P:2 * P + 1]).then_inc(s["sg"], 1)

            def group(b, j, more):
                n = 2 * j + b
                if more:
                    onehots(1 - b, n + 1, n + 2)
                dve.wait_ge(s["silu"], n + 1)
                v.tensor_tensor(w.hid[:, b, :], w.gate[:, b, :], w.pgu[:, FF:2 * FF],
                                ALU.mult).then_inc(s["hidden"], 1)
                if more:
                    xg(n + 2)
                    xt(1 - b, n + 2)
                for half in range(2):
                    dve.wait_ge(s["o_hi"], 2 * n + half + 2)
                    v.scalar_tensor_tensor(w.olo[:, half, :], w.po[:, half, :], w.sg[:, b:b + 1],
                                           w.ohi[:, half, :].bitcast(F32), ALU.mult,
                                           ALU.subtract).then_inc(s["o_lo"], 1)
                if more:
                    sg(1 - b, n + 2)
                for i in range(NB):
                    dve.wait_ge(s["y_psum"], NB * n + (i + 2))
                    take_in(k, w, i).then_inc(s["y_added"], 1)

            onehots(0, 0, 1)
            xg(1)
            xt(0, 1)
            sg(0, 1)
            each_group(dve, group)


def overflow_rounds(k, layer, m, w):
    nc = k.nc
    rounds = nc.values_load(m.rounds[0:1, 0:1], min_val=0, max_val=RNDS - 1)
    with nc.If(rounds > 0):
        with nc.Fori(0, rounds):
            with nc.Fori(0, NGRP) as g:
                overflow_group(k, layer, m, w, g)
    for e in (nc.sync, nc.tensor, nc.vector, nc.scalar, nc.gpsimd):
        e.nop()


def overflow_group(k, layer, m, w, g):
    nc = k.nc
    s = phase_sems(k, ("weights", "oh", "ohg", "picked", "xg", "xt_psum", "xt_ready", "oht_psum", "oht", "sg",
                       "gu_psum", "silu", "hidden", "ht_psum", "ht_ready", "o_psum", "o_hi", "o_lo", "y_psum",
                       "y_added", "next_slots"))

    @nc_block(k, s, repeated=True)
    def _(block):
        @block.sync
        def _(sp):
            for u in range(UNITS):
                ring_load(k, sp, layer, g, u, s["weights"])

        @block.tensor
        def _(pe):
            pe.wait_ge(s["oh"], 1)
            pick_rows(k, m, w, 0).then_inc(s["picked"], 1)
            pe.wait_ge(s["xg"], 2)
            turn_rows(k, w).then_inc(s["xt_psum"], 1)
            pe.wait_ge(s["xt_ready"], 2)
            pe.wait_ge(s["ohg"], 1)
            turn_onehot(k, w, 0).then_inc(s["oht_psum"], 1)
            pe.wait_ge(s["weights"], sum(fill_count(u) for u in range(UNITS)))
            for kt in range(KD):
                i = gate_up(k, w, 0, kt)
            i.then_inc(s["gu_psum"], 1)
            pe.wait_ge(s["hidden"], 1)
            turn_hidden(k, w, 0).then_inc(s["ht_psum"], 1)
            pe.wait_ge(s["ht_ready"], 1)
            down(k, w, 0, 0)
            down(k, w, 0, 1).then_inc(s["o_psum"], 1)
            pe.wait_ge(s["o_lo"], 2)
            pe.wait_ge(s["oht"], 1)
            for i in range(2 * T):
                if i >= 2:
                    pe.wait_ge(s["y_added"], i - 1)
                give_back(k, w, 0, i).then_inc(s["y_psum"], 1)

        @block.scalar
        def _(act):
            copy = nc.scalar.activation
            act.wait_ge(s["picked"], 1)
            for half in range(2):
                copy(w.xg[:, half * 512:half * 512 + 512], w.px[:, half, :], ACT.Copy).then_inc(s["xg"], 1)
            act.wait_ge(s["xt_psum"], 1)
            for half in range(2):
                copy(w.xt[:, 0, 4 * half:4 * half + 4, :], w.px[:, half, :].rearrange("p (k s) -> p k s", k=4),
                     ACT.Copy).then_inc(s["xt_ready"], 1)
            act.wait_ge(s["oht_psum"], 1)
            copy(w.oht[:, 0, :, :], w.px[:, 0, :].rearrange("p (t s) -> p t s", t=T), ACT.Copy).then_inc(s["oht"], 1)
            act.wait_ge(s["gu_psum"], 1)
            copy(w.gate[:, 0, :], w.pgu[:, 0:FF], ACT.Silu).then_inc(s["silu"], 1)
            act.wait_ge(s["ht_psum"], 1)
            copy(w.ht[:, 0, :, :], w.pht[:, 0:2 * P].rearrange("p (t s) -> p t s", t=2),
                 ACT.Copy).then_inc(s["ht_ready"], 1)
            act.wait_ge(s["o_psum"], 1)
            act.wait_ge(s["sg"], 1)
            for half in range(2):
                copy(w.ohi[:, half, :], w.po[:, half, :], ACT.Copy, scale=w.sg[:, 0:1]).then_inc(s["o_hi"], 1)

        @block.vector
        def _(dve):
            v = nc.vector
            step = k.c["round_step"][:, bass.ds(g, 1)]
            v.tensor_scalar(m.iota[:, :], m.iota[:, :], step, None, ALU.add).then_inc(s["next_slots"], 1)
            dve.wait_ge(s["next_slots"], 1)
            first, with_share = build_onehot(k, m, w, 0, g)
            first.then_inc(s["oh"], 1)
            dve.wait_ge(s["oh"], 1)
            with_share().then_inc(s["ohg"], 1)
            dve.wait_ge(s["oht_psum"], 1)
            v.tensor_copy(w.sg[:, 0:1], w.pht[:, 2 * P:2 * P + 1]).then_inc(s["sg"], 1)
            dve.wait_ge(s["silu"], 1)
            v.tensor_tensor(w.hid[:, 0, :], w.gate[:, 0, :], w.pgu[:, FF:2 * FF], ALU.mult).then_inc(s["hidden"], 1)
            for half in range(2):
                dve.wait_ge(s["o_hi"], half + 1)
                v.scalar_tensor_tensor(w.olo[:, half, :], w.po[:, half, :], w.sg[:, 0:1],
                                       w.ohi[:, half, :].bitcast(F32), ALU.mult, ALU.subtract).then_inc(s["o_lo"], 1)
            for i in range(2 * T):
                dve.wait_ge(s["y_psum"], i + 1)
                take_in(k, w, i).then_inc(s["y_added"], 1)


def kernel(**inputs):
    import concourse.bacc as _bacc
    from concourse.bass_utils import run_bass_kernel_spmd as _run

    def lay(name):
        return np.ascontiguousarray(np.asarray(inputs[name]))

    nc = _bacc.Bacc("TRN2", target_bir_lowering=False, num_devices=1)
    order = list(range(0, H, 2)) + list(range(1, H, 2))
    w_in = lay("hy_w_in")[0]
    gates = np.concatenate([w_in[:, 2048:2056][:, order], w_in[:, 2056:2064][:, order], w_in[:, 3600:3608]], 1)
    taps = lay("hy_conv_w")[0].reshape(CONV_K, NQKV, P).transpose(2, 0, 1).reshape(P, -1)
    rows = np.concatenate([np.repeat(np.float32([-1, 1, -1]), H), np.zeros(H, np.float32),
                           lay("gdn_dt_bias")[0][order], lay("fox_f_bias")[0], lay("gdn_a_log")[0][order],
                           lay("gdn_norm_w")[0]])
    params = np.concatenate([taps, np.broadcast_to(rows, (P, rows.size)),
                             lay("mla_q_norm")[0].reshape(-1, P).T, lay("mla_kv_norm")[0].reshape(-1, P).T], 1)
    uq = lay("mla_w_uq")[0].reshape(QL, MH, QK)
    ukv = lay("mla_w_ukv")[0].reshape(KVL, MH, 2 * NOPE)
    uq = np.concatenate([uq[:, :, :NOPE].reshape(QL, -1), uq[:, :, NOPE:].reshape(QL, -1)], 1)
    ukv = np.concatenate([ukv[:, :, :NOPE].reshape(KVL, -1), ukv[:, :, NOPE:].reshape(KVL, -1)], 1)
    host = {
        "const": const_array(),
        "params": np.ascontiguousarray(params),
        "w_gates": np.ascontiguousarray(gates.reshape(KD, P, 24).transpose(1, 0, 2).reshape(P, -1)),
        "x": lay("x")[0],
        "positions": lay("positions").astype(np.int32),
        "ln_gain": lay("ln_gain").reshape(2 * DEPTH, D),
        "ln_bias": lay("ln_bias").reshape(2 * DEPTH, D),
        "router_w": lay("router_w"),
        "router_bias": lay("router_bias")[None],
        "w_gate": lay("moe_w_gate").reshape(DEPTH * E, D, FF),
        "w_up": lay("moe_w_up").reshape(DEPTH * E, D, FF),
        "w_down": lay("moe_w_down").reshape(DEPTH * E, FF, D),
        "hy_w_in": w_in,
        "hy_w_out": lay("hy_w_out")[0],
        "mla_w_in": lay("mla_w_in")[0],
        "mla_w_uq": np.ascontiguousarray(uq),
        "mla_w_ukv": np.ascontiguousarray(ukv),
        "mla_w_out": lay("mla_w_out")[0],
    }
    a = {n: nc.dram_tensor(f"in_{n}", v.shape, mybir.dt.from_np(v.dtype), kind="ExternalInput").ap()
         for n, v in host.items()}
    out = nc.dram_tensor("out", [S, D], F32, kind="ExternalOutput").ap()
    build(nc, a, out)
    r = _run(nc, [{f"in_{n}": v for n, v in host.items()}], core_ids=[0])
    return r.results[0]["out"].reshape(1, S, D)
```

```python
from contextlib import ExitStack

import numpy as np

import concourse.bass as bass
from concourse import mybir

F32 = mybir.dt.float32
F32R = mybir.dt.float32r
I32 = mybir.dt.int32
ALU = mybir.AluOpType
ACT = mybir.ActivationFunctionType
AX = mybir.AxisListType.X

P = 128
S = 512
D = 1024
T = S // P
KD = D // P
DEPTH = 2
ALPHA = (2.0 * DEPTH) ** 0.25
LN_EPS = 1e-5
RMS_EPS = 1e-6
NEG = -1e30

H = 8
DH = 64
C = 64
NCH = S // C
CONV_K = 4
NQKV = 3 * H * DH // P

MH = 16
NOPE, ROPE = 64, 32
QK = NOPE + ROPE
QL, KVL = 512, 256
MIN = QL + KVL + ROPE

E = 64
G = 8
FF = 256
CAP = 32
EPG = 4
NGRP = E // EPG
RNDS = S // CAP
UNITS = 6
RW = EPG * D


def const_layout():
    widths = [("ident", P), ("ones", P), ("chunk_ones", P), ("chunk_incl", P), ("tri_incl", P),
              ("tri_strict", P), ("causal", P), ("first_half", P), ("second_half", P),
              ("rope_swap", P), ("ident64", C), ("chunk_neg", C), ("levels", 6 * C),
              ("expert_rev", E), ("group_rev", G), ("slot_iota", CAP), ("round_step", NGRP),
              ("round_edges", RNDS - 1), ("inv_freq", 1)]
    at, n = {}, 0
    for name, w in widths:
        at[name] = (n, n + w)
        n += w
    return at, n


def const_array():
    at, n = const_layout()
    c = np.zeros((P, n), np.float32)
    j, i = np.arange(P)[:, None], np.arange(P)[None, :]

    def put(name, a):
        c[:, at[name][0]:at[name][1]] = a

    put("ident", j == i)
    put("ones", np.ones((P, P)))
    put("chunk_ones", j // C == i // C)
    put("chunk_incl", (j // C == i // C) & (j <= i))
    put("tri_incl", j <= i)
    put("tri_strict", j < i)
    put("causal", np.where(i > j, NEG, 0.0))
    put("first_half", (j < C) * np.ones((1, P)))
    put("second_half", (j >= C) * np.ones((1, P)))
    half = ROPE // 2
    same = j // ROPE == i // ROPE
    put("rope_swap", np.where(same & (i % ROPE < half) & (j == i + half), -1.0,
                              np.where(same & (i % ROPE >= half) & (j == i - half), 1.0, 0.0)))
    jj, ii = np.arange(P)[:, None] % C, np.arange(C)[None, :]
    put("ident64", jj == ii)
    put("chunk_neg", np.where(jj <= ii, 0.0, NEG))
    lv = [(ii // (2 * s) == jj // (2 * s)) & (ii // s % 2 == 1) & (jj // s % 2 == 0)
          for s in (1, 2, 4, 8, 16, 32)]
    put("levels", np.concatenate([x.astype(np.float32) for x in lv], 1))
    put("expert_rev", E - np.arange(E)[None, :] + 0.0 * j)
    put("round_step", np.where(np.arange(NGRP)[None, :] == 0, CAP, 0) + 0.0 * j)
    put("group_rev", G - np.arange(G)[None, :] + 0.0 * j)
    put("slot_iota", np.arange(CAP)[None, :] + 0.0 * j)
    put("round_edges", CAP * np.arange(1, RNDS)[None, :] + 0.0 * j)
    fr = np.float32(10000.0) ** (-np.arange(0, ROPE, 2, dtype=np.float32) / np.float32(ROPE))
    put("inv_freq", np.tile(fr, P // half)[:, None])
    return c


class Named:
    pass


def keep_warm(nc, bank, c, width):
    nc.tensor.matmul(bank[:, 0:width], c["ones"], c["filler"][:, 0:width], start=True, stop=True)


class Chain:

    def __init__(self, eng, sem):
        self.eng, self.sem, self.n = eng, sem, 0

    def mark(self, ins):
        self.n += 1
        ins.then_inc(self.sem, 1)
        return self.n

    def link(self, ins):
        self.n += 1
        ins.then_inc(self.sem, 1)
        self.eng.wait_ge(self.sem, self.n)


def build(nc, a, out):
    with ExitStack() as outer:
        names = [0]

        def sem(name):
            names[0] += 1
            return outer.enter_context(nc.semaphore(f"{name}_{names[0]}"))

        def opened(stack):
            def sb(name, shape, dt=F32):
                names[0] += 1
                return stack.enter_context(nc.sbuf_tensor(f"{name}_{names[0]}", shape, dt))

            def ps(name, shape, dt=F32):
                names[0] += 1
                return stack.enter_context(nc.psum_tensor(f"{name}_{names[0]}", shape, dt))
            return sb, ps

        sb, _ = opened(outer)
        at, ncol = const_layout()
        cst = sb("cst", [P, ncol])
        k = Named()
        k.count, k.cleared = 0, []
        k.nc, k.a, k.out, k.opened = nc, a, out, opened
        k.cst, k.c = cst, {n: cst[:, x:y] for n, (x, y) in at.items()}
        k.c["filler"] = cst[:, 0:512]
        k.ring = sb("ring", [P, UNITS * RW])
        k.ring_full = [sem(f"ring_full{u}") for u in range(UNITS)]
        k.x = sb("x", [P, T, D])
        k.rounds = sb("rounds", [P, DEPTH], I32)
        hybrid_mixer(k)
        for layer in range(DEPTH):
            if layer == 1:
                latent_mixer(k)
            moe_layer(k, layer)


def ringview(kn, lo, words, pattern, **kw):
    return kn.ring[:, lo:lo + words].rearrange(pattern, **kw)



def hybrid_mixer(k):
    nc = k.nc
    W2 = KD * 512
    wb = [ringview(k, b * W2, W2, "p (k n) -> p k n", k=KD) for b in range(2)]
    qkvc = ringview(k, 2 * W2, NQKV * S, "p (n s) -> p n s", n=NQKV)
    base = 2 * W2 + NQKV * S
    z = ringview(k, base, T * 512, "p (t n) -> p t n", t=T)
    vf = ringview(k, base + 2048, T * 512, "p (t n) -> p t n", t=T)
    qf = ringview(k, base + 4096, 4 * S, "p (n s) -> p n s", n=4)
    kf = ringview(k, base + 6144, 4 * S, "p (n s) -> p n s", n=4)
    with ExitStack() as st:
        sb, _ = k.opened(st)
        prm = sb("params", [P, k.a["params"].shape[1]])
        gate = sb("gate", [P, T, 24])
        h = Named()
        h.wb, h.qkvc, h.z, h.vf, h.qf, h.kf, h.prm, h.gate = wb, qkvc, z, vf, qf, kf, prm, gate
        g = Named()
        g.beta, g.g, g.eg, g.etail, g.logf, g.beg, g.cneg, g.cpos = (
            sb(n, [P, T, H]) for n in ("beta", "g", "eg", "etail", "logf", "beg", "cneg", "cpos"))
        g.estate = sb("estate", [P, NCH, 4])
        hybrid_project(k, h, g)
        mix = sb("mix", [P, T, D])
        delta_rule(k, h, g, mix)
        forgetting_attention(k, h, g, mix)
        project_out(k, mix, k.a["hy_w_out"], h.wb[1], 0)


def hybrid_project(k, h, g):
    nc, c = k.nc, k.c
    with ExitStack() as st:
        sb, ps = k.opened(st)
        xhi, xlo = sb("xt_hi", [P, KD, S], F32R), sb("xt_lo", [P, KD, S], F32R)
        SLOTS = 4
        whi, wlo = sb("w_hi", [P, SLOTS, 1024], F32R), sb("w_lo", [P, SLOTS, 1024], F32R)
        wsm = sb("w_gates", [P, KD, 24])
        wsm_hi, wsm_lo = sb("w_gates_hi", [P, KD, 24], F32R), sb("w_gates_lo", [P, KD, 24], F32R)
        acc, sq, rt, logits = (k.x[:, i, :].rearrange("p (a i) -> p a i", a=2) for i in range(4))
        y, ny, e, s2, poly, sp_ = (sb(n, [P, T, 24]) for n in ("y", "ny", "e", "s2", "poly", "softplus"))
        ea = sb("ea", [P, H])
        ld, lf, pref, dif = (sb(n, [P, T, H]) for n in ("log_decay", "log_forget", "before", "dif"))
        pt = ps("pt", [P, 2, 512])
        pg = ps("pg", [P, 512])
        pgs = ps("pgs", [P, 512])
        pb = ps("pb", [P, 4, 512])
        s = phase_sems(k, (
            "const_in", "x_in", "wsm_in", "w_in0", "w_in1", "xt_psum", "xt_hi", "xt_lo", "w_hi", "w_lo",
            "unit_used", "gate_w_hi", "gate_w_lo", "gate_psum", "gate_rows", "gate_t_psum",
            "proj_psum", "conv_done", "silu_done", "copied", "dve", "squared", "summed", "eps_added", "rooted",
            "inverse", "normed", "gates_to_act", "gates_acted", "gates_to_pe", "gates_psum"))
        w_in = [s["w_in0"], s["w_in1"]]
        starts = [0, 512, 1024, 2064, 2576, 1536, 3088]
        NP = 4 * len(starts)
        NW = 20
        NN = 8
        NORM_AT = 12
        np_ = CONV_K * NQKV
        sgn, off, alog = h.prm[:, np_:np_ + 24], h.prm[:, np_ + 24:np_ + 48], h.prm[:, np_ + 48:np_ + 56]

        def wide(x):
            return x.unsqueeze(1).to_broadcast([P, T, x.shape[1]])

        def unit(x, n):
            a, b = (KD, P) if n < NW else (2, 512)
            return x[:, n % SLOTS, :].rearrange("p (a b) -> p a b", a=a)

        def unit_source(n):
            w, j = h.wb[(n // 4) % 2], n % 4
            return w[:, :, j * P:(j + 1) * P] if n < NW else w[:, 2 * j:2 * j + 2, :]

        def wait_used(eng, n):
            if n < NW or n % 4 == 3:
                eng.wait_ge(s["proj_psum"], n + 1)
            else:
                eng.wait_ge(s["unit_used"], 3 * (n // 4 - NW // 4) + n % 4 + 1)

        def wait_read(eng, n):
            if n < NQKV:
                eng.wait_ge(s["conv_done"], n + 1)
            else:
                eng.wait_ge(s["copied"], n - NQKV + 1 + 1)

        @nc_block(k, s)
        def _(block):
            @block.sync
            def _(sp):
                sp.dma_start(k.cst[:, :], k.a["const"]).then_inc(s["const_in"], 16)
                sp.dma_start(k.x[:, :, :], k.a["x"].rearrange("(t p) d -> p t d", p=P)).then_inc(s["x_in"], 16)
                for n, col in enumerate(starts):
                    if n >= 2:
                        sp.wait_ge(s["w_lo"], 4 * (n - 1))
                    src = k.a["hy_w_in"][:, col:col + 512].rearrange("(k p) n -> p k n", p=P)
                    sp.dma_start(h.wb[n % 2], src).then_inc(w_in[n % 2], 16)

            @block.tensor
            def _(pe):
                mm = nc.tensor.matmul
                pe.wait_ge(s["const_in"], 16)
                pe.wait_ge(s["x_in"], 16)
                for kt in range(KD):
                    if kt >= 2:
                        pe.wait_ge(s["xt_lo"], kt - 1)
                    for t in range(T):
                        last = nc.tensor.transpose(pt[:, kt % 2, t * P:(t + 1) * P],
                                                   k.x[:, t, kt * P:(kt + 1) * P], c["ident"])
                    last.then_inc(s["xt_psum"], 1)
                pe.wait_ge(s["xt_lo"], KD)
                pe.wait_ge(s["gate_w_lo"], 1)
                for kt in range(KD):
                    for m, (x, w) in enumerate(((xhi, wsm_hi), (xlo, wsm_hi), (xhi, wsm_lo))):
                        last = mm(pg[0:24, :], w[:, kt, :], x[:, kt, :], start=(kt == 0 and m == 0),
                                  stop=(kt == KD - 1 and m == 2))
                last.then_inc(s["gate_psum"], 1)
                for n in range(NP):
                    pe.wait_ge(s["w_lo"], n + 1)
                    parts = ((xhi, unit(whi, n)), (xlo, unit(whi, n)), (xhi, unit(wlo, n)))
                    if n < NW:
                        if n >= 4:
                            wait_read(pe, n - 4)
                        for kt in range(KD):
                            for m, (x, w) in enumerate(parts):
                                last = mm(pb[:, n % 4, :], w[:, kt, :], x[:, kt, :], start=(kt == 0 and m == 0),
                                          stop=(kt == KD - 1 and m == 2))
                        last.then_inc(s["proj_psum"], 1)
                    else:
                        q = n % 4
                        for t in range(T):
                            if q == 0:
                                wait_read(pe, n - 4 + t)
                            for kt in (0, 1):
                                for m, (x, w) in enumerate(parts):
                                    last = mm(pb[:, t, :], x[:, 2 * q + kt, t * P:(t + 1) * P], w[:, kt, :],
                                              start=(q == 0 and kt == 0 and m == 0), stop=(q == 3 and kt == 1 and m == 2))
                            if q == 3:
                                last.then_inc(s["proj_psum"], 1)
                        if q < 3:
                            last.then_inc(s["unit_used"], 1)
                    if n == 0:
                        pe.wait_ge(s["gate_rows"], 1)
                        for t in range(T):
                            last = nc.tensor.transpose(pg[:, t * 24:(t + 1) * 24], logits[0:24, 0, t * P:(t + 1) * P],
                                                       c["ident"][0:24, 0:24])
                        last.then_inc(s["gate_t_psum"], 1)
                    if n == 3:
                        pe.wait_ge(s["gates_to_pe"], 1)
                        w = T * H
                        for i, m in enumerate(("chunk_incl", "chunk_ones", "first_half", "second_half")):
                            mm(pgs[:, i * w:(i + 1) * w], c[m], ld[:, :, :], start=True, stop=True)
                        mm(pgs[:, 4 * w:5 * w], c["tri_incl"], lf[:, :, :], start=True, stop=False)
                        mm(pgs[:, 4 * w:5 * w], c["ones"], pref[:, :, :], start=False,
                           stop=True).then_inc(s["gates_psum"], 1)
                    i = n - NORM_AT
                    if 0 <= i < NN:
                        pe.wait_ge(s["squared"], i + 1)
                        if i >= 2:
                            pe.wait_ge(s["eps_added"], i - 1)
                        mm(pt[:, i % 2, :], c["chunk_ones"], sq[:, i % 2, :], start=True,
                           stop=True).then_inc(s["summed"], 1)

            @block.gpsimd
            def _(pool):
                for n in range(NP):
                    pool.wait_ge(s["w_hi"], n + 1)
                    nc.gpsimd.tensor_tensor(unit(wlo, n), unit_source(n), unit(whi, n).bitcast(F32),
                                            ALU.subtract).then_inc(s["w_lo"], 1)

            @block.vector
            def _(dve):
                ch = Chain(dve, s["dve"])
                v = nc.vector
                for kt in range(KD):
                    dve.wait_ge(s["xt_hi"], kt + 1)
                    v.tensor_tensor(xlo[:, kt, :], pt[:, kt % 2, :], xhi[:, kt, :].bitcast(F32),
                                    ALU.subtract).then_inc(s["xt_lo"], 1)
                dve.wait_ge(s["gate_w_hi"], 1)
                v.tensor_tensor(wsm_lo[:, :, :], wsm[:, :, :], wsm_hi[:, :, :].bitcast(F32),
                                ALU.subtract).then_inc(s["gate_w_lo"], 1)
                dve.wait_ge(s["wsm_in"], 32)
                cw = h.prm[:, 0:CONV_K * NQKV].rearrange("p (k n) -> p k n", k=CONV_K)

                def gate_logs():
                    dve.wait_ge(s["copied"], 1)
                    ch.link(v.tensor_tensor(y[:, :, :], h.gate[:, :, :], wide(off), ALU.add))
                    ch.link(v.tensor_tensor(y[:, :, :], y[:, :, :], wide(sgn), ALU.mult))
                    ch.link(v.tensor_scalar(ny[:, :, :], y[:, :, :], -1.0, None, ALU.mult))
                    v.tensor_tensor(ny[:, :, :], ny[:, :, :], y[:, :, :], ALU.max).then_inc(s["gates_to_act"], 1)
                    dve.wait_ge(s["gates_acted"], 1)
                    ch.link(v.tensor_scalar(s2[:, :, :], e[:, :, :], 2.0, None, ALU.add))
                    ch.link(v.reciprocal(s2[:, :, :], s2[:, :, :]))
                    ch.link(v.tensor_tensor(e[:, :, :], e[:, :, :], s2[:, :, :], ALU.mult))
                    ch.link(v.tensor_tensor(s2[:, :, :], e[:, :, :], e[:, :, :], ALU.mult))
                    ch.link(v.tensor_scalar(poly[:, :, :], s2[:, :, :], 1 / 17, 1 / 15, ALU.mult, ALU.add))
                    for d in (13, 11, 9, 7, 5, 3, 1):
                        ch.link(v.tensor_tensor(poly[:, :, :], poly[:, :, :], s2[:, :, :], ALU.mult))
                        ch.link(v.tensor_scalar(poly[:, :, :], poly[:, :, :], 1.0 / d, None, ALU.add))
                    ch.link(v.tensor_tensor(poly[:, :, :], poly[:, :, :], e[:, :, :], ALU.mult))
                    ch.link(v.tensor_scalar(sp_[:, :, :], y[:, :, :], 0.0, None, ALU.max))
                    ch.link(v.scalar_tensor_tensor(sp_[:, :, :], poly[:, :, :], 2.0, sp_[:, :, :], ALU.mult, ALU.add))
                    ch.link(v.tensor_scalar(ea[:, :], ea[:, :], -1.0, None, ALU.mult))
                    ch.link(v.tensor_tensor(ld[:, :, :], sp_[:, :, 8:16], wide(ea[:, :]), ALU.mult))
                    ch.link(v.tensor_scalar(lf[:, :, :], sp_[:, :, 16:24], -1.0, None, ALU.mult))
                    ch.link(v.memset(pref[:, 0, :], 0.0))
                    for t in range(1, T):
                        ch.link(v.tensor_tensor(pref[:, t, :], pref[:, t - 1, :], lf[:, t - 1, :], ALU.add))
                    v.nop().then_inc(s["gates_to_pe"], 1)

                def gate_sums():
                    dve.wait_ge(s["gates_psum"], 1)
                    w = T * H

                    def cols(n):
                        return pgs[:, n * w:(n + 1) * w].rearrange("p (t h) -> p t h", t=T)
                    ch.link(v.tensor_copy(g.g[:, :, :], cols(0)))
                    ch.link(v.tensor_tensor(dif[:, :, :], cols(1), g.g[:, :, :], ALU.subtract))
                    ch.link(v.tensor_copy(g.cpos[:, :, :], cols(4)))
                    ch.link(v.tensor_scalar(g.cneg[:, :, :], cols(4), -1.0, None, ALU.mult))
                    for par in range(2):
                        for cc in range(2):
                            ch.link(v.tensor_copy(g.estate[64 * par:64 * par + 64, cc::2, :],
                                                  cols(2 + cc)[64 * par:64 * par + 64, :, 4 * par:4 * par + 4]))
                    v.nop().then_inc(s["gates_to_act"], 1)
                    dve.wait_ge(s["gates_acted"], 2)
                    ch.link(v.tensor_tensor(g.beg[:, :, :], g.beta[:, :, :], g.eg[:, :, :], ALU.mult))

                gate_logs()
                for n in range(NQKV):
                    dve.wait_ge(s["proj_psum"], n + 1)
                    if n >= 2:
                        dve.wait_ge(s["silu_done"], n - 1)
                    u, o = pb[:, n % 4, :], acc[:, n % 2, :]
                    ch.link(v.tensor_scalar(o, u, cw[:, 3, n:n + 1], None, ALU.mult))
                    for tap in (2, 1, 0):
                        d = CONV_K - 1 - tap
                        ins = v.scalar_tensor_tensor(o[:, d:], u[:, 0:S - d], cw[:, tap, n:n + 1],
                                                     o[:, d:], ALU.mult, ALU.add)
                        if tap:
                            ch.link(ins)
                    ins.then_inc(s["conv_done"], 1)
                    if n == 1:
                        gate_sums()
                def add_eps(n):
                    dve.wait_ge(s["summed"], n + 1)
                    if n >= 2:
                        dve.wait_ge(s["normed"], n - 1)
                    v.tensor_scalar(rt[:, n % 2, :], pt[:, n % 2, :], RMS_EPS, None, ALU.add).then_inc(s["eps_added"], 1)

                def divide(n):
                    dve.wait_ge(s["rooted"], n + 1)
                    v.reciprocal(rt[:, n % 2, :], rt[:, n % 2, :]).then_inc(s["inverse"], 1)
                    dve.wait_ge(s["inverse"], n + 1)
                    v.scalar_tensor_tensor(h.qkvc[:, n, :], h.qkvc[:, n, :], DH ** -0.5 if n < 4 else 1.0,
                                           rt[:, n % 2, :], ALU.mult, ALU.mult).then_inc(s["normed"], 1)
                for n in range(NN):
                    add_eps(n)
                    if n >= 1:
                        divide(n - 1)
                divide(NN - 1)

            @block.scalar
            def _(act):
                copy = nc.scalar.activation
                act.dma_start(wsm[:, :, :], k.a["w_gates"].rearrange("p (k n) -> p k n", k=KD)).then_inc(s["wsm_in"], 16)
                act.dma_start(h.prm[:, :], k.a["params"]).then_inc(s["wsm_in"], 16)

                def round_w(n):
                    if n >= NP:
                        return
                    act.wait_ge(w_in[n // 4 % 2], 16 * (n // 8 + 1))
                    if n >= SLOTS:
                        wait_used(act, n - SLOTS)
                    copy(unit(whi, n), unit_source(n), ACT.Copy).then_inc(s["w_hi"], 1)

                def square(i):
                    if 0 <= i < NN:
                        if i >= 2:
                            act.wait_ge(s["summed"], i - 1)
                        copy(sq[:, i % 2, :], h.qkvc[:, i, :], ACT.Square).then_inc(s["squared"], 1)

                def root(i):
                    if 0 <= i < NN:
                        act.wait_ge(s["eps_added"], i + 1)
                        copy(rt[:, i % 2, :], rt[:, i % 2, :], ACT.Sqrt).then_inc(s["rooted"], 1)

                act.wait_ge(s["wsm_in"], 32)
                copy(wsm_hi[:, :, :], wsm[:, :, :], ACT.Copy).then_inc(s["gate_w_hi"], 1)
                for kt in range(KD):
                    act.wait_ge(s["xt_psum"], kt + 1)
                    copy(xhi[:, kt, :], pt[:, kt % 2, :], ACT.Copy).then_inc(s["xt_hi"], 1)
                for n in range(SLOTS - 1):
                    round_w(n)
                act.wait_ge(s["gate_psum"], 1)
                copy(logits[0:24, 0, :], pg[0:24, :], ACT.Copy).then_inc(s["gate_rows"], 1)
                round_w(SLOTS - 1)
                act.wait_ge(s["gate_t_psum"], 1)
                copy(h.gate[:, :, :], pg[:, 0:T * 24].rearrange("p (t g) -> p t g", t=T), ACT.Copy).then_inc(s["copied"], 1)
                act.wait_ge(s["gates_to_act"], 1)
                copy(ea[:, :], alog, ACT.Exp)
                copy(e[:, :, :], ny[:, :, :], ACT.Exp, scale=-1.0).then_inc(s["gates_acted"], 1)
                for n in range(NQKV):
                    if n:
                        round_w(n + SLOTS - 1)
                    act.wait_ge(s["conv_done"], n + 1)
                    copy(h.qkvc[:, n, :], acc[:, n % 2, :], ACT.Silu).then_inc(s["silu_done"], 1)
                    if n == 1:
                        act.wait_ge(s["gates_to_act"], 2)
                        copy(g.eg[:, :, :], g.g[:, :, :], ACT.Exp)
                        copy(g.etail[:, :, :], dif[:, :, :], ACT.Exp)
                        copy(g.estate[:, :, :], g.estate[:, :, :], ACT.Exp)
                        copy(g.beta[:, :, :], y[:, :, 0:8], ACT.Sigmoid, scale=-1.0).then_inc(s["gates_acted"], 1)
                    if n == NORM_AT - 1:
                        act.wait_ge(s["silu_done"], 1)
                        square(0)
                for n in range(NQKV, NP):
                    round_w(n + SLOTS - 1)
                    if n == NW:
                        root(NN - 1)
                    act.wait_ge(s["proj_psum"], n + 1)
                    ch, j = n // 4, n % 4
                    dst = {3: h.qf, 4: h.kf, 5: h.z, 6: h.vf}[ch][:, j, :]
                    copy(dst, pb[:, n % 4, :], ACT.Copy,
                         scale=DH ** -0.5 if ch == 3 else 1.0).then_inc(s["copied"], 1)
                    square(n - (NORM_AT - 1))
                    if n < NW:
                        root(n - (NORM_AT + 1))


def phase_sems(k, names):
    k.count += 1
    return {n: k.nc.alloc_semaphore(f"{n}_{k.count}") for n in names}


def clear(k, s):
    with k.nc.Block() as block:
        @block.vector
        def _(dve):
            for x in s.values():
                dve.sem_clear(x)
    for x in s.values():
        k.nc.release_semaphore(x)


def nc_block(k, s, repeated=False):
    def run(f):
        with k.nc.Block() as block:
            f(block)
        if repeated:
            clear(k, s)
        else:
            for x in s.values():
                k.nc.gpsimd.sem_clear(x)
            for x in k.cleared:
                k.nc.release_semaphore(x)
            k.cleared = list(s.values())
    return run


def delta_rule(k, h, g, mix):
    nc, c = k.nc, k.c
    HC = [P, 2, 4, C]
    with ExitStack() as st:
        sb, ps = k.opened(st)
        dg, db, dt, m, u, ti, y, kb, vb, uu, o1 = (
            sb(n, [P, H, C]) for n in ("diag_g", "diag_b", "decay", "m", "u", "t_inv", "y", "k_beta", "v_beta",
                                       "u_rows", "o_first"))
        ml, att = sb("m_level", [P, 2, H, C]), sb("attn_t", [P, 2, H, C])
        kt_, vn = sb("k_tail", [P, H * C]), sb("v_new", [P, H * C])
        wt = sb("w_t", [P, 2, 4, C])
        sq, ss = sb("square", [P, H * DH]), sb("sum_sq", [P, T * H])
        np_ = CONV_K * NQKV + 56
        gain = h.prm[:, np_:np_ + DH]
        state = sb("state", [P, 4, P])
        bank = ps("bank", [P, 8, 512])
        s = phase_sems(k, (
            "dve", "diags", "rows_psum", "expo", "decay", "gram_psum", "tok_psum", "tok_read", "m_ready",
            "u_ready", "t_psum",
            "t_copied", "m_level", "y_psum", "y_copied", "z_psum", "z2_psum", "t_grown", "u_grown", "wu_psum",
            "wu_copied", "state_ready", "ws_psum", "v_new", "kv_psum", "av_psum", "dve_end", "silu",
            "mean", "rooted"))

        def bk(n):
            return bank[:, n, :]

        def heads(n):
            return bk(n).rearrange("p (h i) -> p h i", h=H)

        def par2(n):
            return bank[:, n:n + 2, 0:4 * C].rearrange("p a (b i) -> p a b i", b=4)

        def hv(x):
            return x[:, :, :].rearrange("p (a b) i -> p a b i", a=2)

        def over_heads(x):
            return x.unsqueeze(1).to_broadcast([P, H, C])

        def over_cols(x):
            return x.unsqueeze(2).to_broadcast([P, H, C])

        LV = c["levels"].rearrange("p (l i) -> p l i", l=6)

        @nc_block(k, s)
        def _(block):
            @block.tensor
            def _(pe):
                mm = nc.tensor.matmul

                def rows(t):
                    pe.wait_ge(s["diags"], 2 * (t + 1))
                    mm(bk(1), c["chunk_ones"], dg[:, :, :], start=True, stop=True)
                    mm(bk(6), c["chunk_ones"], db[:, :, :], start=True, stop=True).then_inc(s["rows_psum"], 1)

                def gram(t, off):
                    if off:
                        pe.wait_ge(s["m_ready"], t + 1)
                    for b in range(4):
                        for cc in range(2):
                            for par in range(2):
                                r, w = slice(64 * par, 64 * par + 64), slice(64 * cc, 64 * cc + 64)
                                tc = slice(t * P + 64 * cc, t * P + 64 * cc + 64)
                                i = mm(par2(4)[w, par, b, :], h.qkvc[r, 4 + b, tc], h.qkvc[r, 4 + b + off, tc],
                                       start=True, stop=True)
                    i.then_inc(s["gram_psum"], 1)

                def token_major(t):
                    pe.wait_ge(s["m_ready"], t + 1)
                    for n, first in ((6, 4), (1, 8)):
                        for b in range(4):
                            i = nc.tensor.transpose(bk(n)[:, b * P:(b + 1) * P],
                                                    h.qkvc[:, first + b, t * P:(t + 1) * P], c["ident"])
                        i.then_inc(s["tok_psum"], 1)

                rows(0)
                gram(0, 0)
                gram(0, -4)
                token_major(0)
                for t in range(T):
                    def blocks(out, lhs, rhs, half):
                        for hp in range(4 * half, 4 * half + 4):
                            for cc in range(2):
                                w = slice(64 * cc, 64 * cc + 64)
                                i = mm(out[w, hp, :], lhs[w, hp, :], rhs(w, hp), start=True, stop=True)
                        return i
                    pe.wait_ge(s["u_ready"], t + 1)
                    for half in range(2):
                        i = blocks(heads(0), u, lambda w, hp: c["ident64"][w, :], half)
                    i.then_inc(s["t_psum"], 1)
                    for lv in range(1, 6):
                        n = 5 * t + lv
                        pe.wait_ge(s["m_level"], n)
                        if lv == 1:
                            pe.wait_ge(s["t_copied"], t + 1)
                            pe.wait_ge(s["tok_read"], t + 1)
                            if t:
                                pe.wait_ge(s["dve_end"], t)
                        for half in range(2):
                            if lv > 1:
                                pe.wait_ge(s["t_grown"], 8 * t + 2 * (lv - 2) + half + 1)
                            blocks(heads(half), ml[:, n % 2], lambda w, hp: ti[w, hp, :], half).then_inc(s["y_psum"], 1)
                        for half in range(2):
                            pe.wait_ge(s["y_copied"], 2 * (n - 1) + half + 1)
                            if lv > 1:
                                pe.wait_ge(s["u_grown"], 2 * (n - 2) + half + 1)
                            if lv < 5:
                                blocks(heads(2 + half), u, lambda w, hp: y[w, hp, :], half).then_inc(s["z_psum"], 1)
                            if lv == 5:
                                blocks(heads(4 + half), y, lambda w, hp: u[w, hp, :], half).then_inc(s["z2_psum"], 1)
                        for half in range(2):
                            if lv < 5:
                                blocks(heads(4 + half), y, lambda w, hp: u[w, hp, :], half).then_inc(s["z2_psum"], 1)
                    for hp in range(H):
                        if hp % 4 == 0:
                            pe.wait_ge(s["u_grown"], 2 * (5 * t + 4) + hp // 4 + 1)
                        par, b = hp // 4, hp % 4
                        for cc in range(2):
                            w = slice(64 * cc, 64 * cc + 64)
                            mm(bank[64 * par:64 * par + 64, 6 + cc, b * C:(b + 1) * C], kb[w, hp, :], u[w, hp, :],
                               start=True, stop=True)
                        for cc in range(2):
                            w = slice(64 * cc, 64 * cc + 64)
                            last = mm(heads(3)[w, 2 * b + par, :], u[w, hp, :], vb[w, hp, :], start=True, stop=True)
                    last.then_inc(s["wu_psum"], 1)
                    for cc in range(2):
                        n = 2 * t + cc
                        w = slice(64 * cc, 64 * cc + 64)
                        tc = slice(t * P + 64 * cc, t * P + 64 * cc + 64)
                        pe.wait_ge(s["state_ready"], n + 1)
                        if cc == 0:
                            pe.wait_ge(s["wu_copied"], 2 * (t + 1))
                        for b in range(4):
                            last = mm(bank[w, 0, b * P:(b + 1) * P], wt[:, cc, b, :], state[:, b, :],
                                      start=True, stop=True)
                        last.then_inc(s["ws_psum"], 1)
                        for b in range(4):
                            last = mm(bank[w, 2, b * P:(b + 1) * P], h.qkvc[:, b, tc], state[:, b, :],
                                      start=True, stop=True)
                        last.then_inc(s["ws_psum"], 1)
                        if t + 1 < T:
                            if cc == 0:
                                rows(t + 1)
                            else:
                                gram(t + 1, -4)
                        pe.wait_ge(s["v_new"], n + 1)
                        for b in range(4):
                            last = mm(bank[:, 7, b * P:(b + 1) * P], kt_[w, b * P:(b + 1) * P],
                                      vn[w, b * P:(b + 1) * P], start=True, stop=True)
                        last.then_inc(s["kv_psum"], 1)
                        if t + 1 < T:
                            if cc == 0:
                                gram(t + 1, 0)
                            else:
                                token_major(t + 1)
                    for hp in range(H):
                        own = slice((2 * (hp % 4) + hp // 4) * C, (2 * (hp % 4) + hp // 4 + 1) * C)
                        for cc in range(2):
                            w = slice(64 * cc, 64 * cc + 64)
                            last = mm(bk(3)[w, own], att[w, t % 2, hp, :], vn[w, own], start=True, stop=True)
                    last.then_inc(s["av_psum"], 1)

            @block.gpsimd
            def _(pool):
                for t in range(T):
                    pool.wait_ge(s["m_ready"], t + 1)
                    for lv in range(1, 6):
                        n = 5 * t + lv
                        if n > 2:
                            pool.wait_ge(s["y_psum"], 2 * (n - 2))
                        nc.gpsimd.tensor_tensor(ml[:, n % 2], m[:, :, :], over_heads(LV[:, lv, :]),
                                                ALU.mult).then_inc(s["m_level"], 1)

            @block.vector
            def _(dve):
                ch = Chain(dve, s["dve"])
                v = nc.vector
                tt = v.tensor_tensor
                ch.link(v.memset(state[:, :, :], 0.0))

                def diagonals(t):
                    tt(dg[:, :, :], over_heads(c["ident64"]), over_cols(g.g[:, t, :]), ALU.mult).then_inc(s["diags"], 1)
                    tt(db[:, :, :], over_heads(c["ident64"]), over_cols(g.beta[:, t, :]), ALU.mult).then_inc(s["diags"], 1)
                    ch.link(tt(dt[:, :, :], over_heads(c["chunk_neg"]), over_cols(g.g[:, t, :]), ALU.subtract))

                def exponents(t):
                    dve.wait_ge(s["rows_psum"], t + 1)
                    tt(dt[:, :, :], dt[:, :, :], heads(1), ALU.add).then_inc(s["expo"], 1)

                def make_m(t):
                    dve.wait_ge(s["decay"], t + 1)
                    dve.wait_ge(s["gram_psum"], 2 * t + 1)
                    ch.link(tt(hv(m), par2(4), hv(dt), ALU.mult))
                    tt(m[:, :, :], m[:, :, :], heads(6), ALU.mult).then_inc(s["m_ready"], 1)
                    dve.wait_ge(s["m_ready"], t + 1)
                    ch.link(tt(u[:, :, :], m[:, :, :], over_heads(LV[:, 0, :]), ALU.mult))
                    tt(u[:, :, :], over_heads(c["ident64"]), u[:, :, :], ALU.subtract).then_inc(s["u_ready"], 1)

                def make_attn(t):
                    dve.wait_ge(s["gram_psum"], 2 * t + 2)
                    ch.link(tt(att[:, t % 2, :, :].rearrange("p (a b) i -> p a b i", a=2), par2(4), hv(dt), ALU.mult))

                def token_major(t):
                    dve.wait_ge(s["tok_psum"], 2 * (t + 1))
                    ktok = bk(6).rearrange("p (b a d) -> p a b d", b=4, a=2)
                    vtok = bk(1).rearrange("p (b a d) -> p a b d", b=4, a=2)

                    def per_head(x):
                        return x.rearrange("p (a b) -> p a b", a=2).unsqueeze(3).to_broadcast(HC)
                    tt(kt_[:, :].rearrange("p (b a d) -> p a b d", b=4, a=2), ktok, per_head(g.etail[:, t, :]),
                       ALU.mult)
                    tt(hv(kb), ktok, per_head(g.beg[:, t, :]), ALU.mult)
                    tt(hv(vb), vtok, per_head(g.beta[:, t, :]), ALU.mult).then_inc(s["tok_read"], 1)

                def gated(t):
                    o = mix[:, t, 0:H * DH]
                    ch.link(tt(sq[:, :], o, o, ALU.mult))
                    v.reduce_sum(ss[:, t * H:(t + 1) * H], sq[:, :].rearrange("p (h d) -> p h d", h=H), axis=AX)
                    zt = h.z[:, t, :].rearrange("p (h d) -> p h d", h=H)
                    dve.wait_ge(s["silu"], 1)
                    ch.link(tt(zt, zt, gain.unsqueeze(1).to_broadcast([P, H, DH]), ALU.mult))
                    ch.link(tt(o, o, h.z[:, t, :], ALU.mult))

                diagonals(0)
                exponents(0)
                make_m(0)
                make_attn(0)
                token_major(0)
                for t in range(T):
                    if t + 1 < T:
                        diagonals(t + 1)
                    if t:
                        gated(t - 1)
                    for lv in range(1, 6):
                        n = 5 * t + lv
                        for half in range(2):
                            hh = slice(4 * half, 4 * half + 4)
                            if lv < 5:
                                dve.wait_ge(s["z_psum"], 8 * t + 2 * (lv - 1) + half + 1)
                                if lv == 1:
                                    dve.wait_ge(s["t_copied"], t + 1)
                                tt(ti[:, hh, :], ti[:, hh, :], heads(2 + half)[:, hh, :],
                                   ALU.subtract).then_inc(s["t_grown"], 1)
                        for half in range(2):
                            hh = slice(4 * half, 4 * half + 4)
                            dve.wait_ge(s["z2_psum"], 2 * (n - 1) + half + 1)
                            tt(u[:, hh, :], u[:, hh, :], heads(4 + half)[:, hh, :], ALU.subtract).then_inc(s["u_grown"], 1)
                    if t == 0:
                        v.nop().then_inc(s["state_ready"], 1)
                    for cc in range(2):
                        n = 2 * t + cc
                        w = slice(64 * cc, 64 * cc + 64)
                        if cc == 0:
                            dve.wait_ge(s["wu_copied"], 2 * (t + 1))
                        dve.wait_ge(s["ws_psum"], 2 * n + 1)
                        tt(vn[w, :], uu[w, :, :].rearrange("p h i -> p (h i)"), bank[w, 0, :],
                           ALU.subtract).then_inc(s["v_new"], 1)
                        dve.wait_ge(s["ws_psum"], 2 * n + 2)
                        ch.link(tt(state[:, :, :], state[:, :, :],
                                   g.estate[:, n, :].unsqueeze(2).to_broadcast([P, 4, P]), ALU.mult))
                        e = g.eg[w, t, :].rearrange("p (a b) -> p b a", a=2).unsqueeze(3).to_broadcast([64, 4, 2, C])
                        ch.link(tt(o1[w, :, :].rearrange("p (b a) d -> p b a d", b=4),
                                   bank[w, 2, :].rearrange("p (b a d) -> p b a d", b=4, a=2), e, ALU.mult))
                        if cc == 0 and t + 1 < T:
                            exponents(t + 1)
                        dve.wait_ge(s["kv_psum"], n + 1)
                        for par in range(2):
                            r = slice(64 * par, 64 * par + 64)
                            own = state[r, :, r]
                            i = tt(own, own, bank[r, 7, :].rearrange("p (b i) -> p b i", b=4)[:, :, r], ALU.add)
                        i.then_inc(s["state_ready"], 1)
                        dve.wait_ge(s["state_ready"], n + 2)
                        if t + 1 < T:
                            if cc == 0:
                                make_m(t + 1)
                            else:
                                make_attn(t + 1)
                                token_major(t + 1)
                    dve.wait_ge(s["av_psum"], t + 1)
                    tt(mix[:, t, 0:H * DH], o1[:, :, :].rearrange("p h d -> p (h d)"), bk(3),
                       ALU.add).then_inc(s["dve_end"], 1)
                    dve.wait_ge(s["dve_end"], t + 1)
                gated(T - 1)
                v.tensor_scalar(ss[:, :], ss[:, :], 1.0 / DH, RMS_EPS, ALU.mult, ALU.add).then_inc(s["mean"], 1)
                dve.wait_ge(s["rooted"], 1)
                ch.link(v.reciprocal(ss[:, :], ss[:, :]))
                for t in range(T):
                    ot = mix[:, t, 0:H * DH].rearrange("p (h d) -> p h d", h=H)
                    i = tt(ot, ot, ss[:, t * H:(t + 1) * H].unsqueeze(2).to_broadcast([P, H, DH]), ALU.mult)
                ch.link(i)

            @block.scalar
            def _(act):
                copy = nc.scalar.activation

                def decay(t):
                    act.wait_ge(s["expo"], t + 1)
                    copy(dt[:, :, :], dt[:, :, :], ACT.Exp).then_inc(s["decay"], 1)

                copy(h.z[:, :, :], h.z[:, :, :], ACT.Silu).then_inc(s["silu"], 1)
                decay(0)
                for t in range(T):
                    act.wait_ge(s["t_psum"], t + 1)
                    copy(ti[:, :, :], heads(0), ACT.Copy).then_inc(s["t_copied"], 1)
                    for lv in range(1, 6):
                        n = 5 * t + lv
                        for half in range(2):
                            hh = slice(4 * half, 4 * half + 4)
                            act.wait_ge(s["y_psum"], 2 * (n - 1) + half + 1)
                            copy(y[:, hh, :], heads(half)[:, hh, :], ACT.Copy).then_inc(s["y_copied"], 1)
                    act.wait_ge(s["wu_psum"], t + 1)
                    copy(wt[:, :, :, :], bank[:, 6:8, 0:4 * C].rearrange("p c (b i) -> p c b i", b=4),
                         ACT.Copy).then_inc(s["wu_copied"], 1)
                    copy(uu[:, :, :], heads(3), ACT.Copy).then_inc(s["wu_copied"], 1)
                    if t + 1 < T:
                        decay(t + 1)
                act.wait_ge(s["mean"], 1)
                copy(ss[:, :], ss[:, :], ACT.Sqrt).then_inc(s["rooted"], 1)


def forgetting_attention(k, h, g, mix):
    def q_of(hd, t):
        return h.qf[64 * (hd % 2):64 * (hd % 2) + 64, hd // 2, t * P:(t + 1) * P]

    def k_of(hd, n):
        return h.kf[64 * (hd % 2):64 * (hd % 2) + 64, hd // 2, 0:n]

    def v_of(hd, kb):
        return h.vf[:, kb, hd * DH:(hd + 1) * DH]

    def out_of(hd, t):
        return mix[:, t, H * DH + hd * DH:H * DH + (hd + 1) * DH]
    attention(k, H, k.a["hy_w_out"], h.wb[1], q_of, k_of, v_of, out_of, 1.0, g)


def attention(k, nh, w_next, w_place, q_of, k_of, v_of, out_of, scale, gates=None):
    nc, c = k.nc, k.c
    N = nh * T
    with ExitStack() as st:
        sb, ps = k.opened(st)
        pr = sb("probs", [P, 2, S])
        prt = sb("probs_t", [P, 2, S])
        mx = sb("row_max", [P, 4])
        rs = sb("row_sum", [P, 4])
        ri = sb("row_inv", [P, 4])
        if gates is not None:
            lg = sb("logits", [P, 2, S])
            dg = sb("diag_c", [P, 2, S])
            ck = sb("c_rows", [P, 2, S])
            ckm = sb("c_rows_causal", [P, 2, S])
            pck = ps("pck", [P, 512])
        pl = ps("pl", [P, 2, 512])
        pt = ps("pt", [P, 2, 512])
        po = ps("po", [P, 2, 512])
        spare = ps("spare", [P, 512])
        s = phase_sems(k, (
            "logit_psum", "masked", "maxed", "probs", "pt_psum", "pt_copied", "o_psum", "o_copied", "dve",
            "diag", "rows_psum", "rows", "rows_causal", "w_in"))

        def size(n):
            return (n % T + 1) * P

        @nc_block(k, s)
        def _(block):
            @block.sync
            def _(sp):
                load_w_out(k, sp, w_next, 0, w_place, s["w_in"])
                if gates is not None:
                    sp.dma_start(k.x[:, :, :], k.a["x"].rearrange("(t p) d -> p t d", p=P)).then_inc(s["w_in"], 16)
                sp.wait_ge(s["w_in"], 32 if gates is not None else 16)

            @block.tensor
            def _(pe):
                def rows(hd):
                    pe.wait_ge(s["diag"], hd + 1)
                    if hd:
                        pe.wait_ge(s["rows"], hd)
                    nc.tensor.matmul(pck[:, :], c["ones"], dg[:, hd % 2, :], start=True,
                                     stop=True).then_inc(s["rows_psum"], 1)

                def logits(n):
                    if n >= 2:
                        pe.wait_ge(s["masked"] if gates is not None else s["probs"], n - 1)
                    nc.tensor.matmul(pl[:, n % 2, 0:size(n)], q_of(n // T, n % T), k_of(n // T, size(n)),
                                     start=True, stop=True).then_inc(s["logit_psum"], 1)

                def transposes(n):
                    pe.wait_ge(s["probs"], n + 1)
                    if n >= 2:
                        pe.wait_ge(s["pt_copied"], n - 1)
                    for kb in range(n % T + 1):
                        last = nc.tensor.transpose(pt[:, n % 2, kb * P:(kb + 1) * P],
                                                   pr[:, n % 2, kb * P:(kb + 1) * P], c["ident"])
                    last.then_inc(s["pt_psum"], 1)

                def values(n):
                    pe.wait_ge(s["pt_copied"], n + 1)
                    if n >= 2:
                        pe.wait_ge(s["o_copied"], n - 1)
                    nb = n % T + 1
                    for kb in range(nb):
                        last = nc.tensor.matmul(po[:, n % 2, 0:DH], prt[:, n % 2, kb * P:(kb + 1) * P],
                                                v_of(n // T, kb), start=(kb == 0), stop=(kb == nb - 1))
                    last.then_inc(s["o_psum"], 1)

                for n in range(N + 2):
                    if gates is not None and n == 0:
                        rows(0)
                    if gates is not None and n % T == 1 and n // T + 1 < nh:
                        rows(n // T + 1)
                    if n < N:
                        logits(n)
                    keep_warm(nc, spare, c, 512 if n == 1 else 128)
                    if 1 <= n <= N:
                        transposes(n - 1)
                    if n >= 2:
                        values(n - 2)

            @block.vector
            def _(dve):
                ch = Chain(dve, s["dve"])
                v = nc.vector

                def diag(hd):
                    if hd >= 2:
                        dve.wait_ge(s["rows_psum"], hd - 1)
                    v.tensor_tensor(dg[:, hd % 2, :].rearrange("p (t i) -> p t i", t=T),
                                    c["ident"].unsqueeze(1).to_broadcast([P, T, P]),
                                    gates.cneg[:, :, hd].unsqueeze(2).to_broadcast([P, T, P]),
                                    ALU.mult).then_inc(s["diag"], 1)

                def invert(n):
                    dve.wait_ge(s["probs"], n + 1)
                    return ch.mark(v.reciprocal(ri[:, n % 4:n % 4 + 1], rs[:, n % 4:n % 4 + 1]))

                def normalise(n, inverted):
                    dve.wait_ge(s["o_psum"], n + 1)
                    dve.wait_ge(s["dve"], inverted)
                    v.tensor_scalar(out_of(n // T, n % T), po[:, n % 2, 0:DH], ri[:, n % 4:n % 4 + 1], None,
                                    ALU.mult).then_inc(s["o_copied"], 1)

                if gates is not None:
                    diag(0)
                for n in range(N):
                    hd, t, w = n // T, n % T, size(n)
                    if gates is not None and t == 0 and hd + 1 < nh:
                        diag(hd + 1)
                    dve.wait_ge(s["logit_psum"], n + 1)
                    if gates is not None:
                        if n >= 2:
                            dve.wait_ge(s["probs"], n - 1)
                        cq = gates.cpos[:, t, hd:hd + 1]
                        if t:
                            dve.wait_ge(s["rows"], hd + 1)
                            v.scalar_tensor_tensor(lg[:, n % 2, 0:t * P], pl[:, n % 2, 0:t * P], cq,
                                                   ck[:, hd % 2, 0:t * P], ALU.add, ALU.add)
                        dve.wait_ge(s["rows_causal"], hd + 1)
                        v.scalar_tensor_tensor(lg[:, n % 2, t * P:w], pl[:, n % 2, t * P:w], cq,
                                               ckm[:, hd % 2, t * P:w], ALU.add, ALU.add).then_inc(s["masked"], 1)
                        src = lg[:, n % 2, 0:w]
                    else:
                        v.tensor_tensor(pl[:, n % 2, t * P:w], pl[:, n % 2, t * P:w], c["causal"],
                                        ALU.add).then_inc(s["masked"], 1)
                        src = pl[:, n % 2, 0:w]
                    if n >= 3:
                        inverted = invert(n - 3)
                    dve.wait_ge(s["masked"], n + 1)
                    m = mx[:, n % 4:n % 4 + 1]
                    reduced = ch.mark(v.reduce_max(m, src, axis=AX))
                    if n >= 3:
                        normalise(n - 3, inverted)
                    dve.wait_ge(s["dve"], reduced)
                    v.tensor_scalar(m, m, -scale, None, ALU.mult).then_inc(s["maxed"], 1)
                for n in range(N - 3, N):
                    normalise(n, invert(n))

            if gates is not None:
                @block.gpsimd
                def _(pool):
                    for hd in range(nh):
                        pool.wait_ge(s["rows"], hd + 1)
                        if hd >= 2:
                            pool.wait_ge(s["masked"], T * (hd - 1))
                        nc.gpsimd.tensor_tensor(ckm[:, hd % 2, :].rearrange("p (t i) -> p t i", t=T),
                                                ck[:, hd % 2, :].rearrange("p (t i) -> p t i", t=T),
                                                c["causal"].unsqueeze(1).to_broadcast([P, T, P]),
                                                ALU.add).then_inc(s["rows_causal"], 1)

            @block.scalar
            def _(act):
                def copy_rows(hd):
                    act.wait_ge(s["rows_psum"], hd + 1)
                    if hd >= 2:
                        act.wait_ge(s["masked"], T * (hd - 1))
                        act.wait_ge(s["rows_causal"], hd - 1)
                    nc.scalar.activation(ck[:, hd % 2, :], pck[:, :], ACT.Copy).then_inc(s["rows"], 1)

                def copy_pt(n):
                    act.wait_ge(s["pt_psum"], n + 1)
                    if n >= 2:
                        act.wait_ge(s["o_psum"], n - 1)
                    nc.scalar.activation(prt[:, n % 2, 0:size(n)], pt[:, n % 2, 0:size(n)],
                                         ACT.Copy).then_inc(s["pt_copied"], 1)

                for n in range(N):
                    if gates is not None and n == 0:
                        copy_rows(0)
                    if gates is not None and n % T == 2 and n // T + 1 < nh:
                        copy_rows(n // T + 1)
                    act.wait_ge(s["maxed"], n + 1)
                    if n >= 2:
                        act.wait_ge(s["pt_psum"], n - 1)
                    src = (lg if gates is not None else pl)[:, n % 2, 0:size(n)]
                    nc.scalar.activation(pr[:, n % 2, 0:size(n)], src, ACT.Exp, bias=mx[:, n % 4:n % 4 + 1],
                                         scale=scale, accum_out=rs[:, n % 4:n % 4 + 1]).then_inc(s["probs"], 1)
                    if n >= 1:
                        copy_pt(n - 1)
                copy_pt(N - 1)


def load_w_out(k, sp, w_out, half, dst, sem):
    src = w_out.rearrange("(k p) n -> p k n", p=P)[:, :, half * 512:half * 512 + 512]
    sp.dma_start(dst, src).then_inc(sem, 16)


def project_out(k, mix, w_out, first, ln):
    nc, c = k.nc, k.c
    W2 = KD * 512
    with ExitStack() as st:
        sb, ps = k.opened(st)
        second = ringview(k, 0, W2, "p (k n) -> p k n", k=KD)
        l = norm_buffers(k, sb, ringview(k, 2 * W2, 2 * D, "p (a n) -> p a n", a=2))
        mhi, mlo = sb("mix_hi", [P, KD, S], F32R), sb("mix_lo", [P, KD, S], F32R)
        whi, wlo = sb("w_hi", [P, 4, 2, 512], F32R), sb("w_lo", [P, 4, 2, 512], F32R)
        pt = ps("pt", [P, 2, 512])
        py = ps("py", [P, 4, 512])
        s = phase_sems(k, ("w_in", "t_psum", "t_hi", "t_lo", "w_hi", "w_lo", "unit_used", "y_psum",
                           "added") + NORM_SEMS)

        def unit_source(n):
            return (first, second)[n // 4][:, 2 * (n % 4):2 * (n % 4) + 2, :]

        @nc_block(k, s)
        def _(block):
            @block.sync
            def _(sp):
                load_w_out(k, sp, w_out, 1, second, s["w_in"])
                load_norm(k, sp, l, s, ln)

            @block.tensor
            def _(pe):
                mm = nc.tensor.matmul
                for kt in range(KD):
                    if kt >= 2:
                        pe.wait_ge(s["t_lo"], kt - 1)
                    for t in range(T):
                        last = nc.tensor.transpose(pt[:, kt % 2, t * P:(t + 1) * P], mix[:, t, kt * P:(kt + 1) * P],
                                                   c["ident"])
                    last.then_inc(s["t_psum"], 1)

                def products(t, q, first_one, last_one):
                    for kt in (0, 1):
                        for m, (x, w) in enumerate(((mhi, whi), (mlo, whi), (mhi, wlo))):
                            i = mm(py[:, t, :], x[:, 2 * q + kt, t * P:(t + 1) * P], w[:, q, kt, :],
                                   start=(first_one and kt == 0 and m == 0), stop=(last_one and kt == 1 and m == 2))
                    return i
                pe.wait_ge(s["t_lo"], KD)
                for q in range(4):
                    pe.wait_ge(s["w_lo"], q + 1)
                    for t in range(T):
                        i = products(t, q, q == 0, q == 3)
                        if q == 3:
                            i.then_inc(s["y_psum"], 1)
                    if q < 3:
                        i.then_inc(s["unit_used"], 1)
                for t in range(T):
                    pe.wait_ge(s["added"], t + 1)
                    for q in range(4):
                        if t == 0:
                            pe.wait_ge(s["w_lo"], 4 + q + 1)
                        i = products(t, q, q == 0, q == 3)
                    i.then_inc(s["y_psum"], 1)

            @block.scalar
            def _(act):
                copy = nc.scalar.activation
                for kt in range(KD):
                    act.wait_ge(s["t_psum"], kt + 1)
                    copy(mhi[:, kt, :], pt[:, kt % 2, :], ACT.Copy).then_inc(s["t_hi"], 1)
                    if kt % 2:
                        copy(whi[:, kt // 2, :, :], unit_source(kt // 2), ACT.Copy).then_inc(s["w_hi"], 1)
                act.wait_ge(s["w_in"], 16)
                for n in range(4, 8):
                    if n < 7:
                        act.wait_ge(s["unit_used"], n - 3)
                    else:
                        act.wait_ge(s["y_psum"], T)
                    copy(whi[:, n % 4, :, :], unit_source(n), ACT.Copy).then_inc(s["w_hi"], 1)
                norm_act(k, act, l, s)

            @block.gpsimd
            def _(pool):
                def rest(n):
                    pool.wait_ge(s["w_hi"], n + 1)
                    nc.gpsimd.tensor_tensor(wlo[:, n % 4, :, :], unit_source(n), whi[:, n % 4, :, :].bitcast(F32),
                                            ALU.subtract).then_inc(s["w_lo"], 1)
                for n in range(7):
                    rest(n)
                norm_pool(k, pool, l, s)

            @block.vector
            def _(dve):
                v = nc.vector
                for kt in range(KD):
                    dve.wait_ge(s["t_hi"], kt + 1)
                    v.tensor_tensor(mlo[:, kt, :], pt[:, kt % 2, :], mhi[:, kt, :].bitcast(F32),
                                    ALU.subtract).then_inc(s["t_lo"], 1)
                def add(t, half):
                    dve.wait_ge(s["y_psum"], T * half + t + 1)
                    xs = k.x[:, t, half * 512:half * 512 + 512]
                    v.scalar_tensor_tensor(xs, xs, ALPHA, py[:, t, :], ALU.mult, ALU.add).then_inc(s["added"], 1)
                for t in range(T):
                    add(t, 0)
                    if t == 0:
                        dve.wait_ge(s["w_lo"], 7)
                        dve.wait_ge(s["w_hi"], 8)
                        v.tensor_tensor(wlo[:, 3, :, :], unit_source(7), whi[:, 3, :, :].bitcast(F32),
                                        ALU.subtract).then_inc(s["w_lo"], 1)

                def ready(t):
                    add(t, 1)
                    dve.wait_ge(s["added"], T + t + 1)
                norm_dve(k, dve, l, s, ready)


NORM_SEMS = ("gain_in", "dve", "var_ready", "rooted", "scales", "normed", "scaled", "shifted")


def norm_buffers(k, sb, gain_bias):
    l = Named()
    l.gain, l.bias = gain_bias[:, 0, :], gain_bias[:, 1, :]
    l.stats, l.mv = sb("stats", [P, T, 2, 6]), sb("mean_var", [P, T, 2])
    l.rstd, l.nmr = sb("rstd", [P, T]), sb("minus_mean_rstd", [P, T])
    return l


def load_norm(k, sp, l, s, ln):
    sp.dma_start(l.gain, k.a["ln_gain"][ln:ln + 1, :].to_broadcast([P, D])).then_inc(s["gain_in"], 16)
    sp.dma_start(l.bias, k.a["ln_bias"][ln:ln + 1, :].to_broadcast([P, D])).then_inc(s["gain_in"], 16)


def norm_dve(k, dve, l, s, ready):
    v = k.nc.vector
    ch = Chain(dve, s["dve"])

    def gain(t):
        if t == 0:
            dve.wait_ge(s["gain_in"], 32)
        dve.wait_ge(s["normed"], t + 1)
        v.tensor_tensor(k.x[:, t, :], k.x[:, t, :], l.gain, ALU.mult).then_inc(s["scaled"], 1)

    for t in range(T):
        ready(t)
        for hf in range(2):
            i = v.bn_stats(l.stats[:, t, hf, :], k.x[:, t, hf * 512:hf * 512 + 512])
        ch.link(i)
        ch.link(v.bn_aggr(l.mv[:, t, :], l.stats[:, t, :, :]))
        r = l.rstd[:, t:t + 1]
        v.tensor_scalar(r, l.mv[:, t, 1:2], LN_EPS, None, ALU.add).then_inc(s["var_ready"], 1)
        if t:
            gain(t - 1)
        dve.wait_ge(s["rooted"], t + 1)
        ch.link(v.reciprocal(r, r))
        v.scalar_tensor_tensor(l.nmr[:, t:t + 1], l.mv[:, t, 0:1], -1.0, r, ALU.mult, ALU.mult).then_inc(s["scales"], 1)
    gain(T - 1)


def norm_act(k, act, l, s):
    a = k.nc.scalar.activation
    for t in range(T):
        act.wait_ge(s["var_ready"], t + 1)
        a(l.rstd[:, t:t + 1], l.rstd[:, t:t + 1], ACT.Sqrt).then_inc(s["rooted"], 1)
        act.wait_ge(s["scales"], t + 1)
        a(k.x[:, t, :], k.x[:, t, :], ACT.Identity, scale=l.rstd[:, t:t + 1],
          bias=l.nmr[:, t:t + 1]).then_inc(s["normed"], 1)


def norm_pool(k, pool, l, s):
    pool.wait_ge(s["gain_in"], 32)
    for t in range(T):
        pool.wait_ge(s["scaled"], t + 1)
        k.nc.gpsimd.tensor_tensor(k.x[:, t, :], k.x[:, t, :], l.bias, ALU.add).then_inc(s["shifted"], 1)


def layer_norm(k, ln, rows_out):
    nc = k.nc
    with ExitStack() as st:
        sb, _ = k.opened(st)
        l = norm_buffers(k, sb, sb("gain_bias", [P, 2, D])[:, :, :])
        s = phase_sems(k, NORM_SEMS + ("stored",))

        @nc_block(k, s)
        def _(block):
            @block.sync
            def _(sp):
                load_norm(k, sp, l, s, ln)
                if rows_out is not None:
                    for t in range(T):
                        sp.wait_ge(s["shifted"], t + 1)
                        sp.dma_start(rows_out[t * P:(t + 1) * P, :], k.x[:, t, :]).then_inc(s["stored"], 16)
                    sp.wait_ge(s["stored"], 16 * T)

            @block.vector
            def _(dve):
                norm_dve(k, dve, l, s, lambda t: None)

            @block.scalar
            def _(act):
                norm_act(k, act, l, s)

            @block.gpsimd
            def _(pool):
                norm_pool(k, pool, l, s)



def latent_mixer(k):
    nc = k.nc
    with ExitStack() as st:
        sb, _ = k.opened(st)
        cthi, ctlo = sb("c_t_hi", [P, 6, S], F32R), sb("c_t_lo", [P, 6, S], F32R)
        wuq = sb("w_uq", [P, QL // P, MH * QK])
        wukv = sb("w_ukv", [P, KVL // P, MH * 2 * NOPE])
        spare = ringview(k, 5 * KD * 512, 8 * S, "p (n s) -> p n s", n=8)
        cos, sin = spare[:, 0, :], spare[:, 1, :]
        kr = sb("k_rope", [P, S])
        h = Named()
        h.cthi, h.ctlo, h.wuq, h.wukv, h.cos, h.sin, h.kr = cthi, ctlo, wuq, wukv, cos, sin, kr
        h.raw, h.turned = spare[:, 2:4, :], spare[:, 4:8, :]
        h.q = ringview(k, 0, MH * S, "p (h s) -> p h s", h=MH)
        h.k = ringview(k, MH * S, MH * S, "p (h s) -> p h s", h=MH)
        h.v = ringview(k, 2 * MH * S, T * MH * NOPE, "p (t n) -> p t n", t=T)
        latent_down(k, h)
        latent_up(k, h)
    with ExitStack() as st:
        sb, _ = k.opened(st)
        mix = sb("mix1", [P, T, D])
        w_out = ringview(k, 5 * KD * 512, KD * 512, "p (k n) -> p k n", k=KD)
        attention(k, MH, k.a["mla_w_out"], w_out,
                  lambda hd, t: h.q[0:QK, hd, t * P:(t + 1) * P], lambda hd, n: h.k[0:QK, hd, 0:n],
                  lambda hd, kb: h.v[:, kb, hd * NOPE:(hd + 1) * NOPE],
                  lambda hd, t: mix[:, t, hd * NOPE:(hd + 1) * NOPE], QK ** -0.5)
        project_out(k, mix, k.a["mla_w_out"], w_out, 2)


def latent_down(k, h):
    nc, c = k.nc, k.c
    xt = ringview(k, 0, KD * S, "p (k s) -> p k s", k=KD)
    wi = ringview(k, 4096, KD * MIN, "p (k n) -> p k n", k=KD)
    lat = ringview(k, 4096 + KD * MIN, T * (QL + KVL), "p (t n) -> p t n", t=T)
    LW = QL + KVL
    with ExitStack() as st:
        sb, ps = k.opened(st)
        prm = sb("params1", [P, k.a["params"].shape[1]])
        posi = sb("pos_int", [P, S], I32)
        ang = sb("angle", [P, S])
        rot = sb("turns", [P, S])
        sq = sb("square", [P, QL])
        ss = sb("sum_sq", [P, 2 * T])
        pt = ps("pt", [P, 2, 512])
        pc = ps("pc", [P, 4, 512])
        pr = ps("prope", [P, 2, 512])
        s = phase_sems(k, (
            "w_in", "prm_in", "wu_in", "t_psum", "t_ready", "rope_psum", "rope_copied", "swap_psum", "lat_psum",
            "lat_copied", "angles", "sines", "dve", "squared", "mean", "rooted", "scaled", "lt_psum", "lt_hi", "lt_lo"))
        np_ = CONV_K * NQKV + 56 + DH
        cuts = ((0, QL), (QL, LW))

        @nc_block(k, s)
        def _(block):
            @block.sync
            def _(sp):
                sp.dma_start(wi, k.a["mla_w_in"].rearrange("(k p) n -> p k n", p=P)).then_inc(s["w_in"], 16)
                sp.dma_start(prm[:, :], k.a["params"]).then_inc(s["prm_in"], 16)
                sp.dma_start(posi[:, :], k.a["positions"].to_broadcast([P, S])).then_inc(s["prm_in"], 16)
                sp.dma_start(h.wuq[:, :, :], k.a["mla_w_uq"].rearrange("(k p) n -> p k n", p=P)).then_inc(s["wu_in"], 16)
                sp.dma_start(h.wukv[:, :, :], k.a["mla_w_ukv"].rearrange("(k p) n -> p k n", p=P)).then_inc(s["wu_in"], 16)
                sp.wait_ge(s["wu_in"], 32)

            @block.tensor
            def _(pe):
                for kt in range(KD):
                    if kt >= 2:
                        pe.wait_ge(s["t_ready"], kt - 1)
                    for t in range(T):
                        last = nc.tensor.transpose(pt[:, kt % 2, t * P:(t + 1) * P], k.x[:, t, kt * P:(kt + 1) * P],
                                                   c["ident"])
                    last.then_inc(s["t_psum"], 1)
                pe.wait_ge(s["t_ready"], KD)
                pe.wait_ge(s["w_in"], 16)

                def turn(t):
                    pe.wait_ge(s["scaled"], 2 * (t + 1))
                    if t:
                        pe.wait_ge(s["lt_lo"], 6 * t)
                    for n in range(6):
                        i = nc.tensor.transpose(pt[:, n // 4, (n % 4) * P:(n % 4 + 1) * P],
                                                lat[:, t, n * P:(n + 1) * P], c["ident"])
                    i.then_inc(s["lt_psum"], 1)

                for kt in range(KD):
                    last = nc.tensor.matmul(pr[NOPE:QK, 0, :], wi[:, kt, LW:MIN], xt[:, kt, :],
                                            start=(kt == 0), stop=(kt == KD - 1))
                last.then_inc(s["rope_psum"], 1)
                for t in range(T):
                    if t >= 2:
                        pe.wait_ge(s["lat_copied"], 2 * (t - 1))
                    for kt in range(KD):
                        lhs = xt[:, kt, t * P:(t + 1) * P]
                        nc.tensor.matmul(pc[:, 2 * (t % 2), :], lhs, wi[:, kt, 0:QL], start=(kt == 0),
                                         stop=(kt == KD - 1))
                        last = nc.tensor.matmul(pc[:, 2 * (t % 2) + 1, 0:KVL], lhs, wi[:, kt, QL:LW],
                                                start=(kt == 0), stop=(kt == KD - 1))
                    last.then_inc(s["lat_psum"], 1)
                    if t == 0:
                        pe.wait_ge(s["rope_copied"], 1)
                        nc.tensor.matmul(pr[NOPE:QK, 1, :], c["rope_swap"][NOPE:QK, NOPE:QK], h.kr[NOPE:QK, :],
                                         start=True, stop=True).then_inc(s["swap_psum"], 1)
                    else:
                        turn(t - 1)
                turn(T - 1)

            @block.scalar
            def _(act):
                for kt in range(KD):
                    act.wait_ge(s["t_psum"], kt + 1)
                    nc.scalar.activation(xt[:, kt, :], pt[:, kt % 2, :], ACT.Copy).then_inc(s["t_ready"], 1)
                act.wait_ge(s["rope_psum"], 1)
                nc.scalar.activation(h.kr[NOPE:QK, :], pr[NOPE:QK, 0, :], ACT.Copy).then_inc(s["rope_copied"], 1)
                act.wait_ge(s["angles"], 2)
                nc.scalar.activation(h.sin, ang[:, :], ACT.Sin)
                nc.scalar.activation(h.cos, rot[:, :], ACT.Sin).then_inc(s["sines"], 1)

                def channel_major(t):
                    act.wait_ge(s["lt_psum"], t + 1)
                    for n in range(6):
                        nc.scalar.activation(h.cthi[:, n, t * P:(t + 1) * P], pt[:, n // 4, (n % 4) * P:(n % 4 + 1) * P],
                                             ACT.Copy, scale=prm[:, np_ + n:np_ + n + 1]).then_inc(s["lt_hi"], 1)

                act.wait_ge(s["prm_in"], 32)
                for t in range(T):
                    act.wait_ge(s["lat_psum"], t + 1)
                    for i, (lo, hi) in enumerate(cuts):
                        if t or i:
                            act.wait_ge(s["squared"], 2 * t + i)
                        nc.scalar.activation(sq[:, 0:hi - lo], pc[:, 2 * (t % 2) + i, 0:hi - lo], ACT.Square,
                                             accum_out=ss[:, 2 * t + i:2 * t + i + 1]).then_inc(s["squared"], 1)
                    for i, (lo, hi) in enumerate(cuts):
                        nc.scalar.activation(lat[:, t, lo:hi], pc[:, 2 * (t % 2) + i, 0:hi - lo],
                                             ACT.Copy).then_inc(s["lat_copied"], 1)
                    act.wait_ge(s["mean"], 2 * (t + 1))
                    nc.scalar.activation(ss[:, 2 * t:2 * t + 2], ss[:, 2 * t:2 * t + 2], ACT.Sqrt).then_inc(s["rooted"], 1)
                    if t:
                        channel_major(t - 1)
                channel_major(T - 1)

            @block.vector
            def _(dve):
                ch = Chain(dve, s["dve"])
                v = nc.vector
                ts, stt = v.tensor_scalar, v.scalar_tensor_tensor
                dve.wait_ge(s["prm_in"], 32)
                ch.link(v.tensor_copy(rot[:, :], posi[:, :]))
                ch.link(ts(ang[:, :], rot[:, :], c["inv_freq"], None, ALU.mult))
                magic = 1.5 * 2.0 ** 23
                p1, p2 = 6.28125, 0.0019340515136718750
                p3 = 2 * np.pi - p1 - p2
                ch.link(ts(rot[:, :], ang[:, :], 1 / (2 * np.pi), magic, ALU.mult, ALU.add))
                ch.link(ts(rot[:, :], rot[:, :], magic, None, ALU.subtract))
                for part in (p1, p2, p3):
                    ch.link(stt(ang[:, :], rot[:, :], -float(part), ang[:, :], ALU.mult, ALU.add))
                ch.link(ts(rot[:, :], ang[:, :], np.pi / 2, -2 * np.pi, ALU.is_gt, ALU.mult))
                ch.link(stt(rot[:, :], ang[:, :], np.pi / 2, rot[:, :], ALU.add, ALU.add))
                lim = 3.1415925
                ts(ang[:, :], ang[:, :], lim, -lim, ALU.min, ALU.max).then_inc(s["angles"], 1)
                ts(rot[:, :], rot[:, :], lim, -lim, ALU.min, ALU.max).then_inc(s["angles"], 1)

                def turn_key():
                    dve.wait_ge(s["sines"], 1)
                    dve.wait_ge(s["swap_psum"], 1)
                    w = slice(NOPE, QK)
                    v.tensor_tensor(h.kr[w, :], h.kr[w, :], h.cos[w, :], ALU.mult)
                    ch.link(v.tensor_tensor(ang[w, :], pr[w, 1, :], h.sin[w, :], ALU.mult))
                    ch.link(v.tensor_tensor(h.kr[w, :], h.kr[w, :], ang[w, :], ALU.add))

                def rest(t):
                    for n in range(6):
                        dve.wait_ge(s["lt_hi"], 6 * t + (4 if n < 4 else 6))
                        tok = slice(t * P, (t + 1) * P)
                        stt(h.ctlo[:, n, tok], pt[:, n // 4, (n % 4) * P:(n % 4 + 1) * P], prm[:, np_ + n:np_ + n + 1],
                            h.cthi[:, n, tok].bitcast(F32), ALU.mult, ALU.subtract).then_inc(s["lt_lo"], 1)

                for t in range(T):
                    dve.wait_ge(s["squared"], 2 * (t + 1))
                    for i, width in enumerate((QL, KVL)):
                        ts(ss[:, 2 * t + i:2 * t + i + 1], ss[:, 2 * t + i:2 * t + i + 1], 1.0 / width, RMS_EPS,
                           ALU.mult, ALU.add).then_inc(s["mean"], 1)
                    dve.wait_ge(s["rooted"], t + 1)
                    ch.link(v.reciprocal(ss[:, 2 * t:2 * t + 2], ss[:, 2 * t:2 * t + 2]))
                    dve.wait_ge(s["lat_copied"], 2 * (t + 1))
                    for i, (lo, hi) in enumerate(cuts):
                        ts(lat[:, t, lo:hi], lat[:, t, lo:hi], ss[:, 2 * t + i:2 * t + i + 1], None,
                           ALU.mult).then_inc(s["scaled"], 1)
                    if t == 0:
                        turn_key()
                    else:
                        rest(t - 1)
                rest(T - 1)


def latent_up(k, h):
    nc, c = k.nc, k.c
    with ExitStack() as st:
        sb, ps = k.opened(st)
        raw, turned = h.raw, h.turned
        whi, wlo = sb("w_hi", [P, 2, 1024], F32R), sb("w_lo", [P, 2, 1024], F32R)
        pb = ps("pb", [P, 4, 512])
        psw = ps("psw", [P, 2, 512])
        s = phase_sems(k, (
            "tile_psum", "plain_copied", "rope_copied", "v_copied", "swap_psum", "sin_part", "cos_part", "roped",
            "q_rope_placed", "k_rope_placed",
            "w_hi", "w_lo"))
        uq, ukv = h.wuq, h.wukv
        RB = MH * NOPE
        QN, QR, KN, VN = 8, 4, 8, 8
        NT = QN + QR + KN + VN

        NU = QN + QR + KN + 2

        def unit_source(u):
            if u < QN:
                return uq[:, :, u * P:(u + 1) * P]
            if u < QN + QR:
                return uq[:, :, RB + (u - QN) * P:RB + (u - QN + 1) * P]
            if u < QN + QR + KN:
                return ukv[:, :, (u - QN - QR) * P:(u - QN - QR + 1) * P]
            hf = u - QN - QR - KN
            return ukv[:, :, RB + hf * 512:RB + hf * 512 + 512]

        def unit(x, u):
            n, w = (QL // P, P) if u < QN + QR else (KVL // P, P) if u < QN + QR + KN else (KVL // P, 512)
            return x[:, u % 2, 0:n * w].rearrange("p (n w) -> p n w", n=n)

        def read(eng, n):
            if n < QN:
                eng.wait_ge(s["plain_copied"], 2 * (n + 1))
            elif n < QN + QR:
                eng.wait_ge(s["rope_copied"], n - QN + 1)
            elif n < QN + QR + KN:
                eng.wait_ge(s["plain_copied"], 2 * (n - QR + 1))
            else:
                eng.wait_ge(s["v_copied"], n - QN - QR - KN + 1)

        @nc_block(k, s)
        def _(block):
            @block.tensor
            def _(pe):
                def swap(g):
                    pe.wait_ge(s["rope_copied"], g + 1)
                    if g >= 2:
                        pe.wait_ge(s["sin_part"], g - 1)
                    nc.tensor.matmul(psw[:, g % 2, :], c["rope_swap"], raw[:, g % 2, :], start=True,
                                     stop=True).then_inc(s["swap_psum"], 1)

                for n in range(NT):
                    if n >= 4:
                        read(pe, n - 4)
                    u = min(n, QN + QR + KN + (n - QN - QR - KN) // 4)
                    pe.wait_ge(s["w_lo"], u + 1)
                    c0, nk = (0, QL // P) if n < QN + QR else (QL // P, KVL // P)
                    for kt in range(nk):
                        for m, (x, w) in enumerate(((h.cthi, whi), (h.ctlo, whi), (h.cthi, wlo))):
                            if n < QN + QR + KN:
                                l, r = unit(w, u)[:, kt, :], x[:, c0 + kt, :]
                            else:
                                l, r = x[:, c0 + kt, (n % 4) * P:(n % 4 + 1) * P], unit(w, u)[:, kt, :]
                            last = nc.tensor.matmul(pb[:, n % 4, :], l, r, start=(kt == 0 and m == 0),
                                                    stop=(kt == nk - 1 and m == 2))
                    last.then_inc(s["tile_psum"], 1)
                    if QN + 1 <= n <= QN + QR:
                        swap(n - QN - 1)

            @block.scalar
            def _(act):
                def round_w(u):
                    if u < NU:
                        if u >= 2:
                            act.wait_ge(s["tile_psum"], u - 1)
                        nc.scalar.activation(unit(whi, u), unit_source(u), ACT.Copy).then_inc(s["w_hi"], 1)

                round_w(0)
                round_w(1)
                for n in range(QN + QR + KN):
                    act.wait_ge(s["tile_psum"], n + 1)
                    round_w(n + 2)
                    if n < QN or n >= QN + QR:
                        dst, j = (h.q, n) if n < QN else (h.k, n - QN - QR)
                        for i in range(2):
                            nc.scalar.activation(dst[0:NOPE, 2 * j + i, :], pb[NOPE * i:NOPE * (i + 1), n % 4, :],
                                                 ACT.Copy).then_inc(s["plain_copied"], 1)

            @block.vector
            def _(dve):
                v = nc.vector

                def turn(g):
                    v.tensor_tensor(turned[:, g, :], raw[:, g % 2, :], h.cos,
                                    ALU.mult).then_inc(s["cos_part"], 1)
                    dve.wait_ge(s["swap_psum"], g + 1)
                    dve.wait_ge(s["cos_part"], g + 1)
                    v.tensor_tensor(raw[:, g % 2, :], psw[:, g % 2, :], h.sin, ALU.mult).then_inc(s["sin_part"], 1)
                    dve.wait_ge(s["sin_part"], g + 1)
                    v.tensor_tensor(turned[:, g, :], turned[:, g, :], raw[:, g % 2, :],
                                    ALU.add).then_inc(s["roped"], 1)

                def rest_w(u):
                    if u < NU:
                        dve.wait_ge(s["w_hi"], u + 1)
                        v.tensor_tensor(unit(wlo, u), unit_source(u), unit(whi, u).bitcast(F32),
                                        ALU.subtract).then_inc(s["w_lo"], 1)

                rest_w(0)
                rest_w(1)
                for n in range(QN + QR + KN):
                    rest_w(n + 2)
                    g = n - QN
                    if 0 <= g < QR:
                        dve.wait_ge(s["tile_psum"], n + 1)
                        if g >= 2:
                            dve.wait_ge(s["roped"], g - 1)
                        v.tensor_copy(raw[:, g % 2, :], pb[:, n % 4, :]).then_inc(s["rope_copied"], 1)
                        dve.wait_ge(s["rope_copied"], g + 1)
                    if 1 <= g <= QR:
                        turn(g - 1)
                for m in range(VN):
                    n = QN + QR + KN + m
                    dve.wait_ge(s["tile_psum"], n + 1)
                    hf, t = m // 4, m % 4
                    v.tensor_copy(h.v[:, t, hf * 512:hf * 512 + 512], pb[:, n % 4, :]).then_inc(s["v_copied"], 1)

            @block.gpsimd
            def _(pool):
                for hd in range(MH):
                    nc.gpsimd.tensor_copy(h.k[NOPE:QK, hd, :], h.kr[NOPE:QK, :]).then_inc(s["k_rope_placed"], 1)
                for g in range(QR):
                    pool.wait_ge(s["roped"], g + 1)
                    for j in range(4):
                        nc.gpsimd.tensor_copy(h.q[NOPE:QK, 4 * g + j, :],
                                                  turned[32 * j:32 * j + 32, g, :]).then_inc(s["q_rope_placed"], 1)



def moe_layer(k, layer):
    with ExitStack() as st:
        sb, _ = k.opened(st)
        m = Named()
        m.rank, m.share = sb("rank", [P, T, E]), sb("share", [P, T, E])
        m.rounds = k.rounds[:, layer:layer + 1]
        m.iota = sb("iota", [P, CAP])
        m.xhi, m.xlo = sb("x_hi", [P, T, D], F32R), sb("x_lo", [P, T, D], F32R)
        route(k, layer, m)
        w = expert_buffers(k, st)
        experts(k, layer, m, w)
        overflow_rounds(k, layer, m, w)
    layer_norm(k, 2 * layer + 1, k.out if layer == DEPTH - 1 else None)


def expert_buffers(k, stack):
    sb, ps = k.opened(stack)
    w = Named()
    w.oh, w.ohg = sb("onehot", [P, 2, T, P], F32R), sb("onehot_gate", [P, 2, T, P])
    w.oht = sb("onehot_t", [P, 2, T, P], F32R)
    w.xg, w.xt = sb("xg", [P, D]), sb("xg_t", [P, 2, KD, P])
    w.gate, w.hid, w.ht = sb("silu", [P, 2, FF]), sb("hidden", [P, 2, FF]), sb("hidden_t", [P, 2, 2, P])
    w.sg = sb("slot_gate", [P, 2])
    w.ohi, w.olo = sb("out_hi", [P, 2, 512], F32R), sb("out_lo", [P, 2, 512], F32R)
    w.px, w.po, w.py = (ps(n, [P, 2, 512]) for n in ("px", "po", "py"))
    w.pgu, w.pht = ps("pgu", [P, 512]), ps("pht", [P, 512])
    return w


def ring_load(k, sp, layer, grp, u, sem=None):
    sem = k.ring_full[u] if sem is None else sem
    e0 = grp * EPG + layer * E
    if u < 4:
        for i, name in enumerate(("w_gate", "w_up")):
            src = k.a[name].rearrange("e (p t) f -> p e (t f)", p=P)[:, bass.ds(e0, EPG), u * 512:(u + 1) * 512]
            dst = k.ring[:, u * RW + i * RW // 2:u * RW + (i + 1) * RW // 2].rearrange("p (e w) -> p e w", e=EPG)
            sp.dma_start(dst, src).then_inc(sem, 16)
    else:
        src = k.a["w_down"].rearrange("e (p t) n -> p e (t n)", p=P)[:, bass.ds(e0 + 2 * (u - 4), 2), :]
        dst = k.ring[:, u * RW:(u + 1) * RW].rearrange("p (e w) -> p e w", e=2)
        sp.dma_start(dst, src).then_inc(sem, 16)


def fill_count(u):
    return 32 if u < 4 else 16


def route(k, layer, m):
    nc, c = k.nc, k.c
    with ExitStack() as st:
        sb, ps = k.opened(st)
        xt = sb("xt", [P, KD, S])
        rw = sb("router_w", [P, KD, E])
        rb = sb("router_b", [P, E])
        sc, bi, sel, oh0, oh1, val, both, pref = (sb(n, [P, T, E]) for n in (
            "scores", "biased", "selected", "first", "second", "value", "both", "before"))
        top = sb("top", [P, T * G, 8])
        gs, geq = sb("group_score", [P, T, G]), sb("group_eq", [P, T, G])
        r1 = sb("r1", [P, T])
        top2 = sb("top2", [P, T, 8])
        edge = sb("edge", [P, RNDS - 1])
        cm = sb("count_max", [P, 1])
        pt = ps("pt", [P, 2, 512])
        pr = ps("pr", [P, 512])
        prk = ps("prk", [P, 512])
        pcn = ps("pcn", [P, 512])
        s = phase_sems(k, ("w_in", "t_psum", "t_ready", "score_psum", "scored", "dve", "counted", "rank_psum",
                           "x_hi", "x_lo"))

        @nc_block(k, s)
        def _(block):
            @block.sync
            def _(sp):
                sp.dma_start(rw[:, :, :], k.a["router_w"].rearrange("(k p) e -> p k e", p=P)).then_inc(s["w_in"], 16)
                sp.dma_start(rb[:, :], k.a["router_bias"].to_broadcast([P, E])).then_inc(s["w_in"], 16)
                for u in range(UNITS):
                    ring_load(k, sp, layer, 0, u)

            @block.tensor
            def _(pe):
                for kt in range(KD):
                    if kt >= 2:
                        pe.wait_ge(s["t_ready"], kt - 1)
                    for t in range(T):
                        last = nc.tensor.transpose(pt[:, kt % 2, t * P:(t + 1) * P], k.x[:, t, kt * P:(kt + 1) * P],
                                                   c["ident"])
                    last.then_inc(s["t_psum"], 1)
                pe.wait_ge(s["t_ready"], KD)
                pe.wait_ge(s["w_in"], 32)
                for t in range(T):
                    for kt in range(KD):
                        last = nc.tensor.matmul(pr[:, t * E:(t + 1) * E], xt[:, kt, t * P:(t + 1) * P], rw[:, kt, :],
                                                start=(kt == 0), stop=(kt == KD - 1))
                last.then_inc(s["score_psum"], 1)
                pe.wait_ge(s["counted"], 1)
                nc.tensor.matmul(prk[:, 0:T * E], c["tri_strict"], both[:, :, :], start=True, stop=False)
                nc.tensor.matmul(prk[:, 0:T * E], c["ones"], pref[:, :, :], start=False, stop=True)
                nc.tensor.matmul(pcn[:, 0:E], c["ones"], val[:, 0, :], start=True,
                                 stop=True).then_inc(s["rank_psum"], 1)

            @block.scalar
            def _(act):
                for kt in range(KD):
                    act.wait_ge(s["t_psum"], kt + 1)
                    nc.scalar.activation(xt[:, kt, :], pt[:, kt % 2, :], ACT.Copy).then_inc(s["t_ready"], 1)
                for t in range(T):
                    nc.scalar.activation(m.xhi[:, t, :], k.x[:, t, :], ACT.Copy).then_inc(s["x_hi"], 1)
                act.wait_ge(s["score_psum"], 1)
                nc.scalar.activation(sc[:, :, :], pr[:, 0:T * E].rearrange("p (t e) -> p t e", t=T),
                                     ACT.Sigmoid).then_inc(s["scored"], 1)

            @block.gpsimd
            def _(pool):
                for t in range(T):
                    pool.wait_ge(s["x_hi"], t + 1)
                    nc.gpsimd.tensor_tensor(m.xlo[:, t, :], k.x[:, t, :], m.xhi[:, t, :].bitcast(F32),
                                            ALU.subtract).then_inc(s["x_lo"], 1)
                    pool.wait_ge(s["x_lo"], t + 1)
                    nc.gpsimd.tensor_scalar(k.x[:, t, :], k.x[:, t, :], ALPHA, None, ALU.mult)

            @block.vector
            def _(dve):
                ch = Chain(dve, s["dve"])
                v = nc.vector
                tt, ts = v.tensor_tensor, v.tensor_scalar

                def tiles(x):
                    return x.unsqueeze(1).to_broadcast([P, T, x.shape[1]])

                def cols(x, n):
                    return x.unsqueeze(2).to_broadcast([P, T, n])

                dve.wait_ge(s["w_in"], 32)
                dve.wait_ge(s["scored"], 1)
                ch.link(tt(bi[:, :, :], sc[:, :, :], tiles(rb[:, :]), ALU.add))
                bg = bi[:, :, :].rearrange("p t (g e) -> p (t g) e", g=G)
                for n in range(T * G):
                    i = v.max(top[:, n, :], bg[:, n, :])
                ch.link(i)
                tg = top[:, :, :].rearrange("p (t g) e -> p t g e", t=T)
                ch.link(tt(gs[:, :, :], tg[:, :, :, 0], tg[:, :, :, 1], ALU.add))
                ch.link(v.reduce_max(r1[:, :], gs[:, :, :], axis=AX))
                ch.link(tt(geq[:, :, :], gs[:, :, :], cols(r1[:, :], G), ALU.is_equal))
                ch.link(tt(geq[:, :, :], geq[:, :, :], tiles(c["group_rev"]), ALU.mult))
                ch.link(v.reduce_max(r1[:, :], geq[:, :, :], axis=AX))
                ch.link(tt(geq[:, :, :], geq[:, :, :], cols(r1[:, :], G), ALU.is_equal))
                selg = sel[:, :, :].rearrange("p t (g e) -> p (t g) e", g=G)
                geqb = geq[:, :, :].rearrange("p t g -> p (t g)").unsqueeze(2).to_broadcast([P, T * G, E // G])
                ch.link(v.tensor_copy(selg, geqb))
                ch.link(tt(bi[:, :, :], bi[:, :, :], sel[:, :, :], ALU.mult))
                ch.link(ts(sel[:, :, :], sel[:, :, :], 1.0, -NEG, ALU.subtract, ALU.mult))
                ch.link(tt(bi[:, :, :], bi[:, :, :], sel[:, :, :], ALU.add))
                for t in range(T):
                    i = v.max(top2[:, t, :], bi[:, t, :])
                ch.link(i)
                for oh, n in ((oh0, 0), (oh1, 1)):
                    ch.link(tt(val[:, :, :], bi[:, :, :], cols(top2[:, :, n], E), ALU.is_equal))
                    if n:
                        ch.link(ts(sel[:, :, :], oh0[:, :, :], -1.0, 1.0, ALU.mult, ALU.add))
                        ch.link(tt(val[:, :, :], val[:, :, :], sel[:, :, :], ALU.mult))
                    ch.link(tt(val[:, :, :], val[:, :, :], tiles(c["expert_rev"]), ALU.mult))
                    ch.link(v.reduce_max(r1[:, :], val[:, :, :], axis=AX))
                    ch.link(tt(oh[:, :, :], val[:, :, :], cols(r1[:, :], E), ALU.is_equal))
                ch.link(tt(both[:, :, :], oh0[:, :, :], oh1[:, :, :], ALU.add))
                ch.link(v.memset(pref[:, 0, :], 0.0))
                for t in range(1, T):
                    ch.link(tt(pref[:, t, :], pref[:, t - 1, :], both[:, t - 1, :], ALU.add))
                tt(val[:, 0, :], pref[:, T - 1, :], both[:, T - 1, :], ALU.add).then_inc(s["counted"], 1)
                ch.link(tt(bi[:, :, :], both[:, :, :], sc[:, :, :], ALU.mult))
                ch.link(v.reduce_sum(r1[:, :], bi[:, :, :], axis=AX))
                ch.link(v.reciprocal(r1[:, :], r1[:, :]))
                tt(m.share[:, :, :], bi[:, :, :], cols(r1[:, :], E), ALU.mult)
                dve.wait_ge(s["rank_psum"], 1)
                ch.link(ts(m.rank[:, :, :], prk[:, 0:T * E].rearrange("p (t e) -> p t e", t=T), 1.0, None, ALU.add))
                ch.link(tt(m.rank[:, :, :], m.rank[:, :, :], both[:, :, :], ALU.mult))
                ts(m.rank[:, :, :], m.rank[:, :, :], 1.0, None, ALU.subtract)
                ch.link(v.reduce_max(cm[:, :], pcn[:, 0:E], axis=AX))
                ch.link(ts(edge[:, :], c["round_edges"], cm[:, 0:1], None, ALU.is_lt))
                ch.link(v.reduce_sum(cm[:, :], edge[:, :], axis=AX))
                v.tensor_copy(m.rounds[:, :], cm[:, :])
                v.tensor_copy(m.iota[:, :], c["slot_iota"])



def build_onehot(k, m, w, b, grp):
    v = k.nc.vector

    def wide(x):
        return x[:, :, bass.ds(grp * EPG, EPG)].unsqueeze(3).to_broadcast([P, T, EPG, CAP])
    slots = w.oh[:, b, :, :].rearrange("p t (e s) -> p t e s", e=EPG)
    iota = m.iota[:, :].unsqueeze(1).unsqueeze(1).to_broadcast([P, T, EPG, CAP])
    first = v.tensor_tensor(slots, wide(m.rank), iota, ALU.is_equal)

    def with_share():
        return v.tensor_tensor(w.ohg[:, b, :, :].rearrange("p t (e s) -> p t e s", e=EPG),
                               w.oh[:, b, :, :].bitcast(F32).rearrange("p t (e s) -> p t e s", e=EPG),
                               wide(m.share), ALU.mult)
    return first, with_share


def pick_rows(k, m, w, b):
    for half in range(2):
        for t in range(T):
            for n, x in enumerate((m.xhi, m.xlo)):
                i = k.nc.tensor.matmul(w.px[:, half, :], w.oh[:, b, t, :], x[:, t, half * 512:half * 512 + 512],
                                       start=(t == 0 and n == 0), stop=(t == T - 1 and n == 1))
    return i


def turn_rows(k, w):
    for kt in range(KD):
        i = k.nc.tensor.transpose(w.px[:, kt // 4, (kt % 4) * P:(kt % 4 + 1) * P], w.xg[:, kt::KD], k.c["ident"])
    return i


def gate_up(k, w, b, kt):
    u, j = kt // 2, kt % 2
    wv = k.ring[:, u * RW:(u + 1) * RW].rearrange("p (g e t f) -> p e t g f", g=2, e=EPG, t=2)
    for e in range(EPG):
        r = slice(CAP * e, CAP * e + CAP)
        i = k.nc.tensor.matmul(w.pgu[r, :], w.xt[:, b, kt, r], wv[:, e, j, :, :], start=(kt == 0),
                               stop=(kt == KD - 1))
    return i


def turn_hidden(k, w, b):
    for ft in range(2):
        i = k.nc.tensor.transpose(w.pht[:, ft * P:(ft + 1) * P], w.hid[:, b, ft::2], k.c["ident"])
    return i


def down(k, w, b, half):
    for ft in range(2):
        for e in range(EPG):
            r = slice(CAP * e, CAP * e + CAP)
            at = (4 + e // 2) * RW + (e % 2) * RW // 2 + ft * D + half * 512
            i = k.nc.tensor.matmul(w.po[r, half, :], w.ht[:, b, ft, r], k.ring[:, at:at + 512], start=(ft == 0),
                                   stop=(ft == 1))
    return i


def turn_onehot(k, w, b):
    for t in range(T):
        k.nc.tensor.transpose(w.px[:, 0, t * P:(t + 1) * P], w.oh[:, b, t, :].bitcast(F32), k.c["ident"])
    for t in range(T):
        i = k.nc.tensor.matmul(w.pht[:, 2 * P:2 * P + 1], w.ohg[:, b, t, :], k.c["ones"][:, 0:1],
                               start=(t == 0), stop=(t == T - 1))
    return i


def give_back(k, w, b, n):
    t, half = n // 2, n % 2
    for x, o in enumerate((w.ohi, w.olo)):
        i = k.nc.tensor.matmul(w.py[:, n % 2, :], w.oht[:, b, t, :], o[:, half, :], start=(x == 0), stop=(x == 1))
    return i


def take_in(k, w, n):
    xs = k.x[:, n // 2, (n % 2) * 512:(n % 2) * 512 + 512]
    return k.nc.vector.tensor_tensor(xs, xs, w.py[:, n % 2, :], ALU.add)


def experts(k, layer, m, w):
    nc, c = k.nc, k.c
    NB = 2 * T
    s = phase_sems(k, ("oh", "ohg", "picked", "xg_act", "xg_dve", "xt_psum", "xt_act", "xt_dve", "oht_psum", "oht",
                       "sg", "unit_used", "silu", "hidden", "ht_psum", "ht_ready", "o_psum", "o_hi", "o_lo",
                       "y_psum", "y_added"))
    fill0 = layer * NGRP
    last = NGRP // 2 - 1

    def each_group(eng, group):
        with eng.Fori(0, last) as j:
            group(0, j, True)
            group(1, j, True)
        group(0, last, True)
        group(1, last, False)

    @nc_block(k, s)
    def _(block):
        @block.sync
        def _(sp):
            with sp.Fori(0, NGRP - 1) as i:
                for u in range(UNITS):
                    if u < 4:
                        sp.wait_ge(s["unit_used"], i * 4 + (u + 1))
                    elif u == 4:
                        sp.wait_ge(s["o_psum"], i * 2 + 2)
                    ring_load(k, sp, layer, i + 1, u)

        @block.tensor
        def _(pe):
            def turned_onehot(b, n1):
                pe.wait_ge(s["xt_act"], n1)
                pe.wait_ge(s["ohg"], n1)
                pe.wait_ge(s["sg"], n1)
                turn_onehot(k, w, b).then_inc(s["oht_psum"], 1)

            def group(b, j, more):
                n = 2 * j + b
                pe.wait_ge(s["xt_act"], n + 1)
                pe.wait_ge(s["xt_dve"], n + 1)
                pe.wait_ge(s["hidden"], n + 1)
                for kt in range(KD):
                    u = kt // 2
                    if kt % 2 == 0:
                        pe.wait_ge(k.ring_full[u], fill_count(u) * (n + 1 + fill0))
                    i = gate_up(k, w, b, kt)
                    if kt % 2:
                        i.then_inc(s["unit_used"], 1)
                if more:
                    pe.wait_ge(s["oh"], n + 2)
                    pe.wait_ge(s["oht"], n + 1)
                    pick_rows(k, m, w, 1 - b).then_inc(s["picked"], 1)
                pe.wait_ge(s["hidden"], n + 2)
                turn_hidden(k, w, b).then_inc(s["ht_psum"], 1)
                if more:
                    pe.wait_ge(s["xg_act"], n + 2)
                    pe.wait_ge(s["xg_dve"], n + 2)
                    turn_rows(k, w).then_inc(s["xt_psum"], 1)
                for u in (4, 5):
                    pe.wait_ge(k.ring_full[u], fill_count(u) * (n + 1 + fill0))
                pe.wait_ge(s["ht_ready"], n + 1)
                pe.wait_ge(s["o_hi"], 2 * n + 1)
                pe.wait_ge(s["o_lo"], 2 * n + 1)
                down(k, w, b, 0).then_inc(s["o_psum"], 1)
                down(k, w, b, 1).then_inc(s["o_psum"], 1)
                if more:
                    turned_onehot(1 - b, n + 2)
                for i in range(NB):
                    if i < 2:
                        pe.wait_ge(s["o_hi"], 2 * n + 2 + i)
                        pe.wait_ge(s["o_lo"], 2 * n + 2 + i)
                    if i == 0:
                        pe.wait_ge(s["oht"], n + 1)
                    pe.wait_ge(s["y_added"], NB * n + (i + 1))
                    give_back(k, w, b, i).then_inc(s["y_psum"], 1)

            pe.wait_ge(s["oh"], 1)
            pick_rows(k, m, w, 0).then_inc(s["picked"], 1)
            pe.wait_ge(s["xg_act"], 1)
            pe.wait_ge(s["xg_dve"], 1)
            turn_rows(k, w).then_inc(s["xt_psum"], 1)
            turned_onehot(0, 1)
            each_group(pe, group)

        @block.scalar
        def _(act):
            act.sem_inc(s["o_hi"], 1)
            copy = nc.scalar.activation

            def xg(n1):
                act.wait_ge(s["picked"], n1)
                copy(w.xg[:, 0:512], w.px[:, 0, :], ACT.Copy).then_inc(s["xg_act"], 1)

            def xt(b, n1):
                act.wait_ge(s["xt_psum"], n1)
                copy(w.xt[:, b, 0:4, :], w.px[:, 0, :].rearrange("p (k s) -> p k s", k=4),
                     ACT.Copy).then_inc(s["xt_act"], 1)

            def oht(b, n1):
                act.wait_ge(s["oht_psum"], n1)
                copy(w.oht[:, b, :, :], w.px[:, 0, :].rearrange("p (t s) -> p t s", t=T),
                     ACT.Copy).then_inc(s["oht"], 1)

            def group(b, j, more):
                n = 2 * j + b
                act.wait_ge(s["unit_used"], 4 * n + 4)
                copy(w.gate[:, b, :], w.pgu[:, 0:FF], ACT.Silu).then_inc(s["silu"], 1)
                if more:
                    xg(n + 2)
                act.wait_ge(s["ht_psum"], n + 1)
                copy(w.ht[:, b, :, :], w.pht[:, 0:2 * P].rearrange("p (t s) -> p t s", t=2),
                     ACT.Copy).then_inc(s["ht_ready"], 1)
                if more:
                    xt(1 - b, n + 2)
                act.wait_ge(s["y_psum"], NB * n + 1)
                act.wait_ge(s["sg"], n + 2)
                for half in range(2):
                    act.wait_ge(s["o_psum"], 2 * n + half + 1)
                    copy(w.ohi[:, half, :], w.po[:, half, :], ACT.Copy,
                         scale=w.sg[:, b:b + 1]).then_inc(s["o_hi"], 1)
                if more:
                    oht(1 - b, n + 2)

            xg(1)
            xt(0, 1)
            oht(0, 1)
            each_group(act, group)

        @block.vector
        def _(dve):
            v = nc.vector
            for name, credit in (("hidden", 1), ("o_lo", 1), ("sg", 1), ("y_added", 2), ("y_psum", 1)):
                dve.sem_inc(s[name], credit)

            def onehots(b, grp, n1):
                first, with_share = build_onehot(k, m, w, b, grp)
                first.then_inc(s["oh"], 1)
                dve.wait_ge(s["oh"], n1)
                with_share().then_inc(s["ohg"], 1)

            def xg(n1):
                dve.wait_ge(s["picked"], n1)
                v.tensor_copy(w.xg[:, 512:D], w.px[:, 1, :]).then_inc(s["xg_dve"], 1)

            def xt(b, n1):
                dve.wait_ge(s["xt_psum"], n1)
                v.tensor_copy(w.xt[:, b, 4:8, :],
                              w.px[:, 1, :].rearrange("p (k s) -> p k s", k=4)).then_inc(s["xt_dve"], 1)

            def sg(b, n1):
                dve.wait_ge(s["oht_psum"], n1)
                v.tensor_copy(w.sg[:, b:b + 1], w.pht[:, 2 * P:2 * P + 1]).then_inc(s["sg"], 1)

            def group(b, j, more):
                n = 2 * j + b
                if more:
                    onehots(1 - b, n + 1, n + 2)
                dve.wait_ge(s["silu"], n + 1)
                v.tensor_tensor(w.hid[:, b, :], w.gate[:, b, :], w.pgu[:, FF:2 * FF],
                                ALU.mult).then_inc(s["hidden"], 1)
                if more:
                    xg(n + 2)
                    xt(1 - b, n + 2)
                for half in range(2):
                    dve.wait_ge(s["o_hi"], 2 * n + half + 2)
                    v.scalar_tensor_tensor(w.olo[:, half, :], w.po[:, half, :], w.sg[:, b:b + 1],
                                           w.ohi[:, half, :].bitcast(F32), ALU.mult,
                                           ALU.subtract).then_inc(s["o_lo"], 1)
                if more:
                    sg(1 - b, n + 2)
                for i in range(NB):
                    dve.wait_ge(s["y_psum"], NB * n + (i + 2))
                    take_in(k, w, i).then_inc(s["y_added"], 1)

            onehots(0, 0, 1)
            xg(1)
            xt(0, 1)
            sg(0, 1)
            each_group(dve, group)


def overflow_rounds(k, layer, m, w):
    nc = k.nc
    rounds = nc.values_load(m.rounds[0:1, 0:1], min_val=0, max_val=RNDS - 1)
    with nc.If(rounds > 0):
        with nc.Fori(0, rounds):
            with nc.Fori(0, NGRP) as g:
                overflow_group(k, layer, m, w, g)
    for e in (nc.sync, nc.tensor, nc.vector, nc.scalar, nc.gpsimd):
        e.nop()


def overflow_group(k, layer, m, w, g):
    nc = k.nc
    s = phase_sems(k, ("weights", "oh", "ohg", "picked", "xg", "xt_psum", "xt_ready", "oht_psum", "oht", "sg",
                       "gu_psum", "silu", "hidden", "ht_psum", "ht_ready", "o_psum", "o_hi", "o_lo", "y_psum",
                       "y_added", "next_slots"))

    @nc_block(k, s, repeated=True)
    def _(block):
        @block.sync
        def _(sp):
            for u in range(UNITS):
                ring_load(k, sp, layer, g, u, s["weights"])

        @block.tensor
        def _(pe):
            pe.wait_ge(s["oh"], 1)
            pick_rows(k, m, w, 0).then_inc(s["picked"], 1)
            pe.wait_ge(s["xg"], 2)
            turn_rows(k, w).then_inc(s["xt_psum"], 1)
            pe.wait_ge(s["xt_ready"], 2)
            pe.wait_ge(s["ohg"], 1)
            turn_onehot(k, w, 0).then_inc(s["oht_psum"], 1)
            pe.wait_ge(s["weights"], sum(fill_count(u) for u in range(UNITS)))
            for kt in range(KD):
                i = gate_up(k, w, 0, kt)
            i.then_inc(s["gu_psum"], 1)
            pe.wait_ge(s["hidden"], 1)
            turn_hidden(k, w, 0).then_inc(s["ht_psum"], 1)
            pe.wait_ge(s["ht_ready"], 1)
            down(k, w, 0, 0)
            down(k, w, 0, 1).then_inc(s["o_psum"], 1)
            pe.wait_ge(s["o_lo"], 2)
            pe.wait_ge(s["oht"], 1)
            for i in range(2 * T):
                if i >= 2:
                    pe.wait_ge(s["y_added"], i - 1)
                give_back(k, w, 0, i).then_inc(s["y_psum"], 1)

        @block.scalar
        def _(act):
            copy = nc.scalar.activation
            act.wait_ge(s["picked"], 1)
            for half in range(2):
                copy(w.xg[:, half * 512:half * 512 + 512], w.px[:, half, :], ACT.Copy).then_inc(s["xg"], 1)
            act.wait_ge(s["xt_psum"], 1)
            for half in range(2):
                copy(w.xt[:, 0, 4 * half:4 * half + 4, :], w.px[:, half, :].rearrange("p (k s) -> p k s", k=4),
                     ACT.Copy).then_inc(s["xt_ready"], 1)
            act.wait_ge(s["oht_psum"], 1)
            copy(w.oht[:, 0, :, :], w.px[:, 0, :].rearrange("p (t s) -> p t s", t=T), ACT.Copy).then_inc(s["oht"], 1)
            act.wait_ge(s["gu_psum"], 1)
            copy(w.gate[:, 0, :], w.pgu[:, 0:FF], ACT.Silu).then_inc(s["silu"], 1)
            act.wait_ge(s["ht_psum"], 1)
            copy(w.ht[:, 0, :, :], w.pht[:, 0:2 * P].rearrange("p (t s) -> p t s", t=2),
                 ACT.Copy).then_inc(s["ht_ready"], 1)
            act.wait_ge(s["o_psum"], 1)
            act.wait_ge(s["sg"], 1)
            for half in range(2):
                copy(w.ohi[:, half, :], w.po[:, half, :], ACT.Copy, scale=w.sg[:, 0:1]).then_inc(s["o_hi"], 1)

        @block.vector
        def _(dve):
            v = nc.vector
            step = k.c["round_step"][:, bass.ds(g, 1)]
            v.tensor_scalar(m.iota[:, :], m.iota[:, :], step, None, ALU.add).then_inc(s["next_slots"], 1)
            dve.wait_ge(s["next_slots"], 1)
            first, with_share = build_onehot(k, m, w, 0, g)
            first.then_inc(s["oh"], 1)
            dve.wait_ge(s["oh"], 1)
            with_share().then_inc(s["ohg"], 1)
            dve.wait_ge(s["oht_psum"], 1)
            v.tensor_copy(w.sg[:, 0:1], w.pht[:, 2 * P:2 * P + 1]).then_inc(s["sg"], 1)
            dve.wait_ge(s["silu"], 1)
            v.tensor_tensor(w.hid[:, 0, :], w.gate[:, 0, :], w.pgu[:, FF:2 * FF], ALU.mult).then_inc(s["hidden"], 1)
            for half in range(2):
                dve.wait_ge(s["o_hi"], half + 1)
                v.scalar_tensor_tensor(w.olo[:, half, :], w.po[:, half, :], w.sg[:, 0:1],
                                       w.ohi[:, half, :].bitcast(F32), ALU.mult, ALU.subtract).then_inc(s["o_lo"], 1)
            for i in range(2 * T):
                dve.wait_ge(s["y_psum"], i + 1)
                take_in(k, w, i).then_inc(s["y_added"], 1)


def kernel(**inputs):
    import concourse.bacc as _bacc
    from concourse.bass_utils import run_bass_kernel_spmd as _run

    def lay(name):
        return np.ascontiguousarray(np.asarray(inputs[name]))

    nc = _bacc.Bacc("TRN2", target_bir_lowering=False, num_devices=1)
    order = list(range(0, H, 2)) + list(range(1, H, 2))
    w_in = lay("hy_w_in")[0]
    gates = np.concatenate([w_in[:, 2048:2056][:, order], w_in[:, 2056:2064][:, order], w_in[:, 3600:3608]], 1)
    taps = lay("hy_conv_w")[0].reshape(CONV_K, NQKV, P).transpose(2, 0, 1).reshape(P, -1)
    rows = np.concatenate([np.repeat(np.float32([-1, 1, -1]), H), np.zeros(H, np.float32),
                           lay("gdn_dt_bias")[0][order], lay("fox_f_bias")[0], lay("gdn_a_log")[0][order],
                           lay("gdn_norm_w")[0]])
    params = np.concatenate([taps, np.broadcast_to(rows, (P, rows.size)),
                             lay("mla_q_norm")[0].reshape(-1, P).T, lay("mla_kv_norm")[0].reshape(-1, P).T], 1)
    uq = lay("mla_w_uq")[0].reshape(QL, MH, QK)
    ukv = lay("mla_w_ukv")[0].reshape(KVL, MH, 2 * NOPE)
    uq = np.concatenate([uq[:, :, :NOPE].reshape(QL, -1), uq[:, :, NOPE:].reshape(QL, -1)], 1)
    ukv = np.concatenate([ukv[:, :, :NOPE].reshape(KVL, -1), ukv[:, :, NOPE:].reshape(KVL, -1)], 1)
    host = {
        "const": const_array(),
        "params": np.ascontiguousarray(params),
        "w_gates": np.ascontiguousarray(gates.reshape(KD, P, 24).transpose(1, 0, 2).reshape(P, -1)),
        "x": lay("x")[0],
        "positions": lay("positions").astype(np.int32),
        "ln_gain": lay("ln_gain").reshape(2 * DEPTH, D),
        "ln_bias": lay("ln_bias").reshape(2 * DEPTH, D),
        "router_w": lay("router_w"),
        "router_bias": lay("router_bias")[None],
        "w_gate": lay("moe_w_gate").reshape(DEPTH * E, D, FF),
        "w_up": lay("moe_w_up").reshape(DEPTH * E, D, FF),
        "w_down": lay("moe_w_down").reshape(DEPTH * E, FF, D),
        "hy_w_in": w_in,
        "hy_w_out": lay("hy_w_out")[0],
        "mla_w_in": lay("mla_w_in")[0],
        "mla_w_uq": np.ascontiguousarray(uq),
        "mla_w_ukv": np.ascontiguousarray(ukv),
        "mla_w_out": lay("mla_w_out")[0],
    }
    a = {n: nc.dram_tensor(f"in_{n}", v.shape, mybir.dt.from_np(v.dtype), kind="ExternalInput").ap()
         for n, v in host.items()}
    out = nc.dram_tensor("out", [S, D], F32, kind="ExternalOutput").ap()
    build(nc, a, out)
    r = _run(nc, [{f"in_{n}": v for n, v in host.items()}], core_ids=[0])
    return r.results[0]["out"].reshape(1, S, D)
```
